# Optimizing a Trainium2 kernel written in Bass

```python
import math
import jax, jax.numpy as jnp
from jax import lax
import numpy as np

D_MODEL = 1024
BATCH = 1
SEQ = 256
DEPTH = 2

MIX_WIDTH = D_MODEL
POOL_WIDTH = D_MODEL // 2
POOL_WINDOWS = (2, 4, 8, 16)
POOL_GROUPS = len(POOL_WINDOWS)
POOL_GC = POOL_WIDTH // POOL_GROUPS
HEAD_DIM = 64
NSA_HEADS = (MIX_WIDTH - POOL_WIDTH) // HEAD_DIM
KV_GROUPS = 2
HEADS_PER_GROUP = NSA_HEADS // KV_GROUPS
N_BRANCH = 3
CMP_LEN = 32
CMP_STRIDE = 16
SEL_LEN = 64
SEL_TOPN = 16
WINDOW = 512
Q_BLOCK = 128
D_FF = 4 * D_MODEL
ROPE_THETA = 10000.0
EPS = 1e-6
NEG = -1e30
FORCED_SCORE = 1e4

Q_COLS = NSA_HEADS * HEAD_DIM
KV_COLS = KV_GROUPS * HEAD_DIM
GATE_COLS = NSA_HEADS * N_BRANCH
IN_COLS = POOL_WIDTH + Q_COLS + 2 * N_BRANCH * KV_COLS + GATE_COLS


def rms_norm(x, g):
    xf = x.astype(jnp.float32)
    y = xf * lax.rsqrt(jnp.mean(xf * xf, axis=-1, keepdims=True) + EPS)
    return (y * g.astype(jnp.float32)).astype(x.dtype)

def rope(x, pos):
    dk = x.shape[-1]
    half = dk // 2
    inv = ROPE_THETA ** (-jnp.arange(half, dtype=jnp.float32) * 2.0 / dk)
    ang = pos.astype(jnp.float32)[:, None] * inv[None, :]
    shape = (1, pos.shape[0]) + (1,) * (x.ndim - 3) + (half,)
    cos = jnp.cos(ang).reshape(shape)
    sin = jnp.sin(ang).reshape(shape)
    xf = x.astype(jnp.float32)
    x1, x2 = xf[..., :half], xf[..., half:]
    return jnp.concatenate([x1 * cos - x2 * sin, x2 * cos + x1 * sin], axis=-1).astype(x.dtype)

def pool_mixer(u, pool_w, pool_scale):
    B, S, _ = u.shape
    ug = u.reshape(B, S, POOL_GROUPS, POOL_GC).astype(jnp.float32)
    cs = jnp.concatenate([jnp.zeros((B, 1, POOL_GROUPS, POOL_GC), jnp.float32),
                          jnp.cumsum(ug, axis=1)], axis=1)
    t = jnp.arange(S)
    win = jnp.array(POOL_WINDOWS, dtype=jnp.int32)
    lower = jnp.maximum(t[:, None] + 1 - win[None, :], 0)
    count = jnp.minimum(t[:, None] + 1, win[None, :]).astype(jnp.float32)
    gidx = jnp.arange(POOL_GROUPS)[None, :]
    sums = cs[:, 1:] - cs[:, lower, gidx]
    pooled = (sums / count[None, :, :, None] - ug).astype(u.dtype)
    y = jnp.einsum('bsgc,gcd->bsgd', pooled, pool_w)
    return y.reshape(B, S, POOL_WIDTH) * pool_scale

def compress(t, pe, w1, w2, blk):
    B = t.shape[0]
    n_cmp = blk.shape[0]
    tb = t[:, blk] + pe[None, None, :, None, :]
    flat = tb.transpose(0, 1, 3, 2, 4).reshape(B, n_cmp, KV_GROUPS, CMP_LEN * HEAD_DIM)
    return jax.nn.silu(flat @ w1) @ w2

def nsa_mixer(q, k_all, v_all, gates, q_norm, k_norm, cmp_pe, cmp_w1, cmp_w2):
    B, S = q.shape[0], q.shape[1]
    G, Hg, dk = KV_GROUPS, HEADS_PER_GROUP, HEAD_DIM
    scale = 1.0 / math.sqrt(dk)
    pos = jnp.arange(S)

    q = rope(rms_norm(q, q_norm), pos).reshape(B, S, G, Hg, dk)
    k_s = rope(rms_norm(k_all[:, :, 1], k_norm[1]), pos)
    k_w = rope(rms_norm(k_all[:, :, 2], k_norm[2]), pos)
    v_s = v_all[:, :, 1]
    v_w = v_all[:, :, 2]

    n_cmp = (S - CMP_LEN) // CMP_STRIDE + 1
    blk = np.arange(n_cmp)[:, None] * CMP_STRIDE + np.arange(CMP_LEN)[None, :]
    cmp_end = jnp.arange(n_cmp) * CMP_STRIDE + (CMP_LEN - 1)
    k_cmp = compress(k_all[:, :, 0], cmp_pe[0], cmp_w1[0], cmp_w2[0], blk)
    v_cmp = compress(v_all[:, :, 0], cmp_pe[1], cmp_w1[1], cmp_w2[1], blk)
    k_cmp = rope(rms_norm(k_cmp, k_norm[0]), cmp_end)
    s_c = jnp.einsum('bsghd,bngd->bsghn', q, k_cmp).astype(jnp.float32) * scale
    mask_c = (cmp_end[None, :] <= pos[:, None])[None, :, None, None, :]
    p_c = jax.nn.softmax(jnp.where(mask_c, s_c, NEG), axis=-1)
    p_c = jnp.where(mask_c, p_c, 0.0)
    o_cmp = jnp.einsum('bsghn,bngd->bsghd', p_c.astype(v_cmp.dtype), v_cmp)

    n_sel = S // SEL_LEN
    cs0 = np.arange(n_cmp) * CMP_STRIDE
    ss0 = np.arange(n_sel) * SEL_LEN
    ov = np.minimum(cs0[:, None] + CMP_LEN, ss0[None, :] + SEL_LEN) - np.maximum(cs0[:, None], ss0[None, :])
    ov_mat = jnp.asarray(np.clip(ov, 0, None).astype(np.float32) / CMP_LEN)
    imp = jnp.einsum('bsghn,nj->bsgj', p_c, ov_mat)
    blk_id = jnp.arange(n_sel)[None, :]
    cur = (pos // SEL_LEN)[:, None]
    causal = blk_id <= cur
    forced = (blk_id == 0) | (blk_id == cur) | (blk_id == cur - 1)
    imp = jnp.where(causal[None, :, None, :],
                    jnp.where(forced[None, :, None, :], FORCED_SCORE, imp), -1.0)
    topn = min(SEL_TOPN, n_sel)
    vals, sel_idx = lax.top_k(imp, topn)
    sel_valid = vals >= 0.0

    k_sb = k_s.reshape(B, n_sel, SEL_LEN, G, dk).transpose(0, 3, 1, 2, 4)
    v_sb = v_s.reshape(B, n_sel, SEL_LEN, G, dk).transpose(0, 3, 1, 2, 4)
    pad = ((0, 0), (WINDOW, 0), (0, 0), (0, 0))
    k_wp = jnp.pad(k_w, pad)
    v_wp = jnp.pad(v_w, pad)
    bi = jnp.arange(B)[:, None, None, None]
    gi = jnp.arange(G)[None, None, :, None]
    C = Q_BLOCK

    def block_fn(qb):
        start = qb * C
        qc = lax.dynamic_slice_in_dim(q, start, C, axis=1)
        tc = start + jnp.arange(C)
        idx = lax.dynamic_slice_in_dim(sel_idx, start, C, axis=1)
        val = lax.dynamic_slice_in_dim(sel_valid, start, C, axis=1)
        kg = k_sb[bi, gi, idx]
        vg = v_sb[bi, gi, idx]
        s = jnp.einsum('bcghd,bcgnld->bcghnl', qc, kg).astype(jnp.float32) * scale
        kpos = idx[..., None] * SEL_LEN + jnp.arange(SEL_LEN)
        m = (kpos <= tc[None, :, None, None, None]) & val[..., None]
        s = jnp.where(m[:, :, :, None], s, NEG)
        sh = s.shape
        p = jax.nn.softmax(s.reshape(sh[:4] + (sh[4] * sh[5],)), axis=-1).reshape(sh)
        o_s = jnp.einsum('bcghnl,bcgnld->bcghd', p.astype(vg.dtype), vg)
        kw = lax.dynamic_slice_in_dim(k_wp, start, C + WINDOW, axis=1)
        vw = lax.dynamic_slice_in_dim(v_wp, start, C + WINDOW, axis=1)
        kpos_w = start - WINDOW + jnp.arange(C + WINDOW)
        diff = tc[:, None] - kpos_w[None, :]
        mw = ((diff >= 0) & (diff < WINDOW) & (kpos_w[None, :] >= 0))[None, :, None, None, :]
        sw = jnp.einsum('bcghd,bkgd->bcghk', qc, kw).astype(jnp.float32) * scale
        pw = jax.nn.softmax(jnp.where(mw, sw, NEG), axis=-1)
        o_w = jnp.einsum('bcghk,bkgd->bcghd', pw.astype(vw.dtype), vw)
        return o_s, o_w

    o_s, o_w = lax.map(block_fn, jnp.arange(S // C))
    o_s = o_s.transpose(1, 0, 2, 3, 4, 5).reshape(B, S, G, Hg, dk)
    o_w = o_w.transpose(1, 0, 2, 3, 4, 5).reshape(B, S, G, Hg, dk)

    g = jax.nn.sigmoid(gates.astype(jnp.float32)).reshape(B, S, G, Hg, N_BRANCH).astype(q.dtype)
    o = g[..., 0:1] * o_cmp + g[..., 1:2] * o_s + g[..., 2:3] * o_w
    return o.reshape(B, S, NSA_HEADS * dk)

def hybrid_layer(x, mod, norm1, norm2, w_in, pool_w, pool_scale, q_norm, k_norm,
                 cmp_pe, cmp_w1, cmp_w2, w_out, w_ff1, w_ff2):
    B, S, _ = x.shape
    shift1, scale1, gate1, shift2, scale2, gate2 = jnp.split(mod[:, None, :], 6, axis=-1)
    h = rms_norm(x, norm1) * (1.0 + scale1) + shift1
    proj = h @ w_in
    o0 = POOL_WIDTH
    o1 = o0 + Q_COLS
    o2 = o1 + 2 * N_BRANCH * KV_COLS
    u = proj[..., :o0]
    q = proj[..., o0:o1].reshape(B, S, NSA_HEADS, HEAD_DIM)
    kv = proj[..., o1:o2].reshape(B, S, 2, N_BRANCH, KV_GROUPS, HEAD_DIM)
    gates = proj[..., o2:]
    y_pool = pool_mixer(u, pool_w, pool_scale)
    y_nsa = nsa_mixer(q, kv[:, :, 0], kv[:, :, 1], gates, q_norm, k_norm, cmp_pe, cmp_w1, cmp_w2)
    mix = jnp.concatenate([y_pool, y_nsa], axis=-1) @ w_out
    x = x + gate1 * mix
    h2 = rms_norm(x, norm2) * (1.0 + scale2) + shift2
    ff = jnp.square(jax.nn.relu(h2 @ w_ff1)) @ w_ff2
    return x + gate2 * ff

def first_inputs(seed: int = 0) -> dict:
    key = jax.random.key(seed)
    ks = jax.random.split(key, 20)
    f32 = jnp.float32
    L, D = DEPTH, D_MODEL
    nrm = lambda k, shape, s: jax.random.normal(k, shape, f32) * s
    return {
        "x": nrm(ks[0], (BATCH, SEQ, D), 1.0),
        "c": nrm(ks[1], (BATCH, D), 1.0),
        "w_mod": nrm(ks[2], (L, D, 6 * D), 0.5 * D ** -0.5),
        "b_mod": nrm(ks[3], (L, 6 * D), 0.01),
        "norm1": 1.0 + nrm(ks[4], (L, D), 0.05),
        "norm2": 1.0 + nrm(ks[5], (L, D), 0.05),
        "w_in": nrm(ks[6], (L, D, IN_COLS), D ** -0.5),
        "pool_w": nrm(ks[7], (L, POOL_GROUPS, POOL_GC, POOL_GC), POOL_GC ** -0.5),
        "pool_scale": 0.5 + nrm(ks[8], (L, POOL_WIDTH), 0.1),
        "q_norm": 1.0 + nrm(ks[9], (L, HEAD_DIM), 0.05),
        "k_norm": 1.0 + nrm(ks[10], (L, N_BRANCH, HEAD_DIM), 0.05),
        "cmp_pe": nrm(ks[11], (L, 2, CMP_LEN, HEAD_DIM), 0.5),
        "cmp_w1": nrm(ks[12], (L, 2, CMP_LEN * HEAD_DIM, HEAD_DIM), (CMP_LEN * HEAD_DIM) ** -0.5),
        "cmp_w2": nrm(ks[13], (L, 2, HEAD_DIM, HEAD_DIM), HEAD_DIM ** -0.5),
        "w_out": nrm(ks[14], (L, MIX_WIDTH, D), MIX_WIDTH ** -0.5),
        "w_ff1": nrm(ks[15], (L, D, D_FF), D ** -0.5),
        "w_ff2": nrm(ks[16], (L, D_FF, D), D_FF ** -0.5),
    }

def first_block(x, c, w_mod, b_mod, norm1, norm2, w_in, pool_w, pool_scale, q_norm, k_norm,
              cmp_pe, cmp_w1, cmp_w2, w_out, w_ff1, w_ff2):
    c_act = jax.nn.silu(c)
    for l in range(DEPTH):
        mod = c_act @ w_mod[l] + b_mod[l]
        x = hybrid_layer(x, mod, norm1[l], norm2[l], w_in[l], pool_w[l], pool_scale[l],
                         q_norm[l], k_norm[l], cmp_pe[l], cmp_w1[l], cmp_w2[l],
                         w_out[l], w_ff1[l], w_ff2[l])
    return x


DEPTH_2 = 1

SSD_EXPAND = 2
D_INNER = SSD_EXPAND * D_MODEL
SSD_HEAD_DIM = 64
SSD_HEADS = D_INNER // SSD_HEAD_DIM
SSD_GROUPS = 4
SSD_HEADS_PER_GROUP = SSD_HEADS // SSD_GROUPS
D_STATE = 128
D_CONV = 5
SSD_CHUNK = 128
CONV_DIM = D_INNER + 2 * SSD_GROUPS * D_STATE
NORM_EPS = 1e-5

ATTN_HEAD_DIM = 64
DIL_PATTERNS = ((128, 1), (512, 4), (2048, 16))
N_PATTERNS = len(DIL_PATTERNS)
HEADS_PER_PATTERN = 4
ATTN_HEADS = N_PATTERNS * HEADS_PER_PATTERN
ATTN_WIDTH = ATTN_HEADS * ATTN_HEAD_DIM
ATTN_OUT_WIDTH = HEADS_PER_PATTERN * ATTN_HEAD_DIM

D_FF_2 = 4 * D_MODEL
N_BRANCHES = 2
IN_SPLITS = (D_INNER, CONV_DIM, SSD_HEADS, SSD_HEADS, ATTN_WIDTH, ATTN_WIDTH, ATTN_WIDTH, N_BRANCHES * D_MODEL)
IN_COLS_2 = sum(IN_SPLITS)


def layer_norm(x, g, b):
    xf = x.astype(jnp.float32)
    mu = jnp.mean(xf, axis=-1, keepdims=True)
    var = jnp.mean(jnp.square(xf - mu), axis=-1, keepdims=True)
    return ((xf - mu) * lax.rsqrt(var + NORM_EPS) * g.astype(jnp.float32) + b.astype(jnp.float32)).astype(x.dtype)

def centred_depthwise_conv(u, w, b):
    pad = D_CONV // 2
    out = lax.conv_general_dilated(u, w[:, None, :].astype(u.dtype), window_strides=(1,), padding=((pad, pad),),
                                   dimension_numbers=('NWC', 'WIO', 'NWC'), feature_group_count=u.shape[-1])
    return out + b.astype(u.dtype)

def segsum_exp(a_cs):
    q = a_cs.shape[-1]
    diff = a_cs[..., :, None] - a_cs[..., None, :]
    mask = jnp.tril(jnp.ones((q, q), dtype=bool))
    return jnp.where(mask, jnp.exp(jnp.where(mask, diff, 0.0)), 0.0)

def ssd_chunked(xh, dt, a_coef, bm, cm):
    bsz, s = xh.shape[:2]
    nc = s // SSD_CHUNK
    g, r, p = SSD_GROUPS, SSD_HEADS_PER_GROUP, SSD_HEAD_DIM
    xc = (xh * dt[..., None]).reshape(bsz, nc, SSD_CHUNK, g, r, p)
    a = (dt * a_coef).reshape(bsz, nc, SSD_CHUNK, g, r).transpose(0, 3, 4, 1, 2)
    bc = bm.reshape(bsz, nc, SSD_CHUNK, g, D_STATE)
    cc = cm.reshape(bsz, nc, SSD_CHUNK, g, D_STATE)
    a_cs = jnp.cumsum(a, axis=-1)
    lmat = segsum_exp(a_cs)
    cb = jnp.einsum('bclgn,bcsgn->bgcls', cc, bc)
    y_diag = jnp.einsum('bgcls,bgrcls,bcsgrp->bclgrp', cb, lmat, xc)
    decay_states = jnp.exp(a_cs[..., -1:] - a_cs)
    states = jnp.einsum('bclgn,bgrcl,bclgrp->bcgrpn', bc, decay_states, xc)
    chunk_decay = jnp.exp(a_cs[..., -1])

    def step(h, inp):
        dec, st = inp
        return dec[..., None, None] * h + st, h

    h0 = jnp.zeros_like(states[:, 0])
    _, prev = lax.scan(step, h0, (jnp.moveaxis(chunk_decay, -1, 0), jnp.moveaxis(states, 1, 0)))
    prev = jnp.moveaxis(prev, 0, 1)
    y_off = jnp.einsum('bclgn,bcgrpn,bgrcl->bclgrp', cc, prev, jnp.exp(a_cs))
    return (y_diag + y_off).reshape(bsz, s, g * r, p)

def ssd_branch(z, xbc, dt_f_raw, dt_b_raw, conv_w, conv_b, dt_bias_f, dt_bias_b, a_log_f, a_log_b, d_skip, ssd_norm_w):
    bsz, s = z.shape[:2]
    xbc = jax.nn.silu(centred_depthwise_conv(xbc, conv_w, conv_b)).astype(jnp.float32)
    xs, bm, cm = jnp.split(xbc, [D_INNER, D_INNER + SSD_GROUPS * D_STATE], axis=-1)
    xh = xs.reshape(bsz, s, SSD_HEADS, SSD_HEAD_DIM)
    bm = bm.reshape(bsz, s, SSD_GROUPS, D_STATE)
    cm = cm.reshape(bsz, s, SSD_GROUPS, D_STATE)
    dt_f = jax.nn.softplus(dt_f_raw.astype(jnp.float32) + dt_bias_f.astype(jnp.float32))
    dt_b = jax.nn.softplus(dt_b_raw.astype(jnp.float32) + dt_bias_b.astype(jnp.float32))
    a_f = -jnp.exp(a_log_f.astype(jnp.float32))
    a_b = -jnp.exp(a_log_b.astype(jnp.float32))
    y_f = ssd_chunked(xh, dt_f, a_f, bm, cm)
    flip = lambda t: jnp.flip(t, axis=1)
    y_b = flip(ssd_chunked(flip(xh), flip(dt_b), a_b, flip(bm), flip(cm)))
    y = y_f + y_b + d_skip.astype(jnp.float32)[:, None] * xh
    y = y.reshape(bsz, s, D_INNER) * jax.nn.silu(z.astype(jnp.float32))
    yg = y.reshape(bsz, s, SSD_GROUPS, D_INNER // SSD_GROUPS)
    yg = yg * lax.rsqrt(jnp.mean(jnp.square(yg), axis=-1, keepdims=True) + NORM_EPS)
    return (yg.reshape(bsz, s, D_INNER) * ssd_norm_w.astype(jnp.float32)).astype(z.dtype)

def dilated_window_attention(q, k, v, slopes, dilation, half):
    bsz, s, h, e = q.shape
    seq_l = s // dilation
    blk = half
    nb = -(-seq_l // blk)
    lp = nb * blk

    def to_strided(a):
        return a.astype(jnp.float32).reshape(bsz, seq_l, dilation, h, e).transpose(0, 2, 3, 1, 4)

    qs = jnp.pad(to_strided(q), ((0, 0), (0, 0), (0, 0), (0, lp - seq_l), (0, 0))).reshape(bsz, dilation, h, nb, blk, e)

    def windows(a):
        a = jnp.pad(to_strided(a), ((0, 0), (0, 0), (0, 0), (blk, blk + lp - seq_l), (0, 0)))
        a = a.reshape(bsz, dilation, h, nb + 2, blk, e)
        return jnp.concatenate([a[:, :, :, :-2], a[:, :, :, 1:-1], a[:, :, :, 2:]], axis=4)

    ks, vs = windows(k), windows(v)
    qpos = jnp.arange(nb)[:, None] * blk + jnp.arange(blk)[None, :]
    kpos = jnp.arange(nb)[:, None] * blk - blk + jnp.arange(3 * blk)[None, :]
    rel = kpos[:, None, :] - qpos[:, :, None]
    valid = (jnp.abs(rel) <= half) & (kpos[:, None, :] >= 0) & (kpos[:, None, :] < seq_l)
    dist = (jnp.abs(rel) * dilation).astype(jnp.float32)
    scores = jnp.einsum('bdhine,bdhime->bdhinm', qs, ks) * (1.0 / math.sqrt(e))
    scores = scores - slopes.astype(jnp.float32)[:, None, None, None] * dist
    scores = jnp.where(valid, scores, -jnp.inf)
    m = jnp.max(scores, axis=-1, keepdims=True)
    p = jnp.exp(scores - m)
    den = jnp.sum(p, axis=-1, keepdims=True)
    o = jnp.einsum('bdhinm,bdhime->bdhine', p, vs) / den
    lse = (m + jnp.log(den))[..., 0]

    def from_strided(a):
        a = a.reshape(bsz, dilation, h, lp, *a.shape[5:])[:, :, :, :seq_l]
        a = jnp.moveaxis(a, 3, 1)
        return a.reshape(bsz, s, h, *a.shape[4:])

    return from_strided(o), from_strided(lse)

def attention_branch(q, k, v):
    bsz, s = q.shape[:2]
    q = q.reshape(bsz, s, ATTN_HEADS, ATTN_HEAD_DIM)
    k = k.reshape(bsz, s, ATTN_HEADS, ATTN_HEAD_DIM)
    v = v.reshape(bsz, s, ATTN_HEADS, ATTN_HEAD_DIM)
    slopes = jnp.asarray(2.0 ** (-8.0 * np.arange(1, ATTN_HEADS + 1) / ATTN_HEADS), dtype=jnp.float32)
    outs, lses = [], []
    for gi, (window, dilation) in enumerate(DIL_PATTERNS):
        hs = slice(gi * HEADS_PER_PATTERN, (gi + 1) * HEADS_PER_PATTERN)
        o, l = dilated_window_attention(q[:, :, hs], k[:, :, hs], v[:, :, hs], slopes[hs], dilation, window // (2 * dilation))
        outs.append(o)
        lses.append(l)
    o = jnp.stack(outs, axis=0)
    lse = jnp.stack(lses, axis=0)
    w = jax.nn.softmax(lse, axis=0)
    y = jnp.sum(w[..., None] * o, axis=0)
    return y.reshape(bsz, s, ATTN_OUT_WIDTH).astype(q.dtype)

def second_inputs(seed: int = 0) -> dict:
    key = jax.random.key(seed)
    ks = jax.random.split(key, 24)
    beta = (8.0 * DEPTH_2) ** -0.25
    nrm = lambda k, shape: jax.random.normal(k, shape, dtype=jnp.float32)

    def dt_bias(k):
        dt = jnp.exp(jax.random.uniform(k, (SSD_HEADS,), minval=math.log(1e-3), maxval=math.log(1e-1)))
        return dt + jnp.log(-jnp.expm1(-dt))

    return {
        "x": nrm(ks[0], (BATCH, SEQ, D_MODEL)),
        "w_in": nrm(ks[1], (D_MODEL, IN_COLS_2)) * D_MODEL ** -0.5,
        "b_gate": 0.02 * nrm(ks[2], (N_BRANCHES * D_MODEL,)),
        "conv_w": nrm(ks[3], (D_CONV, CONV_DIM)) * D_CONV ** -0.5,
        "conv_b": 0.02 * nrm(ks[4], (CONV_DIM,)),
        "dt_bias_f": dt_bias(ks[5]),
        "dt_bias_b": dt_bias(ks[6]),
        "a_log_f": jnp.log(jax.random.uniform(ks[7], (SSD_HEADS,), minval=1.0, maxval=16.0)),
        "a_log_b": jnp.log(jax.random.uniform(ks[8], (SSD_HEADS,), minval=1.0, maxval=16.0)),
        "d_skip": 1.0 + 0.1 * nrm(ks[9], (SSD_HEADS,)),
        "ssd_norm_w": 1.0 + 0.1 * nrm(ks[10], (D_INNER,)),
        "w_proj_ssd": nrm(ks[11], (D_INNER, D_MODEL)) * D_INNER ** -0.5 * beta,
        "w_proj_attn": nrm(ks[12], (ATTN_OUT_WIDTH, D_MODEL)) * ATTN_OUT_WIDTH ** -0.5 * beta,
        "w_out": nrm(ks[13], (D_MODEL, D_MODEL)) * D_MODEL ** -0.5 * beta,
        "ln1_g": 1.0 + 0.1 * nrm(ks[14], (D_MODEL,)),
        "ln1_b": 0.02 * nrm(ks[15], (D_MODEL,)),
        "w_up": nrm(ks[16], (D_MODEL, D_FF_2)) * D_MODEL ** -0.5 * beta,
        "w_down": nrm(ks[17], (D_FF_2, D_MODEL)) * D_FF_2 ** -0.5 * beta,
        "ln2_g": 1.0 + 0.1 * nrm(ks[18], (D_MODEL,)),
        "ln2_b": 0.02 * nrm(ks[19], (D_MODEL,)),
    }

def second_block(x, w_in, b_gate, conv_w, conv_b, dt_bias_f, dt_bias_b, a_log_f, a_log_b, d_skip, ssd_norm_w,
              w_proj_ssd, w_proj_attn, w_out, ln1_g, ln1_b, w_up, w_down, ln2_g, ln2_b):
    alpha = (2.0 * DEPTH_2) ** 0.25
    h = x
    for _ in range(DEPTH_2):
        bsz, s = h.shape[:2]
        u = h @ w_in
        z, xbc, dt_f_raw, dt_b_raw, q, k, v, gate_logits = jnp.split(u, list(np.cumsum(IN_SPLITS)[:-1]), axis=-1)
        y_ssd = ssd_branch(z, xbc, dt_f_raw, dt_b_raw, conv_w, conv_b, dt_bias_f, dt_bias_b,
                           a_log_f, a_log_b, d_skip, ssd_norm_w) @ w_proj_ssd
        y_att = attention_branch(q, k, v) @ w_proj_attn
        gates = jax.nn.sigmoid(gate_logits + b_gate).reshape(bsz, s, N_BRANCHES, D_MODEL)
        mix = (gates[:, :, 0] * y_ssd + gates[:, :, 1] * y_att) @ w_out
        h = layer_norm(alpha * h + mix, ln1_g, ln1_b)
        f = jnp.square(jax.nn.relu(h @ w_up)) @ w_down
        h = layer_norm(alpha * h + f, ln2_g, ln2_b)
    return h


def setup_inputs(seed=0):
    out = dict(first_inputs(seed))
    for name, value in second_inputs(seed + 1).items():
        if name != "x":
            out[name + "_2"] = value
    return out


def reference(
    x, c, w_mod, b_mod, norm1, norm2, w_in, pool_w, pool_scale, q_norm, k_norm, cmp_pe, cmp_w1,
    cmp_w2, w_out, w_ff1, w_ff2, w_in_2, b_gate_2, conv_w_2, conv_b_2, dt_bias_f_2, dt_bias_b_2,
    a_log_f_2, a_log_b_2, d_skip_2, ssd_norm_w_2, w_proj_ssd_2, w_proj_attn_2, w_out_2, ln1_g_2,
    ln1_b_2, w_up_2, w_down_2, ln2_g_2, ln2_b_2,
):
    x = first_block(
        x, c, w_mod, b_mod, norm1, norm2, w_in, pool_w, pool_scale, q_norm, k_norm, cmp_pe,
        cmp_w1, cmp_w2, w_out, w_ff1, w_ff2,
    )
    return second_block(
        x, w_in_2, b_gate_2, conv_w_2, conv_b_2, dt_bias_f_2, dt_bias_b_2, a_log_f_2, a_log_b_2,
        d_skip_2, ssd_norm_w_2, w_proj_ssd_2, w_proj_attn_2, w_out_2, ln1_g_2, ln1_b_2, w_up_2,
        w_down_2, ln2_g_2, ln2_b_2,
    )


_drawn_inputs = setup_inputs


def setup_inputs(seed=0):
    import zlib

    import numpy as np

    out = dict(_drawn_inputs(seed))
    spreads = {}
    factors = {'norm1': 6.053,
     'q_norm': 8.0,
     'k_norm': 8.0,
     'b_gate_2': 35.312,
     'conv_b_2': 8.0,
     'd_skip_2': 64.0,
     'ssd_norm_w_2': 4.103,
     'ln1_b_2': 2.852}
    for name, (base, spread) in spreads.items():
        noise = np.random.default_rng([zlib.crc32(name.encode()), seed]).standard_normal(out[name].shape)
        drawn = base * np.exp(spread * noise) if base else spread * noise
        out[name] = __import__('jax').numpy.asarray(drawn.astype(out[name].dtype))
    for name, factor in factors.items():
        out[name] = (out[name] * factor).astype(out[name].dtype)
    return out
```

```python
import math
from contextlib import ExitStack

import numpy as np
import concourse.bass as bass
from concourse import mybir

F32 = mybir.dt.float32
F32R = mybir.dt.float32r
BF16 = mybir.dt.bfloat16
ALU = mybir.AluOpType
ACT = mybir.ActivationFunctionType
AX = mybir.AxisListType

P = 128
T = 256
TT = T // P
D = 1024
KC = D // P
DEPTH = 2
EPS = 1e-6
LN_EPS = 1e-5
NEG = -1e30

PANEL = KC * 256
RAW = 2
SPLIT = 4
L_K0K1, L_K2V0, L_V1V2, L_Q0, L_Q1, L_CMP, L_U0, L_U1, L_OUT, L_FF = 0, 1, 2, 3, 4, 5, 6, 7, 8, 12
L_PANELS = 44
FF_STEPS = 16
MOD_PANELS = 24

LC_BM, LC_N1, LC_N2, LC_PS, LC_QN, LC_KN, LC_PE, LC_W2, LC_PW, LC_GW, LC = 0, 48, 56, 64, 68, 69, 72, 104, 168, 680, 872

C_ID, C_BD, C_ROT, C_ONE, C_COS, C_SIN, C_CCOS, C_CSIN, C_CAUS, C_CMPM, C_VALID, C_EPS, C_LEPS, C_MF, C_MB, C_SG, C_NM, C_RC, CN = (
    0, 128, 256, 384, 512, 768, 1024, 1040, 1056, 1184, 1216, 1217, 1218, 1219, 1347, 1475, 1476, 1477, 2501)
N_CMP = (T - 32) // 16 + 1


D_INNER, N_HEADS, CONV_DIM, D_CONV = 2048, 32, 3072, 5
N_SPLITS = np.cumsum([0, D_INNER, CONV_DIM, N_HEADS, N_HEADS, 768, 768, 768, 2 * D])
L2_WDT, L2_DTB, L2_ALOG, L2_CW, L2_CB, L2_DS, L2_SN, L2_BG, L2_LN1G, L2_LN1B, L2_LN2G, L2_LN2B, LC2 = (
    0, 512, 513, 514, 634, 658, 674, 690, 706, 714, 722, 730, 738)
FAR = 1e30


def distances():
    t = np.arange(T).reshape(TT, P).T[:, :, None, None]
    s = np.arange(T)[None, None, None, :]
    dil = np.array((1, 4, 16))[None, None, :, None]
    dd = np.abs(t - s)
    return np.where((dd % dil == 0) & (dd <= 64 * dil), dd, FAR).astype(np.float32).reshape(P, TT * 3 * T)


def constants():
    c = np.zeros((P, CN), np.float32)
    p = np.arange(P)[:, None]
    f = np.arange(P)[None, :]
    c[:, C_ID:C_ID + P] = p == f
    c[:, C_BD:C_BD + P] = p // 64 == f // 64
    c[:, C_ROT:C_ROT + P] = np.where((f % 64 < 32) & (p == f + 32), -1.0, np.where((f % 64 >= 32) & (p == f - 32), 1.0, 0.0))
    c[:, C_ONE:C_ONE + P] = 1.0
    inv = np.float32(10000.0) ** (-(np.arange(32, dtype=np.float32)) * np.float32(2.0) / np.float32(64))
    inv = np.tile(inv.astype(np.float32), 4)[:, None]
    ang = (np.arange(T, dtype=np.float32)[None, :] * inv).astype(np.float32)
    c[:, C_COS:C_COS + T], c[:, C_SIN:C_SIN + T] = np.cos(ang), np.sin(ang)
    end = np.arange(N_CMP) * 16 + 31
    ang = (end.astype(np.float32)[None, :] * inv).astype(np.float32)
    c[:, C_CCOS:C_CCOS + N_CMP], c[:, C_CSIN:C_CSIN + N_CMP] = np.cos(ang), np.sin(ang)
    c[:, C_CAUS:C_CAUS + P] = np.where(f > p, NEG, 0.0)
    for tt in range(TT):
        c[:, C_CMPM + 16 * tt:C_CMPM + 16 * tt + N_CMP] = np.where(end[None, :] > p + P * tt, NEG, 0.0)
    c[:, C_VALID] = np.arange(P) >= 31
    c[:, C_EPS] = EPS
    c[:, C_LEPS] = LN_EPS
    c[:, C_MF:C_MF + P] = np.where(p > f, NEG, 0.0)
    c[:, C_MB:C_MB + P] = np.where(f > p, NEG, 0.0)
    c[:, C_SG] = np.where(np.arange(P) % 64 < 32, 1.0, -1.0)
    c[:, C_NM] = np.where(np.arange(P) % 64 < 32, 0.0, -1.0)
    for g, w in enumerate((2, 4, 8, 16)):
        c[:, C_RC + g * T:C_RC + (g + 1) * T] = 1.0 / np.minimum(np.arange(T) + 1, w)
    return c


def build(nc, a, out, layers=DEPTH, dump=None):
    ctx = ExitStack()

    def sb(name, shape, dt=F32):
        return ctx.enter_context(nc.sbuf_tensor(name, shape, dt))

    def sem(name):
        return ctx.enter_context(nc.semaphore(name))

    with ctx:
        raw = sb("raw", [P, RAW, PANEL])
        w_hi = [sb(f"w_hi{i}", [P, PANEL], F32R) for i in range(SPLIT)]
        w_lo = [sb(f"w_lo{i}", [P, PANEL], F32R) for i in range(SPLIT)]
        x = sb("x", [P, KC, T])
        act_hi, act_lo = sb("act_hi", [P, KC, T], F32R), sb("act_lo", [P, KC, T], F32R)
        with nc.sbuf_tensor("mixf", [P, 2 * KC * T], F32) as mixf:
            pass
        mix_hi, mix_lo = sb("mix_hi", [P, KC, T], F32R), sb("mix_lo", [P, KC, T], F32R)
        ff_hi, ff_lo = sb("ff_hi", [P, 2, 2 * T], F32R), sb("ff_lo", [P, 2, 2 * T], F32R)
        cst = sb("cst", [P, CN])
        lc = sb("lc", [P, LC])
        idb = sb("idb", [P, P], BF16)
        causb = sb("causb", [P, P], BF16)
        cmpmb = sb("cmpmb", [P, 32], BF16)
        ccol = sb("ccol", [P, KC])
        cact = sb("cact", [P, KC])
        modc = sb("modc", [P, 48])
        macc = sb("macc", [P, 2, 256])
        gcol = sb("gcol", [P, 2 * KC])
        rs = sb("rs", [P, T])
        small = sb("small", [P, 160])
        ARENA = 17920
        arena = sb("arena", [P, ARENA])
        at = [0]

        def area(n, *dims):
            v = arena[:, at[0]:at[0] + n]
            at[0] += n
            assert at[0] <= ARENA, at[0]
            if len(dims) == 2:
                v = v.rearrange("p (a b) -> p a b", a=dims[0])
            if len(dims) == 3:
                v = v.rearrange("p (a b c) -> p a b c", a=dims[0], b=dims[1])
            return v

        bank = [ctx.enter_context(nc.psum_tensor(f"bank{i}", [P, 512], F32)) for i in range(8)]

        def win(ap, start, n_part, dims, col=0):
            full = ap[start:start + n_part, col:col + 1]
            return bass.AP(full.tensor, full.offset, [[full.ap[0][0], n_part], *dims])

        x_loaded, cst_loaded, c_loaded = sem("x_loaded"), sem("cst_loaded"), sem("c_loaded")
        masks_ready = sem("masks_ready")
        cact_ready = sem("cact_ready")
        x_turned = sem("x_turned")
        x_ready = sem("x_ready")
        lc_ready = sem("lc_ready")
        sq_done = sem("sq_done")
        ss_done = sem("ss_done")
        rs_done = sem("rs_done")
        t_done = sem("t_done")
        act_his = sem("act_his")
        act_ready = sem("act_ready")
        raw_ready = [sem(f"raw_ready{i}") for i in range(RAW)]
        hi_done = sem("hi_done")
        lo_done = sem("lo_done")
        split_free = sem("split_free")
        modraw = [sem(f"modraw{i}") for i in range(2)]
        mod_used = sem("mod_used")
        macc_free = sem("macc_free")
        modc_ready = sem("modc_ready")
        gfull = sem("gfull")
        gfree = [sem(f"gfree{i}") for i in range(2)]
        nr_sq = sem("nr_sq")
        nr_mm = sem("nr_mm")
        nr_rs = sem("nr_rs")
        nr_yc = sem("nr_yc")
        nr_out = sem("nr_out")
        tb_k, tb_v, tb_pe, tb_hi, tb_lo = sem("tb_k"), sem("tb_v"), sem("tb_pe"), sem("tb_hi"), sem("tb_lo")
        cmp_h, cmp_e, cmp_s, cmp_w2, cmp_y = sem("cmp_h"), sem("cmp_e"), sem("cmp_s"), sem("cmp_w2"), sem("cmp_y")
        gw_hi, gw_lo = sem("gw_hi"), sem("gw_lo")
        u_copied = sem("u_copied")
        pooled_ready = sem("pooled_ready")
        at_sc = sem("at_sc")
        at_nm = sem("at_nm")
        at_exp = sem("at_exp")
        at_p = sem("at_p")
        at_tr = sem("at_tr")
        at_ev0, at_ev1 = sem("at_ev0"), sem("at_ev1")
        at_pv = sem("at_pv")
        mix_his = sem("mix_his")
        out_done = sem("out_done")
        ff_full = sem("ff_full")
        ff_relu = sem("ff_relu")
        ff_sq = sem("ff_sq")
        ff_his = sem("ff_his")
        ff_ready = sem("ff_ready")
        ff_out = sem("ff_out")
        dve_links, act_links, pool_links = sem("dve_links"), sem("act_links"), sem("pool_links")
        out_written = sem("out_written")

        class Chain:

            def __init__(self, eng, s, per_layer):
                self.eng, self.s, self.per, self.base, self.n, self.first = eng, s, per_layer, 0, 0, 0

            def __call__(self, ins):
                ins.then_inc(self.s, 1)
                self.n += 1
                self.eng.wait_ge(self.s, self.base + self.n)

            def layer(self, l):
                self.base, self.n0, self.n = l * self.per + self.first, 0, 0

            def end(self):
                assert self.n == self.per, (self.eng, self.n)

        at[0] = 0
        modw = area(2 * PANEL, 2, PANEL)
        tbuf = area(KC * T, KC, T)
        L_ARENA = at[0]
        ybuf = [area(2 * T, 2, T) for _ in range(3)]
        q_at = at[0]
        qr = area(4 * T, 4, T)
        kr = area(2 * T, 2, T)
        vt = area(TT * T, TT, T)
        tb = area(960, 16, 60)
        pbuf = [area(800) for _ in range(2)]
        pts = [area(1024) for _ in range(2)]
        fr = [v[:, 0:2 * T] for v in pts]
        ub = area(4 * (T + 16), 4, T + 16)
        wb = [area(4 * (T + 16), 4, T + 16) for _ in range(2)]
        tbh, tbl = [v[:, :, :].rearrange("p a b -> p (a b)")[:, 0:960].rearrange("p (j n) -> p j n", j=16) for v in (ff_hi, ff_lo)]
        gwh, gwl = sb("gwh", [P, KC, 24], F32R), sb("gwl", [P, KC, 24], F32R)
        kcmp = small[:, 0:15]
        vcmp = sb("vcmp", [16, P])
        hs = small[:, 16:76]
        ce = small[:, 76:136]
        ycmp = small[:, 136:151]
        gts = sb("gts", [P, TT, 24])
        sqc = sb("sqc", [P, 48])
        dens = sb("dens", [P, 2, 6])
        nm = sb("nm", [P, 2, 6])
        fac = sb("fac", [P, 2, 6])

        ident = cst[:, C_ID:C_ID + P]
        ones = cst[:, C_ONE:C_ONE + P]
        x_in = arena[:, q_at:q_at + TT * D].rearrange("p (t d) -> p t d", t=TT)


        def slot(k):
            return k % SPLIT

        n_panels = a["panels"].shape[0]

        L_AHEAD = 5

        def load(sp, m, k):
            sp.wait_ge(lo_done, 4 * m + k - RAW + 1)
            sp.dma_start(raw[:, k % RAW, :], a["panels"][4 * m + k]).then_inc(raw_ready[k % RAW], 16)

        def load_mod(sp, l, mp):
            sp.wait_ge(mod_used, MOD_PANELS * l + mp + 1)
            sp.dma_start(modw[:, mp % 2, :], a["modw"][l, mp]).then_inc(modraw[mp % 2], 16)


        def split_hi(act, m, k):
            act.wait_ge(raw_ready[k % RAW], 16 * (2 * m + k // 2 + 1))
            act.wait_ge(split_free, 4 * m + k + 1)
            nc.scalar.activation(w_hi[slot(k)][:, :], raw[:, k % RAW, :], ACT.Copy).then_inc(hi_done, 1)

        def split_lo(dve, m, k):
            dve.wait_ge(hi_done, 4 * m + k + 1)
            nc.vector.tensor_tensor(w_lo[slot(k)][:, :], raw[:, k % RAW, :], w_hi[slot(k)][:, :].bitcast(F32),
                                    ALU.subtract).then_inc(lo_done, 1)

        def mm3(o, wh, wl, xh, xl, start, stop, skip=False):
            nc.tensor.matmul(o, wh, xh, start=start, stop=False, skip_group_check=skip)
            nc.tensor.matmul(o, wh, xl, start=False, stop=False, skip_group_check=skip)
            return nc.tensor.matmul(o, wl, xh, start=False, stop=stop, skip_group_check=skip)

        def pool_rope(pool, l):
            for j in range(3):
                pool.wait_ge(nr_mm, 4 * l + j + 1)
                y = ybuf[j]
                nc.gpsimd.tensor_tensor(y, y, cst[:, C_COS:C_COS + T].unsqueeze(1).to_broadcast([P, 2, T]), ALU.mult).then_inc(nr_yc, 1)

        def pool_window(pool, l, link):
            pool.wait_ge(u_copied, 2 * l + 2)
            b, c = wb

            def cols(t, g0, off=0, step=1):
                return t[:, g0:4:step, 16 - off:16 - off + T]

            link(nc.gpsimd.tensor_tensor(cols(b, 0), cols(ub, 0), cols(ub, 0, 1), ALU.add))
            link(nc.gpsimd.tensor_tensor(cols(c, 1), cols(b, 1), cols(b, 1, 2), ALU.add))
            link(nc.gpsimd.tensor_tensor(cols(b, 2), cols(c, 2), cols(c, 2, 4), ALU.add))
            link(nc.gpsimd.tensor_tensor(cols(c, 3), cols(b, 3), cols(b, 3, 8), ALU.add))
            rc = cst[:, C_RC:C_RC + 4 * T].rearrange("p (g t) -> p g t", g=4)
            for t, g0 in ((b, 0), (c, 1)):
                link(nc.gpsimd.tensor_tensor(cols(t, g0, 0, 2), cols(t, g0, 0, 2), rc[:, g0:4:2, :], ALU.mult))
                last = nc.gpsimd.tensor_tensor(cols(t, g0, 0, 2), cols(t, g0, 0, 2), cols(ub, g0, 0, 2), ALU.subtract)
                if g0 == 0:
                    link(last)
            last.then_inc(pooled_ready, 1)


        def pe_gfree(pe, l, g):
            pe.wait_ge(gfree[g % 2], 7 * l + g // 2 + 1)

        def pe_panel(pe, m, k, o, xh, xl, arrive=None, after=None):
            pe.wait_ge(lo_done, 4 * m + k + 1)
            wh, wl = w_hi[slot(k)], w_lo[slot(k)]
            for c in range(2):
                for kc in range(KC):
                    if c == 0 and arrive:
                        arrive(kc)
                    s = kc * 256 + c * P
                    last = mm3(o[:, c * T:(c + 1) * T], wh[:, s:s + P], wl[:, s:s + P], xh[:, kc, :], xl[:, kc, :],
                               kc == 0, kc == KC - 1)
            return last

        def pe_panel_rows(pe, m, k, o, xh, xl, first, last_panel):
            pe.wait_ge(lo_done, 4 * m + k + 1)
            wh, wl = w_hi[slot(k)], w_lo[slot(k)]
            for kk in range(2):
                for c in range(8):
                    s = kk * D + c * P
                    last = mm3(o[c // 2][:, (c % 2) * T:(c % 2 + 1) * T], wh[:, s:s + P], wl[:, s:s + P], xh(kk), xl(kk),
                               first and kk == 0 and c % 2 == 0, last_panel and kk == 1, skip=True)
            return last

        def pe_used(pe, last):
            last.then_inc(split_free, 1)

        MOD_AT = 448

        def pe_mod(pe, l, p0, p1):
            for mp in range(p0, p1):
                pe.wait_ge(mod_used, 2 + MOD_PANELS * l + mp + 1)
                for c in range(2):
                    col = MOD_AT + 2 * mp + c
                    last = nc.tensor.matmul(bank[7][:, col:col + 1], macc[:, mp % 2, c * P:(c + 1) * P], ones[:, 0:1],
                                            start=True, stop=True)
                last.then_inc(macc_free, 1)

        def pe_norm_sum(pe, q):
            for kc in range(KC):
                pe.wait_ge(sq_done, KC * q + kc + 1)
                last = nc.tensor.matmul(bank[6][:, 0:T], ones, tbuf[:, kc, :], start=kc == 0, stop=kc == KC - 1)
            last.then_inc(ss_done, 1)

        def mod_part(pe, l, part):
            pe.wait_ge(modc_ready, 4 * l + part + 1)

        def pe_layer(pe, l):
            m = 11 * l
            pe.wait_ge(lc_ready, 16 * l + 16)
            pe_mod(pe, l, 0, 8)
            pe_norm_sum(pe, 2 * l)

            def arrive(kc):
                pe.wait_ge(act_ready, 16 * l + kc + 1)

            G = lambda g: bank[4 + g % 2]
            for g, k in ((0, L_K0K1), (1, L_K2V0)):
                pe_gfree(pe, l, g)
                pe_used(pe, pe_panel(pe, m, k, G(g), act_hi, act_lo, arrive if g == 0 else None))
            mod_part(pe, l, 0)
            pe_mod(pe, l, 8, 12)
            pe_gfree(pe, l, 2)
            pe.wait_ge(lo_done, 4 * m + L_V1V2 + 1)
            wh, wl = w_hi[slot(L_V1V2)], w_lo[slot(L_V1V2)]
            for tt in range(TT):
                for kc in range(KC):
                    ts = slice(tt * P, (tt + 1) * P)
                    last = mm3(G(2)[:, tt * T:(tt + 1) * T], act_hi[:, kc, ts], act_lo[:, kc, ts],
                               wh[:, kc * 256:(kc + 1) * 256], wl[:, kc * 256:(kc + 1) * 256], kc == 0, kc == KC - 1)
            pe_used(pe, last)
            pe_gfree(pe, l, 3)
            pe.wait_ge(gw_lo, l + 1)
            for tt in range(TT):
                for kc in range(KC):
                    ts = slice(tt * P, (tt + 1) * P)
                    last = mm3(G(3)[:, tt * 24:(tt + 1) * 24], act_hi[:, kc, ts], act_lo[:, kc, ts], gwh[:, kc, :], gwl[:, kc, :],
                               kc == 0, kc == KC - 1)
            last.then_inc(gfull, 1)
            for g, k in ((4, L_Q0), (5, L_Q1)):
                pe_gfree(pe, l, g)
                pe_used(pe, pe_panel(pe, m, k, G(g), act_hi, act_lo))
            for j in range(3):
                if j == 0:
                    pe.wait_ge(nr_sq, 5 * l + 2)
                    pe.wait_ge(gfree[0], 7 * l + 2)
                    pe.wait_ge(gfree[1], 7 * l + 2)
                else:
                    pe.wait_ge(nr_sq, 5 * l + 2 + j)
                    pe.wait_ge(gfree[(j + 1) % 2], 7 * l + 4)
                if j == 2:
                    mod_part(pe, l, 1)
                    pe_mod(pe, l, 12, 16)
                    pe.wait_ge(nr_out, 4 * l + 1)
                o = 2 * (j % 2)
                nc.tensor.matmul(bank[o][:, :], cst[:, C_BD:C_BD + P], tbuf[:, 2 * j:2 * j + 2, :], start=True, stop=True)
                nc.tensor.matmul(bank[o + 1][:, :], cst[:, C_ROT:C_ROT + P], ybuf[j], start=True, stop=True).then_inc(nr_mm, 1)
            pe_mod(pe, l, 16, 18)
            pe.wait_ge(tb_lo, l + 1)
            pe.wait_ge(lo_done, 4 * m + L_CMP + 1)
            for jj in range(16):
                s = slice(jj * P, (jj + 1) * P)
                last = mm3(bank[6][:, 0:60], w_hi[slot(L_CMP)][:, s], w_lo[slot(L_CMP)][:, s], tbh[:, jj, :], tbl[:, jj, :],
                           jj == 0, jj == 15)
            pe_used(pe, last)
            def second_layer(kc):
                if kc == 0:
                    pe.wait_ge(cmp_s, l + 1)
                if kc == 1:
                    w2 = lc[:, LC_W2:LC_W2 + 64]
                    nc.tensor.matmul(bank[6][0:64, 64:79], w2[0:64, :], hs[0:64, 0:15], start=True, stop=True)
                    nc.tensor.matmul(bank[6][64:128, 64:79], w2[0:64, :], hs[0:64, 15:30], start=True, stop=True)
                    for v in range(2):
                        last = nc.tensor.matmul(bank[6][0:15, 128 + 64 * v:192 + 64 * v], hs[64:128, 30 + 15 * v:45 + 15 * v],
                                                w2[64:128, :], start=True, stop=True)
                    last.then_inc(cmp_w2, 1)

            for g, k in ((6, L_U0), (7, L_U1)):
                pe_gfree(pe, l, g)
                pe_used(pe, pe_panel(pe, m, k, G(g), act_hi, act_lo, second_layer if g == 7 else None))
            pe_mod(pe, l, 18, 20)
            pe.wait_ge(nr_sq, 5 * l + 5)
            pe.wait_ge(cmp_y, l + 1)
            nc.tensor.matmul(bank[6][:, 256:271], cst[:, C_BD:C_BD + P], sqc[:, 0:15], start=True, stop=True)
            nc.tensor.matmul(bank[6][:, 288:303], cst[:, C_ROT:C_ROT + P], ycmp, start=True, stop=True).then_inc(nr_mm, 1)
            pe.wait_ge(nr_out, 4 * l + 3)
            pe.wait_ge(masks_ready, 3)
            pe_scores(pe, l, 0, False)
            pe_scores(pe, l, 1, False)
            pe.wait_ge(nr_out, 4 * l + 4)
            pe_scores(pe, l, 0, True)
            pe_scores(pe, l, 1, True)
            mod_part(pe, l, 2)
            for i in range(8):
                pe_turn(pe, l, i)
                pe_pv(pe, l, i)
                if i + 2 < 8:
                    pe.wait_ge(at_exp, 8 * l + i + 1)
                    pe_scores(pe, l, i + 2, False)
                    pe_scores(pe, l, i + 2, True)
            pe.wait_ge(pooled_ready, l + 1)
            for g in range(4):
                if g % 2 == 0:
                    pe_gfree(pe, l, 12 + g // 2)
                src = wb[g % 2]
                last = nc.tensor.matmul(bank[4 + g // 2][:, (g % 2) * T:(g % 2 + 1) * T], lc[:, LC_PW + g * P:LC_PW + (g + 1) * P],
                                        src[:, g, 16:16 + T], start=True, stop=True)
                if g % 2:
                    last.then_inc(gfull, 1)
            for i in range(4):
                if i < 2:
                    pe.wait_ge(gfree[i], 7 * l + 8)
                    pe.wait_ge(gfree[1 - i], 7 * l + 8)
                else:
                    pe.wait_ge(x_ready, 16 * l + 8 + 2 * (i - 2) + 2)
                last = pe_panel(pe, m, L_OUT + i, bank[4 + i % 2], mix_hi, mix_lo)
                pe_used(pe, last)
            pe_norm_sum(pe, 2 * l + 1)
            pe_ff(pe, l, m, lambda kc: pe.wait_ge(act_ready, 16 * l + KC + kc + 1), 16 * l, L_FF)
            pe_mod(pe, l, 20, 24)

        def pe_ff(pe, l, m, arrive, j0, k0):
            def up(mm, k, jn, par, arr=None):
                pe.wait_ge(ff_relu, jn + 1)
                last = pe_panel(pe, mm, k, bank[4 + par], act_hi, act_lo, arr)
                pe_used(pe, last)

            def down(mm, k, jn, par, first, final):
                pe.wait_ge(ff_ready, 2 + jn + 1)
                last = pe_panel_rows(pe, mm, k, bank[0:4], lambda kk: ff_hi[:, par, kk * T:(kk + 1) * T],
                                     lambda kk: ff_lo[:, par, kk * T:(kk + 1) * T], first, final)
                pe_used(pe, last)

            up(m, k0, j0, 0, arrive)
            up(m, k0 + 1, j0 + 1, 1)
            down(m, k0 + 2, j0, 0, True, False)
            up(m, k0 + 3, j0 + 2, 0)
            down(m, k0 + 4, j0 + 1, 1, False, False)
            with pe.Fori(1, FF_STEPS // 2 - 1) as i:
                up(m + i, k0 + 1, j0 + 2 * i + 1, 1)
                down(m + i, k0 + 2, j0 + 2 * i, 0, False, False)
                up(m + i, k0 + 3, j0 + 2 * i + 2, 0)
                down(m + i, k0 + 4, j0 + 2 * i + 1, 1, False, False)
            e = m + FF_STEPS // 2 - 1
            up(e, k0 + 1, j0 + FF_STEPS - 1, 1)
            down(e, k0 + 2, j0 + FF_STEPS - 2, 0, False, False)
            down(e, k0 + 3, j0 + FF_STEPS - 1, 1, False, True)

        def pe_scores(pe, l, i, cmp):
            b, g = i // 2, i % 2
            h = slice(64 * g, 64 * g + 64)
            s0, s1 = bank[2 * (i % 2)], bank[2 * (i % 2) + 1]
            if cmp:
                for tt in range(TT):
                    o = s0[:, 256 + 16 * tt:271 + 16 * tt]
                    nc.tensor.matmul(o, qr[h, b, tt * P:(tt + 1) * P], kcmp[h, :], start=True, stop=False)
                    last = nc.tensor.matmul(o, idb[:, :], cmpmb[:, 16 * tt:16 * tt + 15], start=False, stop=True)
                last.then_inc(at_sc, 1)
                return
            for br in range(2):
                o = s0[:, br * P:(br + 1) * P]
                nc.tensor.matmul(o, qr[h, b, 0:P], kr[h, br, 0:P], start=True, stop=False)
                nc.tensor.matmul(o, idb[:, :], causb[:, :], start=False, stop=True)
            for br in range(2):
                o = s1[:, br * T:(br + 1) * T]
                nc.tensor.matmul(o, qr[h, b, P:T], kr[h, br, :], start=True, stop=False, skip_group_check=True)
                nc.tensor.matmul(o[:, P:T], idb[:, :], causb[:, :], start=False, stop=True, skip_group_check=True)

        def pe_turn(pe, l, i):
            pe.wait_ge(at_p, 8 * l + i + 1)
            if i:
                pe.wait_ge(at_ev0, 8 * l + i)
                pe.wait_ge(at_ev1, 8 * l + i)
            pb = pbuf[i % 2]
            for n in range(6):
                br, part = n // 3, n % 3
                src = pb[:, br * P:(br + 1) * P] if part == 0 else pb[:, 288 + br * T + (part - 1) * P:288 + br * T + part * P]
                nc.tensor.transpose(bank[6 + n // 4][:, (n % 4) * P:(n % 4 + 1) * P], src, ident)
            for tt in range(TT):
                last = nc.tensor.transpose(bank[7][0:15, T + tt * P:T + (tt + 1) * P], pb[:, 256 + 16 * tt:271 + 16 * tt], ident)
            last.then_inc(at_tr, 1)

        def pe_pv(pe, l, i):
            b, g = i // 2, i % 2
            o = bank[4 + b % 2][64 * g:64 * g + 64, 0:T]
            if g == 0:
                pe_gfree(pe, l, 8 + b)
            pe.wait_ge(at_ev0, 8 * l + i + 1)
            pe.wait_ge(at_ev1, 8 * l + i + 1)
            pt = pts[i % 2]
            for br in range(2):
                v = slice(br * P + 64 * g, br * P + 64 * g + 64)
                nc.tensor.matmul(o, vt[:, 0, v], pt[:, br * 384:br * 384 + T], start=br == 0, stop=False, skip_group_check=True)
                nc.tensor.matmul(o[:, P:T], vt[:, 1, v], pt[:, br * 384 + T:br * 384 + 384], start=False, stop=False, skip_group_check=True)
            nc.tensor.matmul(o, vcmp[0:15, 64 * g:64 * g + 64], pt[0:15, 768:1024], start=False, stop=True,
                             skip_group_check=True).then_inc(at_pv, 1)


        ACT_LINKS = 7

        def rsqrt(link, o, src, scale, eps):
            link(nc.scalar.activation(o, src, ACT.Ln, bias=eps, scale=scale))
            return nc.scalar.activation(o, o, ACT.Exp, scale=-0.5)

        def act_norm(act, l, q, link, shift, extra=()):
            for kc in range(KC):
                act.wait_ge(x_ready, 8 * q + kc + 1)
                nc.scalar.activation(tbuf[:, kc, :], x[:, kc, :], ACT.Square).then_inc(sq_done, 1)
            for f in extra:
                f()
            act.wait_ge(ss_done, q + 1)
            rsqrt(link, rs[:, :], bank[6][:, 0:T], 1.0 / D, cst[:, C_EPS:C_EPS + 1]).then_inc(rs_done, 1)
            for kc in range(KC):
                act.wait_ge(t_done, 8 * q + kc + 1)
                nc.scalar.activation(act_hi[:, kc, :], tbuf[:, kc, :], ACT.Identity, bias=modc[:, shift + kc:shift + kc + 1])\
                    .then_inc(act_his, 1)

        def act_layer(act, l, link):
            m = 11 * l
            used = lambda k: act.wait_ge(split_free, SPLIT + 4 * m + k + 1)
            act.wait_ge(lc_ready, 16 * l + 16)
            nc.scalar.activation(gwh[:, :, :], lc[:, LC_GW:LC_GW + 192].rearrange("p (k n) -> p k n", k=KC), ACT.Copy).then_inc(gw_hi, 1)
            act_norm(act, l, 2 * l, link, 0, (lambda: split_hi(act, m, 3),))
            G = lambda g: bank[4 + g % 2]
            used(L_K0K1)
            nc.scalar.activation(tbuf[:, 0, :], G(0)[:, T:2 * T], ACT.Square).then_inc(nr_sq, 1)
            for g in range(2):
                for j2 in range(2):
                    src = win(G(0), 64 * g, 64, [[2, 16], [16, 15]], j2)
                    last = nc.scalar.activation(tb[64 * j2:64 * j2 + 64, :, 15 * g:15 * g + 15], src, ACT.Copy)
            last.then_inc(tb_k, 1)
            split_hi(act, m, 4)
            used(L_K2V0)
            nc.scalar.activation(tbuf[:, 1, :], G(1)[:, 0:T], ACT.Square).then_inc(nr_sq, 1)
            split_hi(act, m, 5)
            split_hi(act, m, 6)
            act.wait_ge(tb_pe, l + 1)
            nc.scalar.activation(tbh[:, :, :], tb, ACT.Copy).then_inc(tb_hi, 1)
            act.wait_ge(gfull, 3 * l + 1)
            nc.scalar.activation(gts[:, :, :], G(3)[:, 0:48].rearrange("p (t n) -> p t n", t=TT), ACT.Exp, scale=-1.0).then_inc(gfree[1], 1)
            used(L_Q0)
            nc.scalar.activation(tbuf[:, 2:4, :], G(4)[:, :].rearrange("p (b t) -> p b t", b=2), ACT.Square).then_inc(nr_sq, 1)
            split_hi(act, m, 7)
            used(L_Q1)
            nc.scalar.activation(tbuf[:, 4:6, :], G(5)[:, :].rearrange("p (b t) -> p b t", b=2), ACT.Square).then_inc(nr_sq, 1)
            split_hi(act, m, 8)
            for j in range(3):
                act.wait_ge(nr_mm, 4 * l + j + 1)
                rsqrt(link, tbuf[:, 2 * j:2 * j + 2, :], bank[2 * (j % 2)][:, :].rearrange("p (b t) -> p b t", b=2), 1.0 / 64,
                      cst[:, C_EPS:C_EPS + 1]).then_inc(nr_rs, 1)
            used(L_CMP)
            nc.scalar.activation(ce, bank[6][:, 0:60], ACT.Exp, scale=-1.0).then_inc(cmp_e, 1)
            split_hi(act, m, 9)
            used(L_U0)
            nc.scalar.activation(ub[:, 0:2, 16:16 + T], G(6)[:, :].rearrange("p (b t) -> p b t", b=2), ACT.Copy).then_inc(gfree[0], 1)
            split_hi(act, m, 10)
            act.wait_ge(cmp_w2, l + 1)
            nc.scalar.activation(sqc[:, 0:15], bank[6][:, 64:79], ACT.Square).then_inc(nr_sq, 1)
            used(L_U1)
            link(nc.scalar.activation(ub[:, 2:4, 16:16 + T], G(7)[:, :].rearrange("p (b t) -> p b t", b=2), ACT.Copy))
            act.sem_inc(gfree[1], 1)
            act.sem_inc(u_copied, 2)
            split_hi(act, m, 11)
            act.wait_ge(nr_mm, 4 * l + 4)
            rsqrt(link, sqc[:, 16:31], bank[6][:, 256:271], 1.0 / 64, cst[:, C_EPS:C_EPS + 1]).then_inc(nr_rs, 1)
            for i in range(8):
                s0, s1, pb = bank[2 * (i % 2)], bank[2 * (i % 2) + 1], pbuf[i % 2]
                if i >= 2:
                    act.wait_ge(at_tr, 8 * l + i - 1)
                act.wait_ge(at_nm, 8 * l + i + 1)
                for n, (src, dst) in enumerate((
                        (s0[:, 0:P], pb[:, 0:P]), (s0[:, P:T], pb[:, P:T]),
                        (s0[:, 256:271], pb[:, 256:271]), (s0[:, 272:287], pb[:, 272:287]),
                        (s1[:, 0:T], pb[:, 288:288 + T]), (s1[:, T:2 * T], pb[:, 288 + T:288 + 2 * T]))):
                    last = nc.scalar.activation(dst, src, ACT.Exp, bias=nm[:, i % 2, n:n + 1], accum_out=dens[:, i % 2, n:n + 1])
                last.then_inc(at_exp, 1)
                if i >= 1:
                    act_pt(act, l, i - 1)
                if i >= 3 and i % 2 == 1:
                    act_mixed(act, l, (i - 3) // 2)
            act_pt(act, l, 7)
            act_mixed(act, l, 3)
            for g in range(4):
                act.wait_ge(gfull, 3 * l + 2 + g // 2)
                nc.scalar.activation(mix_hi[:, g, :], bank[4 + g // 2][:, (g % 2) * T:(g % 2 + 1) * T], ACT.Copy,
                                     scale=lc[:, LC_PS + g:LC_PS + g + 1]).then_inc(mix_his, 1)
            for k in range(3):
                split_hi(act, m, 12 + k)
            act_norm(act, l, 2 * l + 1, link, 24)
            act_ff(act, l, m, L_FF, 16 * l)

        def act_pt(act, l, i):
            act.wait_ge(at_tr, 8 * l + i + 1)
            if i >= 2:
                act.wait_ge(at_pv, 8 * l + i - 1)
            nc.scalar.activation(pts[i % 2][:, 0:512], bank[6][:, :], ACT.Copy).then_inc(at_ev0, 1)

        def act_mixed(act, l, b):
            act.wait_ge(at_pv, 8 * l + 2 * b + 2)
            nc.scalar.activation(mix_hi[:, 4 + b, :], bank[4 + b % 2][:, 0:T], ACT.Copy).then_inc(mix_his, 1)

        def act_ff(act, l, m, k0, j0, final=False):
            def step(mm, jn, kf, par, kd, s):
                act.wait_ge(split_free, SPLIT + 4 * mm + kf + 1)
                act.wait_ge(ff_ready, jn + 1)
                nc.scalar.activation(fr[par], bank[4 + par][:, :], ACT.Relu).then_inc(ff_relu, 1)
                for k in s[:1]:
                    split_hi(act, mm, k)
                act.wait_ge(ff_sq, jn + 1)
                if kd is not None:
                    act.wait_ge(split_free, SPLIT + 4 * mm + kd + 1)
                nc.scalar.activation(ff_hi[:, par, :], fr[par], ACT.Copy).then_inc(ff_his, 1)
                for k in s[1:]:
                    split_hi(act, mm, k)

            ff_schedule(act, m, k0, j0, step, final)

        def ff_schedule(eng, m, k0, j0, step, final):
            step(m, j0, k0, 0, None, (k0 + 3, k0 + 4))
            step(m, j0 + 1, k0 + 1, 1, None, (k0 + 5, k0 + 6))
            with eng.Fori(1, FF_STEPS // 2 - 1) as i:
                step(m + i, j0 + 2 * i, k0 - 1, 0, k0 - 2, (k0 + 3, k0 + 4))
                step(m + i, j0 + 2 * i + 1, k0 + 1, 1, k0, (k0 + 5, k0 + 6))
            e = m + FF_STEPS // 2 - 1
            step(e, j0 + FF_STEPS - 2, k0 - 1, 0, k0 - 2, (k0 + 3,) if final else (k0 + 3, k0 + 4))
            step(e, j0 + FF_STEPS - 1, k0 + 1, 1, k0, () if final else (k0 + 5, k0 + 6))


        DVE_LINKS = 32 + 7 * MOD_PANELS

        def dve_mod(dve, l, p0, p1, link):
            for mp in range(p0, p1):
                dve.wait_ge(modraw[mp % 2], 16 * (MOD_PANELS // 2 * l + mp // 2 + 1))
                dve.wait_ge(macc_free, MOD_PANELS * l + mp + 1)
                o = macc[:, mp % 2, :]
                link(nc.vector.tensor_scalar(o, modw[:, mp % 2, 0:256], cact[:, 0:1], None, ALU.mult))
                for kc in range(1, KC):
                    ins = nc.vector.scalar_tensor_tensor(o, modw[:, mp % 2, kc * 256:kc * 256 + 256], cact[:, kc:kc + 1], o,
                                                         ALU.mult, ALU.add)
                    if kc < KC - 1:
                        link(ins)
                ins.then_inc(mod_used, 1)

        def dve_modc(dve, l, part, c0, c1, link):
            dve.wait_ge(macc_free, 2 + MOD_PANELS * l + c1 // 2)
            nc.vector.tensor_tensor(modc[:, c0:c1], bank[7][:, MOD_AT + c0:MOD_AT + c1], lc[:, LC_BM + c0:LC_BM + c1], ALU.add)\
                .then_inc(modc_ready, 1)
            dve.wait_ge(modc_ready, 4 * l + part + 1)

        def dve_norm(dve, q, g0, shift):
            dve.wait_ge(rs_done, q + 1)
            for kc in range(KC + 1):
                if kc < KC:
                    nc.vector.scalar_tensor_tensor(tbuf[:, kc, :], x[:, kc, :], gcol[:, g0 + kc:g0 + kc + 1], rs[:, :], ALU.mult, ALU.mult)\
                        .then_inc(t_done, 1)
                if kc:
                    c = kc - 1
                    dve.wait_ge(act_his, 8 * q + c + 1)
                    nc.vector.scalar_tensor_tensor(act_lo[:, c, :], tbuf[:, c, :], modc[:, shift + c:shift + c + 1],
                                                   act_hi[:, c, :].bitcast(F32), ALU.add, ALU.subtract).then_inc(act_ready, 1)

        def dve_layer(dve, l, link):
            m = 11 * l
            used = lambda k: dve.wait_ge(split_free, SPLIT + 4 * m + k + 1)
            G = lambda g: bank[4 + g % 2]
            two = lambda ap: ap.rearrange("p (b t) -> p b t", b=2)
            dve.wait_ge(gw_hi, l + 1)
            nc.vector.tensor_tensor(gwl[:, :, :], lc[:, LC_GW:LC_GW + 192].rearrange("p (k n) -> p k n", k=KC), gwh[:, :, :].bitcast(F32),
                                    ALU.subtract).then_inc(gw_lo, 1)
            dve_mod(dve, l, 0, 8, link)
            dve_modc(dve, l, 0, 0, 16, link)
            link(nc.vector.scalar_tensor_tensor(gcol[:, 0:KC], modc[:, 8:16], 1.0, lc[:, LC_N1:LC_N1 + KC], ALU.add, ALU.mult))
            split_lo(dve, m, 3)
            dve_norm(dve, 2 * l, 0, 0)
            dve_mod(dve, l, 8, 12, link)
            used(L_K0K1)
            dve.wait_ge(tb_k, l + 1)
            nc.vector.tensor_scalar(ybuf[0][:, 0, :], G(0)[:, T:2 * T], lc[:, LC_KN + 1:LC_KN + 2], None, ALU.mult).then_inc(gfree[0], 1)
            split_lo(dve, m, 4)
            used(L_K2V0)
            dve.wait_ge(nr_sq, 5 * l + 2)
            for g in range(2):
                for j2 in range(2):
                    src = win(G(1), 64 * g, 64, [[2, 16], [16, 15]], T + j2)
                    last = nc.vector.tensor_copy(tb[64 * j2:64 * j2 + 64, :, 30 + 15 * g:45 + 15 * g], src)
            last.then_inc(tb_v, 1)
            nc.vector.tensor_scalar(ybuf[0][:, 1, :], G(1)[:, 0:T], lc[:, LC_KN + 2:LC_KN + 3], None, ALU.mult).then_inc(gfree[1], 1)
            split_lo(dve, m, 5)
            dve.wait_ge(tb_v, l + 1)
            pe_bc = win(lc, 0, P, [[2, 16], [1, 2], [0, 30]], LC_PE)
            tb4 = tb.rearrange("p j (v n) -> p j v n", v=2)
            nc.vector.tensor_tensor(tb4, tb4, pe_bc, ALU.add).then_inc(tb_pe, 1)
            used(L_V1V2)
            nc.vector.tensor_copy(vt, two(G(2)[:, :])).then_inc(gfree[0], 1)
            split_lo(dve, m, 6)
            dve_modc(dve, l, 1, 16, 24, link)
            dve.wait_ge(tb_hi, l + 1)
            nc.vector.tensor_tensor(tbl[:, :, :], tb, tbh[:, :, :].bitcast(F32), ALU.subtract).then_inc(tb_lo, 1)
            dve.wait_ge(gfree[1], 7 * l + 3)
            link(nc.vector.tensor_scalar(gts[:, :, :], gts[:, :, :], 1.0, None, ALU.add))
            link(nc.vector.reciprocal(gts[:, :, :], gts[:, :, :]))
            link(nc.vector.tensor_scalar(gts[:, 0, 0:24:3], gts[:, 0, 0:24:3], cst[:, C_VALID:C_VALID + 1], None, ALU.mult))
            for j in (1, 2):
                dve.wait_ge(nr_sq, 5 * l + 2 + j)
                nc.vector.tensor_scalar(ybuf[j], two(G(3 + j)[:, :]), lc[:, LC_QN:LC_QN + 1], 0.125, ALU.mult, ALU.mult).then_inc(gfree[(j + 1) % 2], 1)
                split_lo(dve, m, 6 + j)
                dve_mod(dve, l, 10 + 2 * j, 12 + 2 * j, link)
            for j in range(3):
                dst = kr if j == 0 else qr[:, 2 * j - 2:2 * j, :]
                dve.wait_ge(nr_mm, 4 * l + j + 1)
                link(nc.vector.tensor_tensor(dst, two(bank[2 * (j % 2) + 1][:, :]), cst[:, C_SIN:C_SIN + T].unsqueeze(1).to_broadcast([P, 2, T]), ALU.mult))
                dve.wait_ge(nr_yc, 3 * l + j + 1)
                link(nc.vector.tensor_tensor(dst, dst, ybuf[j], ALU.add))
                dve.wait_ge(nr_rs, 4 * l + j + 1)
                nc.vector.tensor_tensor(dst, dst, tbuf[:, 2 * j:2 * j + 2, :], ALU.mult).then_inc(nr_out, 1)
                if j == 0:
                    dve_mod(dve, l, 16, 18, link)
            dve.wait_ge(cmp_e, l + 1)
            link(nc.vector.tensor_scalar(ce, ce, 1.0, None, ALU.add))
            link(nc.vector.reciprocal(ce, ce))
            nc.vector.tensor_tensor(hs, bank[6][:, 0:60], ce, ALU.mult).then_inc(cmp_s, 1)
            split_lo(dve, m, 9)
            dve_mod(dve, l, 18, 20, link)
            split_lo(dve, m, 10)
            dve.wait_ge(cmp_w2, l + 1)
            dve.wait_ge(nr_sq, 5 * l + 5)
            nc.vector.tensor_copy(vcmp[0:15, :], bank[6][0:15, P:T])
            nc.vector.tensor_scalar(ycmp, bank[6][:, 64:79], lc[:, LC_KN:LC_KN + 1], None, ALU.mult).then_inc(cmp_y, 1)
            split_lo(dve, m, 11)
            dve.wait_ge(nr_mm, 4 * l + 4)
            link(nc.vector.tensor_tensor(ycmp, ycmp, cst[:, C_CCOS:C_CCOS + 15], ALU.mult))
            dve.wait_ge(nr_rs, 4 * l + 4)
            link(nc.vector.tensor_tensor(kcmp, bank[6][:, 288:303], cst[:, C_CSIN:C_CSIN + 15], ALU.mult))
            link(nc.vector.tensor_tensor(kcmp, kcmp, ycmp, ALU.add))
            nc.vector.tensor_tensor(kcmp, kcmp, sqc[:, 16:31], ALU.mult).then_inc(nr_out, 1)
            dve_modc(dve, l, 2, 24, 40, link)
            link(nc.vector.scalar_tensor_tensor(gcol[:, KC:2 * KC], modc[:, 32:40], 1.0, lc[:, LC_N2:LC_N2 + KC], ALU.add, ALU.mult))

            def maxima(i):
                s0, s1, o = bank[2 * (i % 2)], bank[2 * (i % 2) + 1], nm[:, i % 2, :]
                dve.wait_ge(at_sc, 8 * l + i + 1)
                nc.vector.tensor_reduce(o[:, 0:2], two(s0[:, 0:T]), AX.X, ALU.max, negate=True)
                nc.vector.tensor_reduce(o[:, 2:4], win(s0, 0, P, [[16, 2], [1, 15]], T), AX.X, ALU.max, negate=True)
                nc.vector.tensor_reduce(o[:, 4:6], two(s1[:, :]), AX.X, ALU.max, negate=True).then_inc(at_nm, 1)

            def weigh(i):
                b, g = i // 2, i % 2
                pb, f, d = pbuf[i % 2], fac[:, i % 2, :], dens[:, i % 2, :]
                dve.wait_ge(at_exp, 8 * l + i + 1)
                link(nc.vector.reciprocal(f, d))
                h0 = 3 * (4 * g + b)
                nc.vector.tensor_tensor(f[:, 0:2], f[:, 0:2], gts[:, 0, h0 + 1:h0 + 3], ALU.mult)
                nc.vector.tensor_tensor(f[:, 2:4], f[:, 2:4], gts[:, :, h0], ALU.mult)
                link(nc.vector.tensor_tensor(f[:, 4:6], f[:, 4:6], gts[:, 1, h0 + 1:h0 + 3], ALU.mult))
                for n, (c0, w) in enumerate(((0, P), (P, P), (256, 15), (272, 15), (288, T), (288 + T, T))):
                    last = nc.vector.tensor_scalar(pb[:, c0:c0 + w], pb[:, c0:c0 + w], f[:, n:n + 1], None, ALU.mult)
                last.then_inc(at_p, 1)

            def copy_pt(i):
                dve.wait_ge(at_tr, 8 * l + i + 1)
                if i >= 2:
                    dve.wait_ge(at_pv, 8 * l + i - 1)
                nc.vector.tensor_copy(pts[i % 2][:, 512:768], bank[7][:, 0:T])
                nc.vector.tensor_copy(pts[i % 2][0:15, 768:1024], bank[7][0:15, T:2 * T]).then_inc(at_ev1, 1)

            def mixed(b):
                dve.wait_ge(mix_his, 8 * l + b + 1)
                nc.vector.tensor_tensor(mix_lo[:, 4 + b, :], bank[4 + b % 2][:, 0:T], mix_hi[:, 4 + b, :].bitcast(F32), ALU.subtract)\
                    .then_inc(gfree[b % 2], 1)

            maxima(0)
            for i in range(8):
                if i + 1 < 8:
                    maxima(i + 1)
                weigh(i)
                copy_pt(i)
                if i >= 3 and i % 2 == 1:
                    mixed((i - 3) // 2)
            mixed(3)
            for g in range(4):
                dve.wait_ge(mix_his, 8 * l + 4 + g // 2 * 2 + 2)
                last = nc.vector.scalar_tensor_tensor(mix_lo[:, g, :], bank[4 + g // 2][:, (g % 2) * T:(g % 2 + 1) * T],
                                                      lc[:, LC_PS + g:LC_PS + g + 1], mix_hi[:, g, :].bitcast(F32), ALU.mult, ALU.subtract)
                if g % 2:
                    last.then_inc(gfree[g // 2], 1)
            for i in range(4):
                if i < 3:
                    split_lo(dve, m, 12 + i)
                used(L_OUT + i)
                for c in range(2):
                    kc = 2 * i + c
                    nc.vector.scalar_tensor_tensor(x[:, kc, :], bank[4 + i % 2][:, c * T:(c + 1) * T], modc[:, 16 + kc:17 + kc], x[:, kc, :],
                                                   ALU.mult, ALU.add).then_inc(x_ready, 1)
            dve_norm(dve, 2 * l + 1, KC, 24)
            dve_mod(dve, l, 20, 22, link)
            dve_ff(dve, m, L_FF, 16 * l)
            dve_mod(dve, l, 22, 24, link)
            dve_modc(dve, l, 3, 40, 48, link)
            dve.wait_ge(split_free, SPLIT + 4 * m + L_PANELS)
            for kc in range(KC):
                nc.vector.scalar_tensor_tensor(x[:, kc, :], bank[kc // 2][:, (kc % 2) * T:(kc % 2 + 1) * T], modc[:, 40 + kc:41 + kc],
                                               x[:, kc, :], ALU.mult, ALU.add).then_inc(x_ready, 1)

        def dve_ff(dve, m, k0, j0, final=False):
            def step(mm, jn, kf, par, kd, s):
                dve.wait_ge(ff_relu, 2 + jn + 1)
                nc.vector.tensor_tensor(fr[par], fr[par], fr[par], ALU.mult).then_inc(ff_sq, 1)
                for k in s[:1]:
                    split_lo(dve, mm, k)
                dve.wait_ge(ff_his, jn + 1)
                nc.vector.tensor_tensor(ff_lo[:, par, :], fr[par], ff_hi[:, par, :].bitcast(F32), ALU.subtract).then_inc(ff_ready, 1)
                for k in s[1:]:
                    split_lo(dve, mm, k)

            ff_schedule(dve, m, k0, j0, step, final)

        M2 = L_PANELS // SPLIT * layers
        used2 = lambda eng, k: eng.wait_ge(split_free, SPLIT + 4 * M2 + k + 1)
        free2 = lambda eng, k: eng.wait_ge(gfree[k % 2], 7 * layers + k // 2 + 1)
        G2 = lambda k: bank[4 + k % 2]
        blocks2 = lambda ap: ap.rearrange("p (b t) -> p b t", b=2)
        XR = 16 * layers + 8

        dt_mm, dt_y, dt_n, dt_e, dt_done, dt_tr, dt_cols = [sem(n) for n in ("dt_mm", "dt_y", "dt_n", "dt_e", "dt_done", "dt_tr", "dt_cols")]
        pads_ready = sem("pads_ready")
        alog_e = sem("alog_e")
        d_stored = sem("d_stored")
        lc2_ready = sem("lc2_ready")
        dist_ready = sem("dist_ready")
        s2_sc = sem("s2_sc")
        s2_nm = sem("s2_nm")
        s2_exp = sem("s2_exp")
        s2_p = sem("s2_p")
        s2_tr = sem("s2_tr")
        s2_ev0, s2_ev1 = sem("s2_ev0"), sem("s2_ev1")
        s2_pv = sem("s2_pv")
        s2_hi, s2_lo = sem("s2_hi"), sem("s2_lo")
        conv_done = sem("conv_done")
        silu_done = sem("silu_done")
        cb_mm, cb_done = sem("cb_mm"), sem("cb_done")
        xt_mm0, xt_mm1, xt_done0, xt_done1 = sem("xt_mm0"), sem("xt_mm1"), sem("xt_done0"), sem("xt_done1")
        db_ready = [sem("db_ready0"), sem("db_ready1")]
        e_sub = sem("e_sub")
        e_mask = sem("e_mask")
        e_exp = sem("e_exp")
        e_mul = sem("e_mul")
        e_used = sem("e_used")
        y_out = sem("y_out")
        z_silu = sem("z_silu")
        y_gated = sem("y_gated")
        y_sq = sem("y_sq")
        y_ss = sem("y_ss")
        y_rs = sem("y_rs")
        y_fin = sem("y_fin")
        y_hi, y_lo = sem("y_hi"), sem("y_lo")
        gates_done = sem("gates_done")
        att_proj = sem("att_proj")
        mx_sum, mx_hi, mx_lo = sem("mx_sum"), sem("mx_hi"), sem("mx_lo")
        x2_ready = sem("x2_ready")
        ln_sum, ln_mean, ln_c, ln_sq, ln_ss, ln_rs, ln_t, ln_hi, ln_x, ln_lo = [
            sem(n) for n in ("ln_sum", "ln_mean", "ln_c", "ln_sq", "ln_ss", "ln_rs", "ln_t", "ln_hi", "ln_x", "ln_lo")]
        o_turned, o_copied = sem("o_turned"), sem("o_copied")

        at[0] = 0
        xb = area(24 * T, 24, T)
        zb_at = at[0]
        zb = area(16 * T, 16, T)
        xt_at = at[0]
        xt = area(8 * T, 2, TT, 2 * T)
        cb = area(4 * T, 2, TT, T)
        eb = [area(6 * T, 4, 3 * P) for _ in range(2)]
        work_at = at[0] - 12 * T
        lc2_at = at[0]
        lc2 = area(LC2)
        dtt = area(T, 2, TT, 64)
        gb = arena[:, xt_at:xt_at + 16 * T].rearrange("p (b t) -> p b t", b=16)
        sq2 = arena[:, xt_at + 16 * T:xt_at + 20 * T].rearrange("p (b t) -> p b t", b=4)
        rs2 = arena[:, xt_at + 20 * T:xt_at + 21 * T]
        v2 = arena[:, zb_at:zb_at + 6 * T].rearrange("p (t n) -> p t n", t=TT)
        pp = [arena[:, zb_at + (6 + 3 * i) * T:zb_at + (9 + 3 * i) * T] for i in range(2)]
        dist = arena[:, zb_at + 12 * T:zb_at + 16 * T + 2 * T].rearrange("p (t a s) -> p t a s", t=TT, a=3)
        pt2 = arena[:, xt_at + 2 * T:xt_at + 8 * T].rearrange("p (n t) -> p n t", n=6)
        up = [arena[:, work_at + i * 520:work_at + (i + 1) * 520].rearrange("p (b t) -> p b t", b=2) for i in range(2)]
        dw = [arena[0:64, work_at + 1040 + i * T:work_at + 1040 + (i + 1) * T] for i in range(6)]
        qk = mixf[:, 0:12 * T].rearrange("p (b t) -> p b t", b=12)
        db = [mixf[:, i * 8 * T:(i + 1) * 8 * T].rearrange("p (d h t) -> p d h t", d=2, h=4) for i in range(2)]
        m2 = zb[:, 0:8, :]
        mx = zb[:, 8:16, :]
        tb2 = xb[:, 0:8, :]
        obuf = xb[:, 8:16, :].rearrange("p b t -> p (b t)").rearrange("p (t d) -> p t d", t=TT)
        ea = small[0:64, 158:159]
        dens2, nm2 = small[:, 150:152], small[:, 152:154]
        dscr = nc.dram_tensor("dscr", (64, T), F32, kind="Internal").ap()
        ATT_SLOT = {0: 0, 1: 1, 3: 2, 4: 3, 6: 4, 7: 5, 9: 6, 10: 7}
        PV_SLOT = {2: 0, 5: 1, 8: 2, 11: 3}
        ALPHA = 2.0 ** 0.25
        slope = lambda h: 2.0 ** (-8.0 * (h + 1) / 12)

        def head2(p, j):
            h = 4 * p + j
            return h // 2, slice(64 * (h % 2), 64 * (h % 2) + 64), h

        def finish(sp):
            load(sp, M2, 5)
            with sp.Fori(0, 19) as i:
                for k in (6, 7, 8, 9):
                    load(sp, M2 + i, k)
            sp.wait_ge(o_copied, 4)
            sp.dma_start(out.rearrange("b (t p) d -> p (b t) d", p=P), obuf).then_inc(out_written, 16)
            sp.wait_ge(out_written, 16)
            sp.wait_ge(d_stored, 16)

        def pool_second(pool):
            pool.wait_ge(x_ready, 16 * layers)
            pool.dma_start(lc2, a["lc2"]).then_inc(lc2_ready, 16)
            pool.wait_ge(x_ready, XR)
            pool.dma_start(dist.rearrange("p t a s -> p (t a s)"), a["dist"]).then_inc(dist_ready, 16)
            for i in range(2):
                for c0 in (0, 258):
                    last = nc.gpsimd.memset(up[i][:, :, c0:c0 + 2], 0.0)
            last.then_inc(pads_ready, 1)
            pool.wait_ge(dt_done, 1)
            pool.dma_start(dscr, dw[5]).then_inc(d_stored, 16)
            pool.wait_ge(d_stored, 16)
            pool.wait_ge(s2_tr, 8)

            def fetch(hu):
                for d in range(2):
                    src = dscr[32 * d + 4 * hu:32 * d + 4 * hu + 4, :].rearrange("h t -> (h t)").partition_broadcast(P)
                    pool.dma_start(db[hu % 2][:, d, :, :].rearrange("p h t -> p (h t)"), src).then_inc(db_ready[hu % 2], 16)

            fetch(0)
            fetch(1)
            pool.wait_ge(dt_cols, 1)
            pool.wait_ge(conv_done, 12)
            for e in range(16):
                hu, st = e // 2, e % 2
                if st == 0:
                    pool.wait_ge(db_ready[hu % 2], 32 * (hu // 2 + 1))
                if e >= 2:
                    pool.wait_ge(e_used, e - 1)
                o, d = eb[e % 2], db[hu % 2]
                far, near = st, 1 - st
                cols = lambda dr: dtt[:, 0, st, 32 * dr + 4 * hu:32 * dr + 4 * hu + 4].unsqueeze(2)
                nc.gpsimd.tensor_tensor(o[:, :, 0:T], d[:, far, :, :], cols(far).to_broadcast([P, 4, T]), ALU.subtract)
                nc.gpsimd.tensor_tensor(o[:, :, T:T + P], d[:, near, :, st * P:(st + 1) * P], cols(near).to_broadcast([P, 4, P]),
                                        ALU.subtract).then_inc(e_sub, 1)
                if st and hu + 2 < 8:
                    pool.wait_ge(e_sub, e + 1)
                    fetch(hu + 2)

        def pe_second(pe):
            arrive = lambda kc: pe.wait_ge(act_ready, 16 * layers + kc + 1)

            def panel2(k, arr=None):
                free2(pe, k)
                pe_used(pe, pe_panel(pe, M2, k, G2(k), act_hi, act_lo, arr))

            for k in range(6):
                panel2(k, arrive if k == 0 else None)
            for k in range(6, 9):
                free2(pe, k)
                pe.wait_ge(lo_done, 4 * M2 + k + 1)
                for tt in range(TT):
                    ts = slice(tt * P, (tt + 1) * P)
                    for kc in range(KC):
                        last = mm3(G2(k)[:, tt * T:(tt + 1) * T], act_hi[:, kc, ts], act_lo[:, kc, ts],
                                   w_hi[slot(k)][:, kc * 256:(kc + 1) * 256], w_lo[slot(k)][:, kc * 256:(kc + 1) * 256], kc == 0, kc == KC - 1)
                pe_used(pe, last)
            pe.wait_ge(lc2_ready, 16)
            for kc in range(KC):
                last = nc.tensor.matmul(bank[6][0:64, 0:T], lc2[:, L2_WDT + 64 * kc:L2_WDT + 64 * kc + 64], x[:, kc, :],
                                        start=kc == 0, stop=kc == KC - 1)
            last.then_inc(dt_mm, 1)
            scores2(pe, 0)
            scores2(pe, 1)
            for i in range(12):
                panel2(9 + i)
                if i == 0:
                    pe.wait_ge(dt_done, 1)
                    for n in range(2):
                        for tt in range(TT):
                            last = nc.tensor.transpose(bank[7][:, (2 * n + tt) * 64:(2 * n + tt + 1) * 64],
                                                       dw[(5, 2)[n]][:, tt * P:(tt + 1) * P], ident[0:64, 0:64])
                    last.then_inc(dt_tr, 1)
                if i in ATT_SLOT:
                    u = ATT_SLOT[i]
                    pe.wait_ge(s2_p, u + 1)
                    if u:
                        pe.wait_ge(s2_ev0, u)
                        pe.wait_ge(s2_ev1, u)
                    else:
                        pe.wait_ge(dt_cols, 1)
                    if u in (4,):
                        pe.wait_ge(s2_lo, u // 4)
                    for n in range(6):
                        last = nc.tensor.transpose(bank[6 + n // 4][:, (n % 4) * P:(n % 4 + 1) * P], pp[u % 2][:, n * P:(n + 1) * P], ident)
                    last.then_inc(s2_tr, 1)
                    if u + 2 < 8:
                        pe.wait_ge(s2_nm, u + 1)
                        scores2(pe, u + 2)
                if i in PV_SLOT:
                    j = PV_SLOT[i]
                    pe.wait_ge(s2_ev0, 2 * j + 2)
                    pe.wait_ge(s2_ev1, 2 * j + 2)
                    o = bank[7][64 * (j % 2):64 * (j % 2) + 64, T:2 * T]
                    for n in range(6):
                        h = 4 * (n // 2) + j
                        last = nc.tensor.matmul(o, v2[:, n % 2, 64 * h:64 * h + 64], pt2[:, n, :], start=n == 0, stop=n == 5)
                    last.then_inc(s2_pv, 1)

            def prepare(g):
                if g == 0:
                    pe.wait_ge(s2_lo, 2)
                    pe.wait_ge(silu_done, 3)
                else:
                    pe.wait_ge(xt_done1, g)
                for st in range(TT):
                    last = nc.tensor.matmul(bank[7][:, st * T:(st + 1) * T], xb[:, 16 + g, st * P:(st + 1) * P], xb[:, 20 + g, :],
                                            start=True, stop=True)
                last.then_inc(cb_mm, 1)
                if g:
                    pe.wait_ge(xt_done0, g)
                for st in range(TT):
                    if st:
                        pe.wait_ge(cb_done, g + 1)
                    for b in range(4):
                        last = nc.tensor.transpose(bank[6 + st][:, b * P:(b + 1) * P], xb[:, 4 * g + b, st * P:(st + 1) * P], ident)
                    last.then_inc((xt_mm0, xt_mm1)[st], 1)

            prepare(0)
            for hu in range(8):
                g = hu // 2
                panel2(21 + hu)
                if hu % 2 and g < 3:
                    prepare(g + 1)
                if hu == 0 or hu % 2 == 0:
                    pe.wait_ge(xt_done0, g + 1)
                    pe.wait_ge(xt_done1, g + 1)
                if hu >= 4:
                    pe.wait_ge(y_out, hu - 3)
                for st in range(TT):
                    e = 2 * hu + st
                    pe.wait_ge(e_mul, e + 1)
                    for h in range(4):
                        o = bank[hu % 4][64 * (h % 2):64 * (h % 2) + 64, (h // 2) * T:(h // 2 + 1) * T]
                        w = xt[:, g % 2, st, 64 * (4 * (hu % 2) + h):64 * (4 * (hu % 2) + h) + 64]
                        nc.tensor.matmul(o, w, eb[e % 2][:, h, 0:T], start=st == 0 and h < 2, stop=False, skip_group_check=True)
                        last = nc.tensor.matmul(o[:, st * P:(st + 1) * P], w, eb[e % 2][:, h, T:T + P], start=False, stop=st == 1,
                                                skip_group_check=True)
                    last.then_inc(e_used, 1)
            for i in range(8):
                panel2(29 + i)
                if i % 2:
                    n = i // 2
                    pe.wait_ge(y_sq, n + 1)
                    if n:
                        pe.wait_ge(y_rs, n)
                    else:
                        pe.wait_ge(xt_done0, 4)
                    for b in range(4):
                        last = nc.tensor.matmul(bank[6][:, 0:T], ones, sq2[:, b, :], start=b == 0, stop=b == 3)
                    last.then_inc(y_ss, 1)
            free2(pe, 37)
            free2(pe, 38)
            pe.wait_ge(y_rs, 4)
            pe.wait_ge(xt_done1, 4)
            pe.wait_ge(s2_lo, 2)
            pe_used(pe, pe_panel_rows(pe, M2, 37, bank[4:8], lambda kk: ff_hi[:, 0, kk * T:(kk + 1) * T],
                                      lambda kk: ff_lo[:, 0, kk * T:(kk + 1) * T], True, True))
            pe.wait_ge(y_out, 8)
            for n in range(8):
                if n % 2 == 0:
                    pe.wait_ge(y_lo, n // 2 + 1)
                hi, lo = (mix_hi, mix_lo) if n < 4 else (act_hi, act_lo)
                c = 2 * n % 8
                pe_used(pe, pe_panel_rows(pe, M2, 38 + n, bank[0:4], lambda kk: hi[:, c + kk, :], lambda kk: lo[:, c + kk, :], n == 0, n == 7))
            pe.wait_ge(att_proj, 4)
            for n in range(4):
                if n == 2:
                    pe.wait_ge(x2_ready, 2)
                if n == 3:
                    pe.wait_ge(x2_ready, 4)
                pe_used(pe, pe_panel(pe, M2, 46 + n, bank[4 + n % 2], mix_hi, mix_lo,
                                     (lambda kc: pe.wait_ge(mx_lo, kc // 2 + 1)) if n == 0 else None))
            pe_layer_norm(pe, 0)
            pe_ff(pe, layers, M2, lambda kc: pe.wait_ge(ln_lo, kc + 1), 16 * layers, 50)
            pe_layer_norm(pe, 1)
            for c in range(4):
                for kc in (2 * c, 2 * c + 1):
                    pe.wait_ge(ln_x, 8 + kc + 1)
                    for tt in range(TT):
                        last = nc.tensor.transpose(bank[c][:, tt * T + (kc % 2) * P:tt * T + (kc % 2 + 1) * P], x[:, kc, tt * P:(tt + 1) * P], ident)
                last.then_inc(o_turned, 1)

        def scores2(pe, u):
            j, tt = u // 2, u % 2
            for p in range(3):
                b, r, _ = head2(p, j)
                o = bank[2 * (u % 2) + p // 2][:, (p % 2) * T:(p % 2 + 1) * T]
                last = nc.tensor.matmul(o, qk[r, b, tt * P:(tt + 1) * P], qk[r, 6 + b, :], start=True, stop=True)
            last.then_inc(s2_sc, 1)

        def pe_layer_norm(pe, q):
            for kc in range(KC):
                pe.wait_ge(x2_ready, 8 * q + kc + 1)
                last = nc.tensor.matmul(bank[6][:, 0:T], ones, x[:, kc, :], start=kc == 0, stop=kc == KC - 1)
            last.then_inc(ln_sum, 1)
            for kc in range(KC):
                pe.wait_ge(ln_sq, 8 * q + kc + 1)
                last = nc.tensor.matmul(bank[7][:, 0:T], ones, tb2[:, kc, :], start=kc == 0, stop=kc == KC - 1)
            last.then_inc(ln_ss, 1)

        def act_second(act):
            link = Chain(act, act_links, 0)
            link.base = layers * ACT_LINKS
            for kc in range(KC):
                act.wait_ge(x_ready, XR - 8 + kc + 1)
                nc.scalar.activation(act_hi[:, kc, :], x[:, kc, :], ACT.Copy).then_inc(act_his, 1)
            split_hi(act, M2, 3)
            for k in range(9):
                used2(act, k)
                if k < 6:
                    if k == 0:
                        act.wait_ge(x_ready, XR)
                    nc.scalar.activation(qk[:, 2 * k:2 * k + 2, :], blocks2(G2(k)[:, :]), ACT.Copy, scale=0.125 if k < 3 else 1.0)\
                        .then_inc(gfree[k % 2], 1)
                split_hi(act, M2, k + 4)
            act.wait_ge(dt_mm, 1)
            nc.scalar.activation(dw[0], bank[6][0:64, 0:T], ACT.Identity, bias=lc2[0:64, L2_DTB:L2_DTB + 1]).then_inc(dt_y, 1)
            nc.scalar.activation(ea, lc2[0:64, L2_ALOG:L2_ALOG + 1], ACT.Exp).then_inc(alog_e, 1)
            act.wait_ge(dt_n, 1)
            nc.scalar.activation(dw[1], dw[1], ACT.Exp).then_inc(dt_e, 1)

            def exp2(u):
                act.wait_ge(s2_nm, u + 1)
                nc.scalar.activation(pp[u % 2], pp[u % 2], ACT.Exp, bias=nm2[:, u % 2:u % 2 + 1], accum_out=dens2[:, u % 2:u % 2 + 1])\
                    .then_inc(s2_exp, 1)

            exp2(0)
            act.wait_ge(pads_ready, 1)
            for i in range(12):
                if i in ATT_SLOT and ATT_SLOT[i] + 1 < 8:
                    exp2(ATT_SLOT[i] + 1)
                used2(act, 9 + i)
                if i >= 2:
                    act.wait_ge(conv_done, i - 1)
                nc.scalar.activation(up[i % 2][:, :, 2:2 + T], blocks2(G2(9 + i)[:, :]), ACT.Copy).then_inc(gfree[(9 + i) % 2], 1)
                split_hi(act, M2, 13 + i)
                if i in ATT_SLOT:
                    u = ATT_SLOT[i]
                    act.wait_ge(s2_tr, u + 1)
                    if u % 2 == 0 and u:
                        act.wait_ge(s2_pv, u // 2)
                    nc.scalar.activation(pt2[:, 0:4, (u % 2) * P:(u % 2 + 1) * P], bank[6][:, :].rearrange("p (n t) -> p n t", n=4), ACT.Copy)\
                        .then_inc(s2_ev0, 1)
                if i in PV_SLOT and PV_SLOT[i] % 2:
                    b = PV_SLOT[i] // 2
                    act.wait_ge(s2_pv, 2 * b + 2)
                    nc.scalar.activation(ff_hi[:, 0, b * T:(b + 1) * T], bank[7][:, T:2 * T], ACT.Copy).then_inc(s2_hi, 1)
            act.wait_ge(conv_done, 12)
            for n in (2, 0, 1):
                nc.scalar.activation(xb[:, 8 * n:8 * n + 8, :], xb[:, 8 * n:8 * n + 8, :], ACT.Silu).then_inc(silu_done, 1)

            def copies(g):
                act.wait_ge(cb_mm, g + 1)
                nc.scalar.activation(cb[:, g % 2, :, :], blocks2(bank[7][:, :]), ACT.Copy).then_inc(cb_done, 1)
                act.wait_ge(xt_mm0, g + 1)
                nc.scalar.activation(xt[:, g % 2, 0, :], bank[6][:, :], ACT.Copy).then_inc(xt_done0, 1)
                act.wait_ge(xt_mm1, g + 1)
                nc.scalar.activation(xt[:, g % 2, 1, :], bank[7][:, :], ACT.Copy).then_inc(xt_done1, 1)

            act.wait_ge(s2_pv, 4)
            copies(0)

            def decay(e):
                act.wait_ge(e_mask, e + 1)
                nc.scalar.activation(eb[e % 2], eb[e % 2], ACT.Exp).then_inc(e_exp, 1)

            decay(0)
            for hu in range(8):
                used2(act, 21 + hu)
                nc.scalar.activation(zb[:, 2 * hu:2 * hu + 2, :], blocks2(G2(21 + hu)[:, :]), ACT.Copy).then_inc(gfree[(21 + hu) % 2], 1)
                split_hi(act, M2, 25 + hu)
                if hu % 2 and hu < 7:
                    if hu > 2:
                        act.wait_ge(e_used, 4 * (hu // 2))
                    copies(hu // 2 + 1)
                for e in (2 * hu + 1, 2 * hu + 2):
                    if e < 16:
                        decay(e)
            act.wait_ge(gfree[0], 7 * layers + 28 // 2 + 1 + 1)
            act.wait_ge(gfree[1], 7 * layers + 28 // 2 + 1)
            for n in range(2):
                nc.scalar.activation(zb[:, 8 * n:8 * n + 8, :], zb[:, 8 * n:8 * n + 8, :], ACT.Silu).then_inc(z_silu, 1)
            act.wait_ge(e_used, 16)
            for i in range(8):
                used2(act, 29 + i)
                for c in range(2):
                    b = 2 * i + c
                    last = nc.scalar.activation(gb[:, b, :], G2(29 + i)[:, c * T:(c + 1) * T], ACT.Identity, bias=lc2[:, L2_BG + b:L2_BG + b + 1])
                last.then_inc(gfree[(29 + i) % 2], 1)
                split_hi(act, M2, 33 + i)
                n = i // 2
                g = (2, 3, 0, 1)[n]
                if i % 2 == 0:
                    act.wait_ge(y_gated, n + 1)
                    if n:
                        act.wait_ge(y_ss, n)
                    nc.scalar.activation(sq2, xb[:, 4 * g:4 * g + 4, :], ACT.Square).then_inc(y_sq, 1)
                else:
                    act.wait_ge(y_ss, n + 1)
                    if n:
                        act.wait_ge(y_fin, n)
                    rsqrt(link, rs2, bank[6][:, 0:T], 1.0 / 512, cst[:, C_LEPS:C_LEPS + 1]).then_inc(y_rs, 1)
                    if n < 2:
                        act.wait_ge(y_fin, n + 1)
                        nc.scalar.activation(mix_hi[:, 4 * n:4 * n + 4, :], xb[:, 4 * g:4 * g + 4, :], ACT.Copy).then_inc(y_hi, 1)
            for n in (2, 3):
                act.wait_ge(y_fin, n + 1)
                nc.scalar.activation(act_hi[:, 4 * n - 8:4 * n - 4, :], xb[:, 4 * n - 8:4 * n - 4, :], ACT.Copy).then_inc(y_hi, 1)
            act.wait_ge(gfree[0], 7 * layers + 19 + 1)
            act.wait_ge(gfree[1], 7 * layers + 18 + 1)
            for n in (1, 0):
                nc.scalar.activation(gb[:, 8 * n:8 * n + 8, :], gb[:, 8 * n:8 * n + 8, :], ACT.Sigmoid).then_inc(gates_done, 1)
            for k in range(41, 50):
                split_hi(act, M2, k)
            for n in range(4):
                act.wait_ge(mx_sum, n + 1)
                nc.scalar.activation(mix_hi[:, 2 * n:2 * n + 2, :], mx[:, 2 * n:2 * n + 2, :], ACT.Copy).then_inc(mx_hi, 1)
            act_layer_norm(act, 0, link, L2_LN1B, (50, 51, 52))
            act_ff(act, layers, M2, 50, 16 * layers, final=True)
            act_layer_norm(act, 1, link, L2_LN2B, ())
            for c in range(4):
                if c % 2 == 0:
                    act.wait_ge(o_turned, c + 1)
                    nc.scalar.activation(obuf[:, :, c * T:(c + 1) * T], blocks2(bank[c][:, :]), ACT.Copy).then_inc(o_copied, 1)

        def act_layer_norm(act, q, link, bias, ks):
            act.wait_ge(ln_sum, q + 1)
            nc.scalar.activation(rs[:, :], bank[6][:, 0:T], ACT.Copy, scale=-1.0 / D).then_inc(ln_mean, 1)
            for kc in range(KC):
                act.wait_ge(ln_c, 8 * q + kc + 1)
                nc.scalar.activation(tb2[:, kc, :], x[:, kc, :], ACT.Square).then_inc(ln_sq, 1)
            for k in ks:
                split_hi(act, M2, k)
            act.wait_ge(ln_ss, q + 1)
            rsqrt(link, rs[:, :], bank[7][:, 0:T], 1.0 / D, cst[:, C_LEPS:C_LEPS + 1]).then_inc(ln_rs, 1)
            for kc in range(KC):
                act.wait_ge(ln_t, 8 * q + kc + 1)
                b = lc2[:, bias + kc:bias + kc + 1]
                if q == 0:
                    nc.scalar.activation(act_hi[:, kc, :], tb2[:, kc, :], ACT.Identity, bias=b).then_inc(ln_hi, 1)
                nc.scalar.activation(x[:, kc, :], tb2[:, kc, :], ACT.Identity, bias=b).then_inc(ln_x, 1)

        def dve_second(dve):
            link = Chain(dve, dve_links, 0)
            link.base = layers * DVE_LINKS
            for kc in range(KC):
                dve.wait_ge(act_his, 16 * layers + kc + 1)
                nc.vector.tensor_tensor(act_lo[:, kc, :], x[:, kc, :], act_hi[:, kc, :].bitcast(F32), ALU.subtract).then_inc(act_ready, 1)
            split_lo(dve, M2, 3)
            for k in range(9):
                if k >= 6:
                    used2(dve, k)
                    nc.vector.tensor_copy(v2[:, :, (k - 6) * T:(k - 5) * T], blocks2(G2(k)[:, :])).then_inc(gfree[k % 2], 1)
                split_lo(dve, M2, k + 4)
            dve.wait_ge(dt_y, 1)
            link(nc.vector.scalar_tensor_tensor(dw[1], dw[0], -1.0, dw[0], ALU.mult, ALU.min))
            dve.sem_inc(dt_n, 1)
            dve.wait_ge(dt_e, 1)
            link(nc.vector.tensor_scalar(dw[2], dw[1], 2.0, None, ALU.add))
            link(nc.vector.reciprocal(dw[2], dw[2]))
            link(nc.vector.tensor_tensor(dw[3], dw[1], dw[2], ALU.mult))
            link(nc.vector.tensor_tensor(dw[4], dw[3], dw[3], ALU.mult))
            link(nc.vector.tensor_scalar(dw[2], dw[4], 1.0 / 15, None, ALU.mult))
            for c in (13, 11, 9, 7, 5, 3):
                link(nc.vector.scalar_tensor_tensor(dw[2], dw[2], 1.0 / c, dw[4], ALU.add, ALU.mult))
            link(nc.vector.scalar_tensor_tensor(dw[2], dw[2], 1.0, dw[3], ALU.add, ALU.mult))
            link(nc.vector.tensor_scalar(dw[0], dw[0], 0.0, None, ALU.max))
            link(nc.vector.scalar_tensor_tensor(dw[2], dw[2], 2.0, dw[0], ALU.mult, ALU.add))
            dve.wait_ge(alog_e, 1)
            link(nc.vector.tensor_scalar(dw[3], dw[2], ea, -1.0, ALU.mult, ALU.mult))
            link(nc.vector.tensor_tensor_scan(dw[4], cst[0:64, C_ONE:C_ONE + 1].to_broadcast([64, T]), dw[3], 0.0, ALU.mult, ALU.add))
            link(nc.vector.scalar_tensor_tensor(dw[4], dw[3], cst[0:64, C_NM:C_NM + 1], dw[4], ALU.mult, ALU.add))
            nc.vector.tensor_scalar(dw[5], dw[4], cst[0:64, C_SG:C_SG + 1], None, ALU.mult).then_inc(dt_done, 1)
            dve.wait_ge(dist_ready, 16)

            def biased(u):
                j, tt = u // 2, u % 2
                dve.wait_ge(s2_sc, u + 1)
                if u >= 2:
                    dve.wait_ge(s2_tr, u - 1)
                for p in range(3):
                    _, _, h = head2(p, j)
                    ins = nc.vector.scalar_tensor_tensor(pp[u % 2][:, p * T:(p + 1) * T], dist[:, tt, p, :], -slope(h),
                                                         bank[2 * (u % 2) + p // 2][:, (p % 2) * T:(p % 2 + 1) * T], ALU.mult, ALU.add)
                link(ins)
                nc.vector.tensor_reduce(nm2[:, u % 2:u % 2 + 1], pp[u % 2], AX.X, ALU.max, negate=True).then_inc(s2_nm, 1)

            biased(0)
            for i in range(12):
                if i in ATT_SLOT:
                    u = ATT_SLOT[i]
                    if u + 1 < 8:
                        biased(u + 1)
                    dve.wait_ge(s2_exp, u + 1)
                    link(nc.vector.reciprocal(dens2[:, u % 2:u % 2 + 1], dens2[:, u % 2:u % 2 + 1]))
                    nc.vector.tensor_scalar(pp[u % 2], pp[u % 2], dens2[:, u % 2:u % 2 + 1], None, ALU.mult).then_inc(s2_p, 1)
                if i == 0:
                    dve.wait_ge(dt_tr, 1)
                    nc.vector.tensor_copy(dtt.rearrange("p a t h -> p (a t h)"), bank[7][:, 0:T]).then_inc(dt_cols, 1)
                dve.wait_ge(gfree[(9 + i) % 2], 7 * layers + (9 + i) // 2 + 2)
                for tap in range(5):
                    for c in range(2):
                        b = 2 * i + c
                        src, w = up[i % 2][:, c, tap:tap + T], lc2[:, L2_CW + 24 * tap + b:L2_CW + 24 * tap + b + 1]
                        if tap == 0:
                            ins = nc.vector.tensor_scalar(xb[:, b, :], src, w, lc2[:, L2_CB + b:L2_CB + b + 1], ALU.mult, ALU.add)
                        else:
                            dve.wait_ge(dve_links, link.base + link.n - 1)
                            ins = nc.vector.scalar_tensor_tensor(xb[:, b, :], src, w, xb[:, b, :], ALU.mult, ALU.add)
                        if tap < 4:
                            ins.then_inc(dve_links, 1)
                            link.n += 1
                        elif c == 1:
                            ins.then_inc(conv_done, 1)
                        else:
                            ins.then_inc(dve_links, 1)
                            link.n += 1
                split_lo(dve, M2, 13 + i)
                if i in ATT_SLOT:
                    u = ATT_SLOT[i]
                    dve.wait_ge(s2_tr, u + 1)
                    if u % 2 == 0 and u:
                        dve.wait_ge(s2_pv, u // 2)
                    nc.vector.tensor_copy(pt2[:, 4:6, (u % 2) * P:(u % 2 + 1) * P], bank[7][:, 0:T].rearrange("p (n t) -> p n t", n=2))\
                        .then_inc(s2_ev1, 1)
                if i in PV_SLOT and PV_SLOT[i] % 2:
                    b = PV_SLOT[i] // 2
                    dve.wait_ge(s2_hi, b + 1)
                    nc.vector.tensor_tensor(ff_lo[:, 0, b * T:(b + 1) * T], bank[7][:, T:2 * T], ff_hi[:, 0, b * T:(b + 1) * T].bitcast(F32),
                                            ALU.subtract).then_inc(s2_lo, 1)

            def mask(e):
                st = e % 2
                o = eb[e % 2]
                dve.wait_ge(e_sub, e + 1)
                mf, mb = [cst[:, c:c + P].unsqueeze(1).to_broadcast([P, 4, P]) for c in (C_MF, C_MB)]
                far, near = (mf, mb) if st == 0 else (mb, mf)
                nc.vector.tensor_tensor(o[:, :, st * P:(st + 1) * P], o[:, :, st * P:(st + 1) * P], far, ALU.min)
                nc.vector.tensor_tensor(o[:, :, T:T + P], o[:, :, T:T + P], near, ALU.min).then_inc(e_mask, 1)

            def weigh2(e):
                hu, st = e // 2, e % 2
                g = hu // 2
                if e % 4 == 0:
                    dve.wait_ge(cb_done, g + 1)
                dve.wait_ge(e_exp, e + 1)
                o = eb[e % 2]
                for h in range(4):
                    far, near = [dtt[:, 1, st, 32 * d + 4 * hu + h:32 * d + 4 * hu + h + 1] for d in (st, 1 - st)]
                    nc.vector.scalar_tensor_tensor(o[:, h, 0:T], o[:, h, 0:T], far, cb[:, g % 2, st, :], ALU.mult, ALU.mult)
                    last = nc.vector.scalar_tensor_tensor(o[:, h, T:T + P], o[:, h, T:T + P], near, cb[:, g % 2, st, st * P:(st + 1) * P],
                                                          ALU.mult, ALU.mult)
                last.then_inc(e_mul, 1)

            def take_y(hu):
                dve.wait_ge(e_used, 2 * hu + 2)
                for c in range(2):
                    b = 2 * hu + c
                    last = nc.vector.scalar_tensor_tensor(xb[:, b, :], xb[:, b, :], lc2[:, L2_DS + b:L2_DS + b + 1],
                                                          bank[hu % 4][:, c * T:(c + 1) * T], ALU.mult, ALU.add)
                last.then_inc(y_out, 1)

            mask(0)
            for hu in range(8):
                mask(2 * hu + 1)
                weigh2(2 * hu)
                split_lo(dve, M2, 25 + hu)
                if hu:
                    dve.wait_ge(xt_mm1, (hu - 1) // 2 + 1)
                    take_y(hu - 1)
                if hu < 7:
                    mask(2 * hu + 2)
                weigh2(2 * hu + 1)
            take_y(7)
            for n in range(4):
                g = (2, 3, 0, 1)[n]
                dve.wait_ge(z_silu, 2)
                dve.wait_ge(y_out, 8)
                nc.vector.tensor_tensor(xb[:, 4 * g:4 * g + 4, :], xb[:, 4 * g:4 * g + 4, :], zb[:, 4 * g:4 * g + 4, :], ALU.mult).then_inc(y_gated, 1)
                split_lo(dve, M2, 33 + 2 * n)
                dve.wait_ge(y_rs, n + 1)
                for b in range(4 * g, 4 * g + 4):
                    last = nc.vector.scalar_tensor_tensor(xb[:, b, :], xb[:, b, :], lc2[:, L2_SN + b:L2_SN + b + 1], rs2, ALU.mult, ALU.mult)
                last.then_inc(y_fin, 1)
                split_lo(dve, M2, 34 + 2 * n)
                if n < 2:
                    dve.wait_ge(y_hi, n + 1)
                    nc.vector.tensor_tensor(mix_lo[:, 4 * n:4 * n + 4, :], xb[:, 4 * g:4 * g + 4, :], mix_hi[:, 4 * n:4 * n + 4, :].bitcast(F32),
                                            ALU.subtract).then_inc(y_lo, 1)
            for n in (0, 1):
                dve.wait_ge(y_hi, n + 3)
                nc.vector.tensor_tensor(act_lo[:, 4 * n:4 * n + 4, :], xb[:, 4 * n:4 * n + 4, :], act_hi[:, 4 * n:4 * n + 4, :].bitcast(F32),
                                        ALU.subtract).then_inc(y_lo, 1)
            used2(dve, 37)
            dve.wait_ge(gates_done, 1)
            for n in range(4):
                nc.vector.tensor_tensor(m2[:, 2 * n:2 * n + 2, :], blocks2(bank[4 + n][:, :]), gb[:, 8 + 2 * n:10 + 2 * n, :], ALU.mult).then_inc(att_proj, 1)
            for k in range(41, 50):
                split_lo(dve, M2, k)
            used2(dve, 45)
            dve.wait_ge(gates_done, 2)
            for n in range(4):
                v = slice(2 * n, 2 * n + 2)
                link(nc.vector.tensor_tensor(mx[:, v, :], blocks2(bank[n][:, :]), gb[:, v, :], ALU.mult))
                nc.vector.tensor_tensor(mx[:, v, :], mx[:, v, :], m2[:, v, :], ALU.add).then_inc(mx_sum, 1)
                if n:
                    mixed2(dve, n - 1)
            mixed2(dve, 3)
            for n in range(4):
                used2(dve, 46 + n)
                for c in range(2):
                    kc = 2 * n + c
                    nc.vector.scalar_tensor_tensor(x[:, kc, :], x[:, kc, :], ALPHA, bank[4 + n % 2][:, c * T:(c + 1) * T], ALU.mult, ALU.add)\
                        .then_inc(x2_ready, 1)
            dve_layer_norm(dve, 0, L2_LN1G, L2_LN1B, (50, 51, 52))
            dve_ff(dve, M2, 50, 16 * layers, final=True)
            used2(dve, 81)
            for kc in range(KC):
                nc.vector.scalar_tensor_tensor(x[:, kc, :], x[:, kc, :], ALPHA, bank[kc // 2][:, (kc % 2) * T:(kc % 2 + 1) * T], ALU.mult, ALU.add)\
                    .then_inc(x2_ready, 1)
            dve_layer_norm(dve, 1, L2_LN2G, L2_LN2B, ())
            for c in range(4):
                if c % 2:
                    dve.wait_ge(o_turned, c + 1)
                    nc.vector.tensor_copy(obuf[:, :, c * T:(c + 1) * T], blocks2(bank[c][:, :])).then_inc(o_copied, 1)

        def mixed2(dve, n):
            v = slice(2 * n, 2 * n + 2)
            dve.wait_ge(mx_hi, n + 1)
            nc.vector.tensor_tensor(mix_lo[:, v, :], mx[:, v, :], mix_hi[:, v, :].bitcast(F32), ALU.subtract).then_inc(mx_lo, 1)

        def dve_layer_norm(dve, q, gain, bias, ks):
            dve.wait_ge(ln_mean, q + 1)
            for kc in range(KC):
                nc.vector.tensor_tensor(x[:, kc, :], x[:, kc, :], rs[:, :], ALU.add).then_inc(ln_c, 1)
            for k in ks:
                split_lo(dve, M2, k)
            dve.wait_ge(ln_rs, q + 1)
            for kc in range(KC + 1):
                if kc < KC:
                    nc.vector.scalar_tensor_tensor(tb2[:, kc, :], x[:, kc, :], lc2[:, gain + kc:gain + kc + 1], rs[:, :], ALU.mult, ALU.mult)\
                        .then_inc(ln_t, 1)
                if kc and q == 0:
                    c = kc - 1
                    dve.wait_ge(ln_hi, c + 1)
                    nc.vector.scalar_tensor_tensor(act_lo[:, c, :], tb2[:, c, :], lc2[:, bias + c:bias + c + 1], act_hi[:, c, :].bitcast(F32),
                                                   ALU.add, ALU.subtract).then_inc(ln_lo, 1)

        block = ctx.enter_context(nc.Block())

        @block.sync
        def _(sp):
            sp.dma_start(x_in, a["x"].rearrange("b (t p) d -> p (b t) d", p=P)).then_inc(x_loaded, 16)
            sp.dma_start(cst[:, :], a["cst"]).then_inc(cst_loaded, 16)
            for n in range(RAW):
                sp.dma_start(raw[:, n, :], a["panels"][n]).then_inc(raw_ready[n], 16)
            for n in range(RAW, L_AHEAD):
                load(sp, 0, n)
            with sp.Fori(0, layers) as l:
                m = 11 * l
                for ring, n0, n1 in (("mod", 0, 10), ("panel", 5, 6), ("mod", 10, 14), ("panel", 6, 10), ("mod", 14, 16),
                                     ("panel", 10, 11), ("mod", 16, 20), ("panel", 11, 12), ("mod", 20, 22), ("panel", 12, 17),
                                     ("mod", 22, 24)):
                    for n in range(n0, n1):
                        if ring == "mod":
                            load_mod(sp, l, n)
                        else:
                            load(sp, m, n)
                for k in (17, 18, 19, 20):
                    load(sp, m, k)
                with sp.Fori(1, 8) as i:
                    for k in (17, 18, 19, 20):
                        load(sp, m + i, k)
            finish(sp)

        @block.gpsimd
        def _(pool):
            link = Chain(pool, pool_links, 7)
            pool.dma_start(ccol[:, :], a["ccol"]).then_inc(c_loaded, 16)
            nc.gpsimd.memset(ub, 0.0)
            nc.gpsimd.memset(wb[0], 0.0)
            link(nc.gpsimd.memset(wb[1], 0.0))
            link.first = link.n
            with pool.Fori(0, layers) as l:
                link.layer(l)
                pool.wait_ge(x_ready, 16 * l + 8)
                pool.dma_start(lc[:, :], a["lcs"][l]).then_inc(lc_ready, 16)
                pool_rope(pool, l)
                pool_window(pool, l, link)
                link.end()
            pool_second(pool)

        @block.tensor
        def _(pe):
            pe.sem_inc(split_free, SPLIT)
            pe.sem_inc(mod_used, 2)
            pe.sem_inc(macc_free, 2)
            pe.sem_inc(gfree[0], 1)
            pe.sem_inc(gfree[1], 1)
            pe.sem_inc(ff_relu, 2)
            pe.sem_inc(ff_ready, 2)
            pe.wait_ge(x_loaded, 16)
            pe.wait_ge(cst_loaded, 16)
            for kc in range(KC):
                for tt in range(TT):
                    o = bank[kc // 2][:, (kc % 2) * T + tt * P:(kc % 2) * T + (tt + 1) * P]
                    last = nc.tensor.transpose(o, x_in[:, tt, kc * P:(kc + 1) * P], ident)
                last.then_inc(x_turned, 1)
            pe.wait_ge(cact_ready, 1)
            with pe.Fori(0, layers) as l:
                pe_layer(pe, l)
            pe_second(pe)

        @block.scalar
        def _(act):
            link = Chain(act, act_links, ACT_LINKS)
            act.wait_ge(cst_loaded, 16)
            nc.scalar.activation(idb[:, :], ident, ACT.Copy).then_inc(masks_ready, 1)
            nc.scalar.activation(causb[:, :], cst[:, C_CAUS:C_CAUS + P], ACT.Copy).then_inc(masks_ready, 1)
            nc.scalar.activation(cmpmb[:, :], cst[:, C_CMPM:C_CMPM + 32], ACT.Copy).then_inc(masks_ready, 1)
            act.wait_ge(c_loaded, 16)
            nc.scalar.activation(cact[:, :], ccol[:, :], ACT.Silu).then_inc(cact_ready, 1)
            for k in range(3):
                split_hi(act, 0, k)
            link.first = link.n
            with act.Fori(0, layers) as l:
                link.layer(l)
                act_layer(act, l, link)
                link.end()
            act_second(act)

        @block.vector
        def _(dve):
            link = Chain(dve, dve_links, DVE_LINKS)
            for kc in range(KC):
                dve.wait_ge(x_turned, kc // 2 * 2 + 2)
                nc.vector.tensor_copy(x[:, kc, :], bank[kc // 2][:, (kc % 2) * T:(kc % 2 + 1) * T]).then_inc(x_ready, 1)
            for k in range(3):
                split_lo(dve, 0, k)
            link.first = link.n
            with dve.Fori(0, layers) as l:
                link.layer(l)
                dve_layer(dve, l, link)
                link.end()
            dve_second(dve)


def col_panel(w, cols):
    return w[:, cols].reshape(KC, P, 256).transpose(1, 0, 2).reshape(P, PANEL)


def row_panel(w, j):
    return w[256 * j:256 * j + 256].reshape(2, P, D).transpose(1, 0, 2).reshape(P, PANEL)


def as_cols(v):
    return v.reshape(-1, P).T


def ff_panels(up, down):
    ups = [col_panel(up, slice(256 * j, 256 * j + 256)) for j in range(FF_STEPS)]
    downs = [row_panel(down, j) for j in range(FF_STEPS)]
    got = [ups[0]]
    for j in range(FF_STEPS - 1):
        got += [ups[j + 1], downs[j]]
    return got + [downs[-1]]


def lay_out(i):
    panels, lcs = [], []
    for l in range(DEPTH):
        w = i["w_in"][l]
        heads = [np.r_[512 + 64 * b:576 + 64 * b, 768 + 64 * b:832 + 64 * b] for b in range(4)]
        for cols in (slice(1024, 1280), slice(1280, 1536), slice(1536, 1792),
                     np.concatenate(heads[:2]), np.concatenate(heads[2:])):
            panels.append(col_panel(w, cols))
        panels.append(i["cmp_w1"][l].reshape(2, 16, 2, 64, 64).transpose(2, 3, 1, 0, 4).reshape(P, PANEL))
        panels += [col_panel(w, slice(0, 256)), col_panel(w, slice(256, 512))]
        rows = np.concatenate([np.arange(512), np.concatenate(heads)])
        panels += [col_panel(i["w_out"][l][rows], slice(256 * j, 256 * j + 256)) for j in range(4)]
        panels += ff_panels(i["w_ff1"][l], i["w_ff2"][l])
        twice = lambda v: np.concatenate([v, v])[:, None]
        lcs.append(np.concatenate([
            as_cols(i["b_mod"][l]), as_cols(i["norm1"][l]), as_cols(i["norm2"][l]), as_cols(i["pool_scale"][l]),
            twice(i["q_norm"][l]), *[twice(i["k_norm"][l, n]) for n in range(3)],
            i["cmp_pe"][l].reshape(2, 16, 2, 64).transpose(2, 3, 1, 0).reshape(P, 32),
            i["cmp_w2"][l].reshape(P, 64), i["pool_w"][l].transpose(1, 0, 2).reshape(P, 512),
            w[:, 1792:1816].reshape(KC, P, 24).transpose(1, 0, 2).reshape(P, 192)], axis=1))
    modw = np.stack([[col_panel(i["w_mod"][l], slice(256 * j, 256 * j + 256)) for j in range(MOD_PANELS)] for l in range(DEPTH)])
    w = i["w_in_2"]
    z, xbc, dt_f, _, q, k, v, gates = [int(n) for n in N_SPLITS[:-1]]
    cols = [n + 256 * j for n, count in ((q, 3), (k, 3), (v, 3), (xbc, 12), (z, 8), (gates, 8)) for j in range(count)]
    panels += [col_panel(w, slice(c, c + 256)) for c in cols]
    panels.append(row_panel(i["w_proj_attn_2"], 0))
    panels += [row_panel(i["w_proj_ssd_2"], j) for j in (4, 5, 6, 7, 0, 1, 2, 3)]
    panels += [col_panel(i["w_out_2"], slice(256 * j, 256 * j + 256)) for j in range(4)]
    panels += ff_panels(i["w_up_2"], i["w_down_2"])
    in_rows = lambda *v: np.concatenate([*v, np.zeros(P - 2 * N_HEADS, np.float32)])[:, None]
    lc2 = np.concatenate([
        w[:, dt_f:dt_f + 64].reshape(KC, P, 64).transpose(1, 0, 2).reshape(P, 512),
        in_rows(i["dt_bias_f_2"], i["dt_bias_b_2"]), in_rows(i["a_log_f_2"], i["a_log_b_2"]),
        *[as_cols(i["conv_w_2"][tap]) for tap in range(D_CONV)], as_cols(i["conv_b_2"]),
        as_cols(np.repeat(i["d_skip_2"], 64)), as_cols(i["ssd_norm_w_2"]), as_cols(i["b_gate_2"]),
        as_cols(i["ln1_g_2"]), as_cols(i["ln1_b_2"]), as_cols(i["ln2_g_2"]), as_cols(i["ln2_b_2"])], axis=1)
    return dict(x=i["x"], ccol=as_cols(i["c"][0]), cst=constants(), lcs=np.stack(lcs), modw=modw, panels=np.stack(panels),
                lc2=lc2, dist=distances())


SETTINGS = dict(target_bir_lowering=False, num_devices=1, dynamic_dma_scratch_size=4096)


def kernel(**inputs):
    import numpy as _np
    import concourse.bacc as _bacc
    from concourse import mybir as _mybir
    from concourse.bass_utils import run_bass_kernel_spmd as _run

    laid_out = lay_out({name: _np.asarray(v) for name, v in inputs.items()})
    nc = _bacc.Bacc("TRN2", **SETTINGS)
    arrays, views = {}, {}
    for name, v in laid_out.items():
        arrays[f"in_{name}"] = _np.ascontiguousarray(v)
        views[name] = nc.dram_tensor(f"in_{name}", v.shape, _mybir.dt.float32, kind="ExternalInput").ap()
    out = nc.dram_tensor("out", (1, T, D), _mybir.dt.float32, kind="ExternalOutput").ap()
    build(nc, views, out)
    return _run(nc, [arrays], core_ids=[0]).results[0]["out"]
```

```python
import math
from contextlib import ExitStack

import numpy as np
import concourse.bass as bass
from concourse import mybir

F32 = mybir.dt.float32
F32R = mybir.dt.float32r
BF16 = mybir.dt.bfloat16
ALU = mybir.AluOpType
ACT = mybir.ActivationFunctionType
AX = mybir.AxisListType

P = 128
T = 256
TT = T // P
D = 1024
KC = D // P
DEPTH = 2
EPS = 1e-6
LN_EPS = 1e-5
NEG = -1e30

PANEL = KC * 256
RAW = 2
SPLIT = 4
L_K0K1, L_K2V0, L_V1V2, L_Q0, L_CMP, L_Q1, L_U0, L_U1, L_OUT, L_FF = 0, 1, 2, 3, 4, 5, 6, 7, 8, 12
L_PANELS = 44
FF_STEPS = 16
MOD_PANELS = 24

LC_BM, LC_BA, LC_NA, LC_N2, LC_PS, LC_QN, LC_KN, LC_PE, LC_W2, LC_PW, LC_GW, LC = 0, 32, 48, 56, 64, 68, 69, 72, 104, 168, 680, 872

C_ID, C_BD, C_ROT, C_ONE, C_COS, C_SIN, C_CCOS, C_CSIN, C_CAUS, C_CMPM, C_VALID, C_EPS, C_LEPS, C_MF, C_MB, C_SG, C_NM, C_RC, CN = (
    0, 128, 256, 384, 512, 768, 1024, 1040, 1056, 1184, 1216, 1217, 1218, 1219, 1347, 1475, 1476, 1477, 2501)
N_CMP = (T - 32) // 16 + 1


D_INNER, N_HEADS, CONV_DIM, D_CONV = 2048, 32, 3072, 5
N_SPLITS = np.cumsum([0, D_INNER, CONV_DIM, N_HEADS, N_HEADS, 768, 768, 768, 2 * D])
L2_WDT, L2_DTB, L2_ALOG, L2_CW, L2_CB, L2_DS, L2_SN, L2_BG, L2_LN1G, L2_LN1B, L2_LN2G, L2_LN2B, LC2 = (
    0, 512, 513, 514, 634, 658, 674, 690, 706, 714, 722, 730, 738)
FAR = 1e30


def distances():
    t = np.arange(T).reshape(TT, P).T[:, :, None, None]
    s = np.arange(T)[None, None, None, :]
    dil = np.array((1, 4, 16))[None, None, :, None]
    dd = np.abs(t - s)
    return np.where((dd % dil == 0) & (dd <= 64 * dil), dd, FAR).astype(np.float32).reshape(P, TT * 3 * T)


def constants():
    c = np.zeros((P, CN), np.float32)
    p = np.arange(P)[:, None]
    f = np.arange(P)[None, :]
    c[:, C_ID:C_ID + P] = p == f
    c[:, C_BD:C_BD + P] = p // 64 == f // 64
    c[:, C_ROT:C_ROT + P] = np.where((f % 64 < 32) & (p == f + 32), -1.0, np.where((f % 64 >= 32) & (p == f - 32), 1.0, 0.0))
    c[:, C_ONE:C_ONE + P] = 1.0
    inv = np.float32(10000.0) ** (-(np.arange(32, dtype=np.float32)) * np.float32(2.0) / np.float32(64))
    inv = np.tile(inv.astype(np.float32), 4)[:, None]
    ang = (np.arange(T, dtype=np.float32)[None, :] * inv).astype(np.float32)
    c[:, C_COS:C_COS + T], c[:, C_SIN:C_SIN + T] = np.cos(ang), np.sin(ang)
    end = np.arange(N_CMP) * 16 + 31
    ang = (end.astype(np.float32)[None, :] * inv).astype(np.float32)
    c[:, C_CCOS:C_CCOS + N_CMP], c[:, C_CSIN:C_CSIN + N_CMP] = np.cos(ang), np.sin(ang)
    c[:, C_CAUS:C_CAUS + P] = np.where(f > p, NEG, 0.0)
    for tt in range(TT):
        c[:, C_CMPM + 16 * tt:C_CMPM + 16 * tt + N_CMP] = np.where(end[None, :] > p + P * tt, NEG, 0.0)
    c[:, C_VALID] = np.arange(P) >= 31
    c[:, C_EPS] = EPS
    c[:, C_LEPS] = LN_EPS
    c[:, C_MF:C_MF + P] = np.where(p > f, NEG, 0.0)
    c[:, C_MB:C_MB + P] = np.where(f > p, NEG, 0.0)
    c[:, C_SG] = np.where(np.arange(P) % 64 < 32, 1.0, -1.0)
    c[:, C_NM] = np.where(np.arange(P) % 64 < 32, 0.0, -1.0)
    for g, w in enumerate((2, 4, 8, 16)):
        c[:, C_RC + g * T:C_RC + (g + 1) * T] = 1.0 / np.minimum(np.arange(T) + 1, w)
    return c


def build(nc, a, out, layers=DEPTH, dump=None):
    ctx = ExitStack()

    def sb(name, shape, dt=F32):
        return ctx.enter_context(nc.sbuf_tensor(name, shape, dt))

    def sem(name):
        return ctx.enter_context(nc.semaphore(name))

    with ctx:
        raw = sb("raw", [P, RAW, PANEL])
        w_hi = [sb(f"w_hi{i}", [P, PANEL], F32R) for i in range(SPLIT)]
        w_lo = [sb(f"w_lo{i}", [P, PANEL], F32R) for i in range(SPLIT)]
        x = sb("x", [P, KC, T])
        act_hi, act_lo = sb("act_hi", [P, KC, T], F32R), sb("act_lo", [P, KC, T], F32R)
        with nc.sbuf_tensor("mixf", [P, 2 * KC * T], F32) as mixf:
            pass
        mix_hi, mix_lo = sb("mix_hi", [P, KC, T], F32R), sb("mix_lo", [P, KC, T], F32R)
        ff_hi, ff_lo = sb("ff_hi", [P, 2, 2 * T], F32R), sb("ff_lo", [P, 2, 2 * T], F32R)
        cst = sb("cst", [P, CN])
        lc = sb("lc", [P, LC])
        idb = sb("idb", [P, P], BF16)
        causb = sb("causb", [P, P], BF16)
        cmpmb = sb("cmpmb", [P, 32], BF16)
        ccol = sb("ccol", [P, 2 * KC + 16])
        cact = sb("cact", [P, KC])
        modc = sb("modc", [P, 48])
        macc = sb("macc", [P, 2, 256])
        gcol = sb("gcol", [P, 2 * KC])
        rs = sb("rs", [P, T])
        small = sb("small", [P, 160])
        ARENA = 17920
        arena = sb("arena", [P, ARENA])
        at = [0]

        def area(n, *dims):
            v = arena[:, at[0]:at[0] + n]
            at[0] += n
            assert at[0] <= ARENA, at[0]
            if len(dims) == 2:
                v = v.rearrange("p (a b) -> p a b", a=dims[0])
            if len(dims) == 3:
                v = v.rearrange("p (a b c) -> p a b c", a=dims[0], b=dims[1])
            return v

        bank = [ctx.enter_context(nc.psum_tensor(f"bank{i}", [P, 512], F32)) for i in range(8)]

        def win(ap, start, n_part, dims, col=0):
            full = ap[start:start + n_part, col:col + 1]
            return bass.AP(full.tensor, full.offset, [[full.ap[0][0], n_part], *dims])

        x_loaded, cst_loaded, c_loaded = sem("x_loaded"), sem("cst_loaded"), sem("c_loaded")
        masks_ready = sem("masks_ready")
        cact_ready = sem("cact_ready")
        gcol_ready = sem("gcol_ready")
        x_turned = sem("x_turned")
        x_ready = sem("x_ready")
        lc_ready = sem("lc_ready")
        sq_done = sem("sq_done")
        ss_done = sem("ss_done")
        rs_done = sem("rs_done")
        t_done = sem("t_done")
        act_his = sem("act_his")
        act_ready = sem("act_ready")
        raw_ready = [sem(f"raw_ready{i}") for i in range(RAW)]
        hi_done = sem("hi_done")
        lo_done = sem("lo_done")
        split_free = sem("split_free")
        modraw = [sem(f"modraw{i}") for i in range(2)]
        mod_used = sem("mod_used")
        macc_free = sem("macc_free")
        mod_links = sem("mod_links")
        modc_ready = sem("modc_ready")
        gfull = sem("gfull")
        gfree = [sem(f"gfree{i}") for i in range(2)]
        nr_sq = sem("nr_sq")
        nr_mm = sem("nr_mm")
        nr_rs = sem("nr_rs")
        nr_yc = sem("nr_yc")
        nr_out = sem("nr_out")
        tb_k, tb_v, tb_pe, tb_hi, tb_lo = sem("tb_k"), sem("tb_v"), sem("tb_pe"), sem("tb_hi"), sem("tb_lo")
        cmp_h, cmp_e, cmp_s, cmp_w2, cmp_y = sem("cmp_h"), sem("cmp_e"), sem("cmp_s"), sem("cmp_w2"), sem("cmp_y")
        gw_hi, gw_lo = sem("gw_hi"), sem("gw_lo")
        u_copied = sem("u_copied")
        pooled_ready = sem("pooled_ready")
        at_sc = sem("at_sc")
        at_nm = sem("at_nm")
        at_exp = sem("at_exp")
        at_p = sem("at_p")
        at_tr = sem("at_tr")
        at_ev0, at_ev1 = sem("at_ev0"), sem("at_ev1")
        at_pv = sem("at_pv")
        mix_his = sem("mix_his")
        out_done = sem("out_done")
        ff_full = sem("ff_full")
        ff_relu = sem("ff_relu")
        ff_sq = sem("ff_sq")
        ff_his = sem("ff_his")
        ff_ready = sem("ff_ready")
        ff_out = sem("ff_out")
        dve_links, act_links, pool_links = sem("dve_links"), sem("act_links"), sem("pool_links")
        out_written = sem("out_written")

        class Chain:

            def __init__(self, eng, s, per_layer):
                self.eng, self.s, self.per, self.base, self.n, self.first = eng, s, per_layer, 0, 0, 0

            def __call__(self, ins):
                ins.then_inc(self.s, 1)
                self.n += 1
                self.eng.wait_ge(self.s, self.base + self.n)

            def layer(self, l):
                self.base, self.n0, self.n = l * self.per + self.first, 0, 0

            def end(self):
                assert self.n == self.per, (self.eng, self.n)

        at[0] = 0
        modw = area(2 * PANEL, 2, PANEL)
        mod_sums = arena[:, at[0]:at[0] + 12 * 256].rearrange("p (n c) -> p n c", n=12)
        tbuf = area(KC * T, KC, T)
        L_ARENA = at[0]
        ybuf = [area(2 * T, 2, T) for _ in range(3)]
        q_at = at[0]
        qr = area(4 * T, 4, T)
        kr = area(2 * T, 2, T)
        vt = area(TT * T, TT, T)
        tb = area(960, 16, 60)
        pbuf = [area(800) for _ in range(2)]
        pts = [area(1024) for _ in range(2)]
        fr = [v[:, 0:2 * T] for v in pts]
        ub = area(4 * (T + 16), 4, T + 16)
        wb = [area(4 * (T + 16), 4, T + 16) for _ in range(2)]
        tbh, tbl = [v[:, :, :].rearrange("p a b -> p (a b)")[:, 0:960].rearrange("p (j n) -> p j n", j=16) for v in (ff_hi, ff_lo)]
        gwh, gwl = sb("gwh", [P, KC, 24], F32R), sb("gwl", [P, KC, 24], F32R)
        kcmp = small[:, 0:15]
        vcmp = sb("vcmp", [16, P])
        hs = small[:, 16:76]
        ce = small[:, 76:136]
        ycmp = small[:, 136:151]
        gts = sb("gts", [P, TT, 24])
        sqc = sb("sqc", [P, 48])
        dens = sb("dens", [P, 2, 6])
        nm = sb("nm", [P, 2, 6])
        fac = sb("fac", [P, 2, 6])

        ident = cst[:, C_ID:C_ID + P]
        ones = cst[:, C_ONE:C_ONE + P]
        x_in = arena[:, q_at:q_at + TT * D].rearrange("p (t d) -> p t d", t=TT)


        def slot(k):
            return k % SPLIT

        n_panels = a["panels"].shape[0]

        def load(sp, m, k):
            sp.wait_ge(lo_done, 4 * m + k - RAW + 1)
            sp.dma_start(raw[:, k % RAW, :], a["panels"][4 * m + k]).then_inc(raw_ready[k % RAW], 16)

        def load_mod(sp, l, mp):
            sp.wait_ge(mod_used, MOD_PANELS * l + mp + 1)
            sp.dma_start(modw[:, mp % 2, :], a["modw"][MOD_PANELS * l + mp]).then_inc(modraw[mp % 2], 16)


        def sp_layer(sp, l, ahead):
            m = 11 * l
            for k in range(2, 8):
                load(sp, m, k)
            load_mod(sp, l, 8)
            load_mod(sp, l, 9)
            for k in range(8, 14):
                load(sp, m, k)
            for mp in range(10, 18):
                load_mod(sp, l, mp)
            load(sp, m, 14)
            for mp in (18, 19):
                load_mod(sp, l, mp)
            load(sp, m, 15)
            if not ahead:
                load_mod(sp, l, 20)
                load_mod(sp, l, 21)
            for k in (16, 17, 18):
                load(sp, m, k)
            with sp.Fori(1, FF_STEPS // 2 - 1) as i:
                load(sp, m + i, 15)
                if ahead:
                    for mp in range(2):
                        sp.wait_ge(mod_used, MOD_PANELS * l + 18 + 2 * i + mp + 1)
                        sp.dma_start(modw[:, mp, :], a["modw"][MOD_PANELS * l + 18 + 2 * i + mp]).then_inc(modraw[mp], 16)
                for k in (16, 17, 18):
                    load(sp, m + i, k)
            e = m + FF_STEPS // 2 - 1
            load(sp, e, 15)
            if not ahead:
                load_mod(sp, l, 22)
                load_mod(sp, l, 23)
            load(sp, e, 16)
            load(sp, e, 17)

        def split_hi(act, m, k):
            act.wait_ge(raw_ready[k % RAW], 16 * (2 * m + k // 2 + 1))
            act.wait_ge(split_free, 4 * m + k + 1)
            nc.scalar.activation(w_hi[slot(k)][:, :], raw[:, k % RAW, :], ACT.Copy).then_inc(hi_done, 1)

        def split_lo(dve, m, k):
            dve.wait_ge(hi_done, 4 * m + k + 1)
            nc.vector.tensor_tensor(w_lo[slot(k)][:, :], raw[:, k % RAW, :], w_hi[slot(k)][:, :].bitcast(F32),
                                    ALU.subtract).then_inc(lo_done, 1)

        def mm3(o, wh, wl, xh, xl, start, stop, skip=False):
            nc.tensor.matmul(o, wh, xh, start=start, stop=False, skip_group_check=skip)
            nc.tensor.matmul(o, wh, xl, start=False, stop=False, skip_group_check=skip)
            return nc.tensor.matmul(o, wl, xh, start=False, stop=stop, skip_group_check=skip)

        def pool_rope(pool, l):
            for j in range(3):
                pool.wait_ge(nr_mm, 4 * l + j + 1)
                y = ybuf[j]
                nc.gpsimd.tensor_tensor(y, y, cst[:, C_COS:C_COS + T].unsqueeze(1).to_broadcast([P, 2, T]), ALU.mult).then_inc(nr_yc, 1)

        def pool_window(pool, l, link):
            pool.wait_ge(u_copied, 2 * l + 2)
            b, c = wb

            def cols(t, g0, off=0, step=1):
                return t[:, g0:4:step, 16 - off:16 - off + T]

            link(nc.gpsimd.tensor_tensor(cols(b, 0), cols(ub, 0), cols(ub, 0, 1), ALU.add))
            link(nc.gpsimd.tensor_tensor(cols(c, 1), cols(b, 1), cols(b, 1, 2), ALU.add))
            link(nc.gpsimd.tensor_tensor(cols(b, 2), cols(c, 2), cols(c, 2, 4), ALU.add))
            link(nc.gpsimd.tensor_tensor(cols(c, 3), cols(b, 3), cols(b, 3, 8), ALU.add))
            rc = cst[:, C_RC:C_RC + 4 * T].rearrange("p (g t) -> p g t", g=4)
            for t, g0 in ((b, 0), (c, 1)):
                link(nc.gpsimd.tensor_tensor(cols(t, g0, 0, 2), cols(t, g0, 0, 2), rc[:, g0:4:2, :], ALU.mult))
                last = nc.gpsimd.tensor_tensor(cols(t, g0, 0, 2), cols(t, g0, 0, 2), cols(ub, g0, 0, 2), ALU.subtract)
                if g0 == 0:
                    link(last)
            last.then_inc(pooled_ready, 1)


        def pe_gfree(pe, l, g):
            pe.wait_ge(gfree[g % 2], 7 * l + g // 2 + 1)

        def pe_panel(pe, m, k, o, xh, xl, arrive=None, after=None):
            pe.wait_ge(lo_done, 4 * m + k + 1)
            wh, wl = w_hi[slot(k)], w_lo[slot(k)]
            for c in range(2):
                for kc in range(KC):
                    if c == 0 and arrive:
                        arrive(kc)
                    s = kc * 256 + c * P
                    last = mm3(o[:, c * T:(c + 1) * T], wh[:, s:s + P], wl[:, s:s + P], xh[:, kc, :], xl[:, kc, :],
                               kc == 0, kc == KC - 1)
            return last

        def pe_panel_rows(pe, m, k, o, xh, xl, first, last_panel):
            pe.wait_ge(lo_done, 4 * m + k + 1)
            wh, wl = w_hi[slot(k)], w_lo[slot(k)]
            for kk in range(2):
                for c in range(8):
                    s = kk * D + c * P
                    last = mm3(o[c // 2][:, (c % 2) * T:(c % 2 + 1) * T], wh[:, s:s + P], wl[:, s:s + P], xh(kk), xl(kk),
                               first and kk == 0 and c % 2 == 0, last_panel and kk == 1, skip=True)
            return last

        def pe_used(pe, last):
            last.then_inc(split_free, 1)

        MOD_AT = 440

        def pe_mod(pe, pair, src, col):
            pe.wait_ge(mod_used, 2 + 2 * pair + 2)
            for n in range(2):
                for c in range(2):
                    last = nc.tensor.matmul(bank[7][:, bass.ds(col + 2 * n + c, 1)], src[:, n, c * P:(c + 1) * P], ones[:, 0:1],
                                            start=True, stop=True)
            last.then_inc(macc_free, 2)

        def pe_norm_sum(pe, q):
            for kc in range(KC):
                pe.wait_ge(sq_done, KC * q + kc + 1)
                last = nc.tensor.matmul(bank[6][:, 0:T], ones, tbuf[:, kc, :], start=kc == 0, stop=kc == KC - 1)
            last.then_inc(ss_done, 1)

        def pe_layer(pe, l, ahead):
            m = 11 * l
            pe.wait_ge(lc_ready, 16 * l + 16)
            pe_norm_sum(pe, 2 * l)

            def arrive(kc):
                pe.wait_ge(act_ready, 16 * l + kc + 1)

            def turn(j):
                if j == 0:
                    pe.wait_ge(nr_sq, 5 * l + 2)
                    pe.wait_ge(gfree[0], 7 * l + 2)
                    pe.wait_ge(gfree[1], 7 * l + 2)
                else:
                    pe.wait_ge(nr_sq, 5 * l + 2 + j)
                    pe.wait_ge(gfree[(j + 1) % 2], 7 * l + 4)
                if j == 2:
                    pe.wait_ge(nr_out, 4 * l + 1)
                o = 2 * (j % 2)
                nc.tensor.matmul(bank[o][:, :], cst[:, C_BD:C_BD + P], tbuf[:, 2 * j:2 * j + 2, :], start=True, stop=True)
                nc.tensor.matmul(bank[o + 1][:, :], cst[:, C_ROT:C_ROT + P], ybuf[j], start=True, stop=True).then_inc(nr_mm, 1)

            G = lambda g: bank[4 + g % 2]
            for g, k in ((0, L_K0K1), (1, L_K2V0)):
                pe_gfree(pe, l, g)
                pe_used(pe, pe_panel(pe, m, k, G(g), act_hi, act_lo, arrive if g == 0 else None))
            pe_gfree(pe, l, 2)
            pe.wait_ge(lo_done, 4 * m + L_V1V2 + 1)
            wh, wl = w_hi[slot(L_V1V2)], w_lo[slot(L_V1V2)]
            for tt in range(TT):
                for kc in range(KC):
                    ts = slice(tt * P, (tt + 1) * P)
                    last = mm3(G(2)[:, tt * T:(tt + 1) * T], act_hi[:, kc, ts], act_lo[:, kc, ts],
                               wh[:, kc * 256:(kc + 1) * 256], wl[:, kc * 256:(kc + 1) * 256], kc == 0, kc == KC - 1)
            pe_used(pe, last)
            pe_gfree(pe, l, 3)
            pe.wait_ge(gw_lo, l + 1)
            for tt in range(TT):
                for kc in range(KC):
                    ts = slice(tt * P, (tt + 1) * P)
                    last = mm3(G(3)[:, tt * 24:(tt + 1) * 24], act_hi[:, kc, ts], act_lo[:, kc, ts], gwh[:, kc, :], gwl[:, kc, :],
                               kc == 0, kc == KC - 1)
            last.then_inc(gfull, 1)
            pe_gfree(pe, l, 4)
            pe_used(pe, pe_panel(pe, m, L_Q0, G(4), act_hi, act_lo))
            turn(0)
            pe.wait_ge(tb_lo, l + 1)
            pe.wait_ge(lo_done, 4 * m + L_CMP + 1)
            for jj in range(16):
                s = slice(jj * P, (jj + 1) * P)
                last = mm3(bank[6][:, 0:60], w_hi[slot(L_CMP)][:, s], w_lo[slot(L_CMP)][:, s], tbh[:, jj, :], tbl[:, jj, :],
                           jj == 0, jj == 15)
            pe_used(pe, last)
            turn(1)
            pe_gfree(pe, l, 5)
            pe_used(pe, pe_panel(pe, m, L_Q1, G(5), act_hi, act_lo, lambda kc: pe.wait_ge(cmp_s, l + 1) if kc == KC - 1 else None))
            w2 = lc[:, LC_W2:LC_W2 + 64]
            nc.tensor.matmul(bank[6][0:64, 64:79], w2[0:64, :], hs[0:64, 0:15], start=True, stop=True)
            nc.tensor.matmul(bank[6][64:128, 64:79], w2[0:64, :], hs[0:64, 15:30], start=True, stop=True)
            for v in range(2):
                last = nc.tensor.matmul(bank[6][0:15, 128 + 64 * v:192 + 64 * v], hs[64:128, 30 + 15 * v:45 + 15 * v],
                                        w2[64:128, :], start=True, stop=True)
            last.then_inc(cmp_w2, 1)
            pe_gfree(pe, l, 6)
            pe_used(pe, pe_panel(pe, m, L_U0, G(6), act_hi, act_lo))
            turn(2)
            pe_gfree(pe, l, 7)
            pe_used(pe, pe_panel(pe, m, L_U1, G(7), act_hi, act_lo))
            pe.wait_ge(nr_sq, 5 * l + 5)
            pe.wait_ge(cmp_y, l + 1)
            nc.tensor.matmul(bank[6][:, 256:271], cst[:, C_BD:C_BD + P], sqc[:, 0:15], start=True, stop=True)
            nc.tensor.matmul(bank[6][:, 288:303], cst[:, C_ROT:C_ROT + P], ycmp, start=True, stop=True).then_inc(nr_mm, 1)
            pe.wait_ge(nr_out, 4 * l + 3)
            pe.wait_ge(masks_ready, 3)
            pe_scores(pe, l, 0, False)
            pe_scores(pe, l, 1, False)
            pe.wait_ge(nr_out, 4 * l + 4)
            pe_scores(pe, l, 0, True)
            pe_scores(pe, l, 1, True)
            pe.wait_ge(modc_ready, 3 * l + 1)
            for i in range(8):
                pe_turn(pe, l, i)
                if i + 2 < 8:
                    pe.wait_ge(at_exp, 8 * l + i + 1)
                    pe_scores(pe, l, i + 2, False)
                    pe_scores(pe, l, i + 2, True)
                pe_pv(pe, l, i)
            for n in range(4):
                pe_mod(pe, 12 * l + 4 + n, mod_sums[:, 2 * n:2 * n + 2, :], MOD_AT + 16 + 4 * n)
            pe.wait_ge(pooled_ready, l + 1)
            for g in range(4):
                if g % 2 == 0:
                    pe_gfree(pe, l, 12 + g // 2)
                src = wb[g % 2]
                last = nc.tensor.matmul(bank[4 + g // 2][:, (g % 2) * T:(g % 2 + 1) * T], lc[:, LC_PW + g * P:LC_PW + (g + 1) * P],
                                        src[:, g, 16:16 + T], start=True, stop=True)
                if g % 2:
                    last.then_inc(gfull, 1)
            for i in range(4):
                if i < 2:
                    pe.wait_ge(gfree[i], 7 * l + 8)
                    pe.wait_ge(gfree[1 - i], 7 * l + 8)
                else:
                    pe.wait_ge(x_ready, 16 * l + 8 + 2 * (i - 2) + 2)
                last = pe_panel(pe, m, L_OUT + i, bank[4 + i % 2], mix_hi, mix_lo)
                pe_used(pe, last)
            pe.wait_ge(modc_ready, 3 * l + 2)
            for n in (4, 5):
                pe_mod(pe, 12 * l + 4 + n, mod_sums[:, 2 * n:2 * n + 2, :], MOD_AT + 16 + 4 * n)
            pe_norm_sum(pe, 2 * l + 1)
            pe.wait_ge(modc_ready, 3 * l + 3)
            pe_ff(pe, l, m, lambda kc: pe.wait_ge(act_ready, 16 * l + KC + kc + 1), 16 * l, L_FF, "ahead" if ahead else "tail")

        def pe_ff(pe, l, m, arrive, j0, k0, mods=None):
            def up(mm, k, jn, par, arr=None):
                pe.wait_ge(ff_relu, jn + 1)
                last = pe_panel(pe, mm, k, bank[4 + par], act_hi, act_lo, arr)
                pe_used(pe, last)

            def down(mm, k, jn, par, first, final):
                pe.wait_ge(ff_ready, 2 + jn + 1)
                last = pe_panel_rows(pe, mm, k, bank[0:4], lambda kk: ff_hi[:, par, kk * T:(kk + 1) * T],
                                     lambda kk: ff_lo[:, par, kk * T:(kk + 1) * T], first, final)
                pe_used(pe, last)

            up(m, k0, j0, 0, arrive)
            up(m, k0 + 1, j0 + 1, 1)
            down(m, k0 + 2, j0, 0, True, False)
            up(m, k0 + 3, j0 + 2, 0)
            down(m, k0 + 4, j0 + 1, 1, False, False)
            if mods == "tail":
                pe_mod(pe, 12 * l + 10, macc, MOD_AT + 40)
            with pe.Fori(1, FF_STEPS // 2 - 1) as i:
                up(m + i, k0 + 1, j0 + 2 * i + 1, 1)
                down(m + i, k0 + 2, j0 + 2 * i, 0, False, False)
                up(m + i, k0 + 3, j0 + 2 * i + 2, 0)
                down(m + i, k0 + 4, j0 + 2 * i + 1, 1, False, False)
                if mods == "ahead":
                    pe_mod(pe, 12 * l + 9 + i, macc, MOD_AT + 36 + 4 * i)
            e = m + FF_STEPS // 2 - 1
            up(e, k0 + 1, j0 + FF_STEPS - 1, 1)
            down(e, k0 + 2, j0 + FF_STEPS - 2, 0, False, False)
            if mods == "tail":
                pe_mod(pe, 12 * l + 11, macc, MOD_AT + 44)
            down(e, k0 + 3, j0 + FF_STEPS - 1, 1, False, True)

        def pe_scores(pe, l, i, cmp):
            b, g = i // 2, i % 2
            h = slice(64 * g, 64 * g + 64)
            s0, s1 = bank[2 * (i % 2)], bank[2 * (i % 2) + 1]
            if cmp:
                for tt in range(TT):
                    o = s0[:, 256 + 16 * tt:271 + 16 * tt]
                    nc.tensor.matmul(o, qr[h, b, tt * P:(tt + 1) * P], kcmp[h, :], start=True, stop=False)
                    last = nc.tensor.matmul(o, idb[:, :], cmpmb[:, 16 * tt:16 * tt + 15], start=False, stop=True)
                last.then_inc(at_sc, 1)
                return
            both = lambda ap, n: ap.rearrange("p (b s) -> p b s", b=2)[:, :, n:n + P]
            mask = causb[:, :].unsqueeze(1).to_broadcast([P, 2, P])
            nc.tensor.matmul(s0[:, 0:T], qr[h, b, 0:P], kr[h, :, 0:P], start=True, stop=False)
            nc.tensor.matmul(s0[:, 0:T], idb[:, :], mask, start=False, stop=True)
            nc.tensor.matmul(s1[:, :], qr[h, b, P:T], kr[h, :, :], start=True, stop=False, skip_group_check=True)
            nc.tensor.matmul(both(s1[:, :], P), idb[:, :], mask, start=False, stop=True, skip_group_check=True)

        def pe_turn(pe, l, i):
            pe.wait_ge(at_p, 8 * l + i + 1)
            if i:
                pe.wait_ge(at_ev0, 8 * l + i)
                pe.wait_ge(at_ev1, 8 * l + i)
            pb = pbuf[i % 2]
            for n in range(6):
                br, part = n // 3, n % 3
                src = pb[:, br * P:(br + 1) * P] if part == 0 else pb[:, 288 + br * T + (part - 1) * P:288 + br * T + part * P]
                nc.tensor.transpose(bank[6 + n // 4][:, (n % 4) * P:(n % 4 + 1) * P], src, ident)
            for tt in range(TT):
                last = nc.tensor.transpose(bank[7][0:15, T + tt * P:T + (tt + 1) * P], pb[:, 256 + 16 * tt:271 + 16 * tt], ident)
            last.then_inc(at_tr, 1)

        def pe_pv(pe, l, i):
            b, g = i // 2, i % 2
            o = bank[4 + b % 2][64 * g:64 * g + 64, 0:T]
            if g == 0:
                pe_gfree(pe, l, 8 + b)
            pe.wait_ge(at_ev0, 8 * l + i + 1)
            pe.wait_ge(at_ev1, 8 * l + i + 1)
            pt = pts[i % 2]
            for br in range(2):
                v = slice(br * P + 64 * g, br * P + 64 * g + 64)
                nc.tensor.matmul(o, vt[:, 0, v], pt[:, br * 384:br * 384 + T], start=br == 0, stop=False, skip_group_check=True)
                nc.tensor.matmul(o[:, P:T], vt[:, 1, v], pt[:, br * 384 + T:br * 384 + 384], start=False, stop=False, skip_group_check=True)
            nc.tensor.matmul(o, vcmp[0:15, 64 * g:64 * g + 64], pt[0:15, 768:1024], start=False, stop=True,
                             skip_group_check=True).then_inc(at_pv, 1)


        ACT_LINKS = 7

        def rsqrt(link, o, src, scale, eps):
            link(nc.scalar.activation(o, src, ACT.Ln, bias=eps, scale=scale))
            return nc.scalar.activation(o, o, ACT.Exp, scale=-0.5)

        def act_norm(act, l, q, link, shift, extra=()):
            for kc in range(KC):
                act.wait_ge(x_ready, 8 * q + kc + 1)
                nc.scalar.activation(tbuf[:, kc, :], x[:, kc, :], ACT.Square).then_inc(sq_done, 1)
            for f in extra:
                f()
            act.wait_ge(ss_done, q + 1)
            rsqrt(link, rs[:, :], bank[6][:, 0:T], 1.0 / D, cst[:, C_EPS:C_EPS + 1]).then_inc(rs_done, 1)
            for kc in range(KC):
                act.wait_ge(t_done, 8 * q + kc + 1)
                nc.scalar.activation(act_hi[:, kc, :], tbuf[:, kc, :], ACT.Identity, bias=modc[:, shift + kc:shift + kc + 1])\
                    .then_inc(act_his, 1)

        def act_layer(act, l, link, ahead):
            m = 11 * l
            used = lambda k: act.wait_ge(split_free, SPLIT + 4 * m + k + 1)
            act.wait_ge(lc_ready, 16 * l + 16)
            nc.scalar.activation(gwh[:, :, :], lc[:, LC_GW:LC_GW + 192].rearrange("p (k n) -> p k n", k=KC), ACT.Copy).then_inc(gw_hi, 1)
            act_norm(act, l, 2 * l, link, 0, (lambda: split_hi(act, m, 1),))
            split_hi(act, m, 2)
            split_hi(act, m, 3)
            G = lambda g: bank[4 + g % 2]
            used(L_K0K1)
            nc.scalar.activation(tbuf[:, 0, :], G(0)[:, T:2 * T], ACT.Square).then_inc(nr_sq, 1)
            for g in range(2):
                for j2 in range(2):
                    src = win(G(0), 64 * g, 64, [[2, 16], [16, 15]], j2)
                    last = nc.scalar.activation(tb[64 * j2:64 * j2 + 64, :, 15 * g:15 * g + 15], src, ACT.Copy)
            last.then_inc(tb_k, 1)
            split_hi(act, m, 4)
            used(L_K2V0)
            nc.scalar.activation(tbuf[:, 1, :], G(1)[:, 0:T], ACT.Square).then_inc(nr_sq, 1)
            split_hi(act, m, 5)
            act.wait_ge(tb_pe, l + 1)
            nc.scalar.activation(tbh[:, :, :], tb, ACT.Copy).then_inc(tb_hi, 1)
            split_hi(act, m, 6)
            act.wait_ge(gfull, 3 * l + 1)
            nc.scalar.activation(gts[:, :, :], G(3)[:, 0:48].rearrange("p (t n) -> p t n", t=TT), ACT.Exp, scale=-1.0).then_inc(gfree[1], 1)
            used(L_Q0)
            nc.scalar.activation(tbuf[:, 2:4, :], G(4)[:, :].rearrange("p (b t) -> p b t", b=2), ACT.Square).then_inc(nr_sq, 1)
            split_hi(act, m, 7)

            def roots(j):
                act.wait_ge(nr_mm, 4 * l + j + 1)
                rsqrt(link, tbuf[:, 2 * j:2 * j + 2, :], bank[2 * (j % 2)][:, :].rearrange("p (b t) -> p b t", b=2), 1.0 / 64,
                      cst[:, C_EPS:C_EPS + 1]).then_inc(nr_rs, 1)

            roots(0)
            used(L_CMP)
            nc.scalar.activation(ce, bank[6][:, 0:60], ACT.Exp, scale=-1.0).then_inc(cmp_e, 1)
            split_hi(act, m, 8)
            roots(1)
            used(L_Q1)
            nc.scalar.activation(tbuf[:, 4:6, :], G(5)[:, :].rearrange("p (b t) -> p b t", b=2), ACT.Square).then_inc(nr_sq, 1)
            act.wait_ge(cmp_w2, l + 1)
            nc.scalar.activation(sqc[:, 0:15], bank[6][:, 64:79], ACT.Square).then_inc(nr_sq, 1)
            split_hi(act, m, 9)
            used(L_U0)
            nc.scalar.activation(ub[:, 0:2, 16:16 + T], G(6)[:, :].rearrange("p (b t) -> p b t", b=2), ACT.Copy).then_inc(gfree[0], 1)
            roots(2)
            split_hi(act, m, 10)
            used(L_U1)
            link(nc.scalar.activation(ub[:, 2:4, 16:16 + T], G(7)[:, :].rearrange("p (b t) -> p b t", b=2), ACT.Copy))
            act.sem_inc(gfree[1], 1)
            act.sem_inc(u_copied, 2)
            act.wait_ge(nr_mm, 4 * l + 4)
            rsqrt(link, sqc[:, 16:31], bank[6][:, 256:271], 1.0 / 64, cst[:, C_EPS:C_EPS + 1]).then_inc(nr_rs, 1)
            split_hi(act, m, 11)

            def exponentials(i):
                s0, s1, pb = bank[2 * (i % 2)], bank[2 * (i % 2) + 1], pbuf[i % 2]
                if i >= 2:
                    act.wait_ge(at_tr, 8 * l + i - 1)
                act.wait_ge(at_nm, 8 * l + i + 1)
                for n, (src, dst) in enumerate((
                        (s0[:, 0:P], pb[:, 0:P]), (s0[:, P:T], pb[:, P:T]),
                        (s0[:, 256:271], pb[:, 256:271]), (s0[:, 272:287], pb[:, 272:287]),
                        (s1[:, 0:T], pb[:, 288:288 + T]), (s1[:, T:2 * T], pb[:, 288 + T:288 + 2 * T]))):
                    last = nc.scalar.activation(dst, src, ACT.Exp, bias=nm[:, i % 2, n:n + 1], accum_out=dens[:, i % 2, n:n + 1])
                last.then_inc(at_exp, 1)

            exponentials(0)
            exponentials(1)
            for i in range(8):
                act_pt(act, l, i)
                if i + 2 < 8:
                    exponentials(i + 2)
                if i >= 2 and i % 2 == 0:
                    act_mixed(act, l, (i - 2) // 2)
            act_mixed(act, l, 3)
            for g in range(4):
                act.wait_ge(gfull, 3 * l + 2 + g // 2)
                nc.scalar.activation(mix_hi[:, g, :], bank[4 + g // 2][:, (g % 2) * T:(g % 2 + 1) * T], ACT.Copy,
                                     scale=lc[:, LC_PS + g:LC_PS + g + 1]).then_inc(mix_his, 1)
            for k in range(3):
                split_hi(act, m, 12 + k)
            act_norm(act, l, 2 * l + 1, link, 24)
            act_ff(act, l, m, L_FF, 16 * l)

        def act_pt(act, l, i):
            act.wait_ge(at_tr, 8 * l + i + 1)
            if i >= 2:
                act.wait_ge(at_pv, 8 * l + i - 1)
            nc.scalar.activation(pts[i % 2][:, 0:512], bank[6][:, :], ACT.Copy).then_inc(at_ev0, 1)

        def act_mixed(act, l, b):
            act.wait_ge(at_pv, 8 * l + 2 * b + 2)
            nc.scalar.activation(mix_hi[:, 4 + b, :], bank[4 + b % 2][:, 0:T], ACT.Copy).then_inc(mix_his, 1)

        def act_ff(act, l, m, k0, j0, final=False):
            def step(mm, jn, kf, par, kd, s, at):
                act.wait_ge(split_free, SPLIT + 4 * mm + kf + 1)
                act.wait_ge(ff_ready, jn + 1)
                nc.scalar.activation(fr[par], bank[4 + par][:, :], ACT.Relu).then_inc(ff_relu, 1)
                for k in s[:1]:
                    split_hi(act, mm, k)
                act.wait_ge(ff_sq, jn + 1)
                if kd is not None:
                    act.wait_ge(split_free, SPLIT + 4 * mm + kd + 1)
                nc.scalar.activation(ff_hi[:, par, :], fr[par], ACT.Copy).then_inc(ff_his, 1)
                for k in s[1:]:
                    split_hi(act, mm, k)

            ff_schedule(act, m, k0, j0, step, final)

        def ff_schedule(eng, m, k0, j0, step, final):
            step(m, j0, k0, 0, None, (k0 + 3, k0 + 4), 0)
            step(m, j0 + 1, k0 + 1, 1, None, (k0 + 5, k0 + 6), 1)
            with eng.Fori(1, FF_STEPS // 2 - 1) as i:
                step(m + i, j0 + 2 * i, k0 - 1, 0, k0 - 2, (k0 + 3, k0 + 4), i)
                step(m + i, j0 + 2 * i + 1, k0 + 1, 1, k0, (k0 + 5, k0 + 6), i)
            e = m + FF_STEPS // 2 - 1
            step(e, j0 + FF_STEPS - 2, k0 - 1, 0, k0 - 2, (k0 + 3,) if final else (k0 + 3, k0 + 4), 14)
            step(e, j0 + FF_STEPS - 1, k0 + 1, 1, k0, (), 15)

        DVE_LINKS = 31

        def dve_mod(dve, pair, o, half):
            if half == 0:
                dve.wait_ge(modraw[0], 16 * (pair + 1))
                dve.wait_ge(modraw[1], 16 * (pair + 1))
            for n in range(8 * half, 8 * half + 8):
                kc, p = n // 2, n % 2
                if n >= 2:
                    dve.wait_ge(mod_links, 14 * pair + n - 1)
                src, c = modw[:, p, kc * 256:kc * 256 + 256], cact[:, kc:kc + 1]
                if n < 2:
                    ins = nc.vector.tensor_scalar(o[:, p, :], src, c, None, ALU.mult)
                else:
                    ins = nc.vector.scalar_tensor_tensor(o[:, p, :], src, c, o[:, p, :], ALU.mult, ALU.add)
                ins.then_inc(mod_links if n < 14 else mod_used, 1)

        def dve_modc(dve, done, count, c0, bias, pair):
            dve.wait_ge(macc_free, 2 + 2 * pair + 2)
            n = bias.shape[1]
            c1 = 0 if c0 == 48 else c0
            nc.vector.tensor_tensor(modc[:, c1:c1 + n], bank[7][:, MOD_AT + c0:MOD_AT + c0 + n], bias, ALU.add).then_inc(done, 1)
            dve.wait_ge(done, count)

        def dve_norm(dve, q, g0, shift):
            dve.wait_ge(rs_done, q + 1)
            for kc in range(KC + 1):
                if kc < KC:
                    nc.vector.scalar_tensor_tensor(tbuf[:, kc, :], x[:, kc, :], gcol[:, g0 + kc:g0 + kc + 1], rs[:, :], ALU.mult, ALU.mult)\
                        .then_inc(t_done, 1)
                if kc:
                    c = kc - 1
                    dve.wait_ge(act_his, 8 * q + c + 1)
                    nc.vector.scalar_tensor_tensor(act_lo[:, c, :], tbuf[:, c, :], modc[:, shift + c:shift + c + 1],
                                                   act_hi[:, c, :].bitcast(F32), ALU.add, ALU.subtract).then_inc(act_ready, 1)

        def dve_layer(dve, l, link, ahead):
            m = 11 * l
            used = lambda k: dve.wait_ge(split_free, SPLIT + 4 * m + k + 1)
            G = lambda g: bank[4 + g % 2]
            two = lambda ap: ap.rearrange("p (b t) -> p b t", b=2)
            dve_norm(dve, 2 * l, 0, 0)
            for k in (1, 2, 3):
                split_lo(dve, m, k)
            dve.wait_ge(gw_hi, l + 1)
            nc.vector.tensor_tensor(gwl[:, :, :], lc[:, LC_GW:LC_GW + 192].rearrange("p (k n) -> p k n", k=KC), gwh[:, :, :].bitcast(F32),
                                    ALU.subtract).then_inc(gw_lo, 1)
            used(L_K0K1)
            dve.wait_ge(tb_k, l + 1)
            nc.vector.tensor_scalar(ybuf[0][:, 0, :], G(0)[:, T:2 * T], lc[:, LC_KN + 1:LC_KN + 2], None, ALU.mult).then_inc(gfree[0], 1)
            split_lo(dve, m, 4)
            used(L_K2V0)
            dve.wait_ge(nr_sq, 5 * l + 2)
            for g in range(2):
                for j2 in range(2):
                    src = win(G(1), 64 * g, 64, [[2, 16], [16, 15]], T + j2)
                    last = nc.vector.tensor_copy(tb[64 * j2:64 * j2 + 64, :, 30 + 15 * g:45 + 15 * g], src)
            last.then_inc(tb_v, 1)
            nc.vector.tensor_scalar(ybuf[0][:, 1, :], G(1)[:, 0:T], lc[:, LC_KN + 2:LC_KN + 3], None, ALU.mult).then_inc(gfree[1], 1)
            dve.wait_ge(tb_v, l + 1)
            pe_bc = win(lc, 0, P, [[2, 16], [1, 2], [0, 30]], LC_PE)
            tb4 = tb.rearrange("p j (v n) -> p j v n", v=2)
            nc.vector.tensor_tensor(tb4, tb4, pe_bc, ALU.add).then_inc(tb_pe, 1)
            split_lo(dve, m, 5)
            used(L_V1V2)
            nc.vector.tensor_copy(vt, two(G(2)[:, :])).then_inc(gfree[0], 1)
            dve.wait_ge(tb_hi, l + 1)
            nc.vector.tensor_tensor(tbl[:, :, :], tb, tbh[:, :, :].bitcast(F32), ALU.subtract).then_inc(tb_lo, 1)
            split_lo(dve, m, 6)
            dve.wait_ge(gfree[1], 7 * l + 3)
            link(nc.vector.tensor_scalar(gts[:, :, :], gts[:, :, :], 1.0, None, ALU.add))
            link(nc.vector.reciprocal(gts[:, :, :], gts[:, :, :]))
            link(nc.vector.tensor_scalar(gts[:, 0, 0:24:3], gts[:, 0, 0:24:3], cst[:, C_VALID:C_VALID + 1], None, ALU.mult))

            def scaled(j):
                dve.wait_ge(nr_sq, 5 * l + 2 + j)
                nc.vector.tensor_scalar(ybuf[j], two(G(3 + j)[:, :]), lc[:, LC_QN:LC_QN + 1], 0.125, ALU.mult, ALU.mult).then_inc(gfree[(j + 1) % 2], 1)

            def rotated(j):
                dst = kr if j == 0 else qr[:, 2 * j - 2:2 * j, :]
                dve.wait_ge(nr_mm, 4 * l + j + 1)
                link(nc.vector.tensor_tensor(dst, two(bank[2 * (j % 2) + 1][:, :]), cst[:, C_SIN:C_SIN + T].unsqueeze(1).to_broadcast([P, 2, T]), ALU.mult))
                dve.wait_ge(nr_yc, 3 * l + j + 1)
                link(nc.vector.tensor_tensor(dst, dst, ybuf[j], ALU.add))
                dve.wait_ge(nr_rs, 4 * l + j + 1)
                nc.vector.tensor_tensor(dst, dst, tbuf[:, 2 * j:2 * j + 2, :], ALU.mult).then_inc(nr_out, 1)

            scaled(1)
            split_lo(dve, m, 7)
            rotated(0)
            dve.wait_ge(cmp_e, l + 1)
            link(nc.vector.tensor_scalar(ce, ce, 1.0, None, ALU.add))
            link(nc.vector.reciprocal(ce, ce))
            nc.vector.tensor_tensor(hs, bank[6][:, 0:60], ce, ALU.mult).then_inc(cmp_s, 1)
            split_lo(dve, m, 8)
            rotated(1)
            scaled(2)
            dve.wait_ge(cmp_w2, l + 1)
            dve.wait_ge(nr_sq, 5 * l + 5)
            nc.vector.tensor_copy(vcmp[0:15, :], bank[6][0:15, P:T])
            nc.vector.tensor_scalar(ycmp, bank[6][:, 64:79], lc[:, LC_KN:LC_KN + 1], None, ALU.mult).then_inc(cmp_y, 1)
            split_lo(dve, m, 9)
            rotated(2)
            split_lo(dve, m, 10)
            dve.wait_ge(nr_mm, 4 * l + 4)
            link(nc.vector.tensor_tensor(ycmp, ycmp, cst[:, C_CCOS:C_CCOS + 15], ALU.mult))
            dve.wait_ge(nr_rs, 4 * l + 4)
            link(nc.vector.tensor_tensor(kcmp, bank[6][:, 288:303], cst[:, C_CSIN:C_CSIN + 15], ALU.mult))
            link(nc.vector.tensor_tensor(kcmp, kcmp, ycmp, ALU.add))
            nc.vector.tensor_tensor(kcmp, kcmp, sqc[:, 16:31], ALU.mult).then_inc(nr_out, 1)
            split_lo(dve, m, 11)

            def maxima(i):
                s0, s1, o = bank[2 * (i % 2)], bank[2 * (i % 2) + 1], nm[:, i % 2, :]
                dve.wait_ge(at_sc, 8 * l + i + 1)
                nc.vector.tensor_reduce(o[:, 0:2], two(s0[:, 0:T]), AX.X, ALU.max, negate=True)
                nc.vector.tensor_reduce(o[:, 2:4], win(s0, 0, P, [[16, 2], [1, 15]], T), AX.X, ALU.max, negate=True)
                nc.vector.tensor_reduce(o[:, 4:6], two(s1[:, :]), AX.X, ALU.max, negate=True).then_inc(at_nm, 1)

            def weigh(i):
                b, g = i // 2, i % 2
                pb, f, d = pbuf[i % 2], fac[:, i % 2, :], dens[:, i % 2, :]
                dve.wait_ge(at_exp, 8 * l + i + 1)
                link(nc.vector.reciprocal(f, d))
                h0 = 3 * (4 * g + b)
                nc.vector.tensor_tensor(f[:, 0:2], f[:, 0:2], gts[:, 0, h0 + 1:h0 + 3], ALU.mult)
                nc.vector.tensor_tensor(f[:, 2:4], f[:, 2:4], gts[:, :, h0], ALU.mult)
                link(nc.vector.tensor_tensor(f[:, 4:6], f[:, 4:6], gts[:, 1, h0 + 1:h0 + 3], ALU.mult))
                for n, (c0, w) in enumerate(((0, P), (P, P), (256, 15), (272, 15), (288, T), (288 + T, T))):
                    last = nc.vector.tensor_scalar(pb[:, c0:c0 + w], pb[:, c0:c0 + w], f[:, n:n + 1], None, ALU.mult)
                last.then_inc(at_p, 1)

            def copy_pt(i):
                dve.wait_ge(at_tr, 8 * l + i + 1)
                if i >= 2:
                    dve.wait_ge(at_pv, 8 * l + i - 1)
                nc.vector.tensor_copy(pts[i % 2][:, 512:768], bank[7][:, 0:T])
                nc.vector.tensor_copy(pts[i % 2][0:15, 768:1024], bank[7][0:15, T:2 * T]).then_inc(at_ev1, 1)

            def mixed(b):
                dve.wait_ge(mix_his, 8 * l + b + 1)
                nc.vector.tensor_tensor(mix_lo[:, 4 + b, :], bank[4 + b % 2][:, 0:T], mix_hi[:, 4 + b, :].bitcast(F32), ALU.subtract)\
                    .then_inc(gfree[b % 2], 1)

            def mod(half):
                pair = half // 2
                dve_mod(dve, 12 * l + 4 + pair, mod_sums[:, 2 * pair:2 * pair + 2, :], half % 2)

            maxima(0)
            maxima(1)
            weigh(0)
            for i in range(8):
                if i + 1 < 8:
                    weigh(i + 1)
                copy_pt(i)
                mod(i)
                if i + 2 < 8:
                    maxima(i + 2)
                if i >= 2 and i % 2 == 0:
                    mixed((i - 2) // 2)
            mixed(3)
            dve_modc(dve, modc_ready, 3 * l + 2, 16, lc[:, LC_BM:LC_BM + 16], 12 * l + 7)
            for g in range(4):
                dve.wait_ge(mix_his, 8 * l + 4 + g // 2 * 2 + 2)
                last = nc.vector.scalar_tensor_tensor(mix_lo[:, g, :], bank[4 + g // 2][:, (g % 2) * T:(g % 2 + 1) * T],
                                                      lc[:, LC_PS + g:LC_PS + g + 1], mix_hi[:, g, :].bitcast(F32), ALU.mult, ALU.subtract)
                if g % 2:
                    last.then_inc(gfree[g // 2], 1)
            for i in range(4):
                mod(8 + i)
                if i < 3:
                    split_lo(dve, m, 12 + i)
                used(L_OUT + i)
                for c in range(2):
                    kc = 2 * i + c
                    nc.vector.scalar_tensor_tensor(x[:, kc, :], bank[4 + i % 2][:, c * T:(c + 1) * T], modc[:, 16 + kc:17 + kc], x[:, kc, :],
                                                   ALU.mult, ALU.add).then_inc(x_ready, 1)
            dve_modc(dve, modc_ready, 3 * l + 3, 32, lc[:, LC_BM + 16:LC_BM + 24], 12 * l + 9)
            link(nc.vector.scalar_tensor_tensor(gcol[:, KC:2 * KC], modc[:, 32:40], 1.0, lc[:, LC_N2:LC_N2 + KC], ALU.add, ALU.mult))
            dve_norm(dve, 2 * l + 1, KC, 24)
            dve_ff(dve, m, L_FF, 16 * l, l=l, mods="ahead" if ahead else "tail")
            if ahead:
                dve.wait_ge(macc_free, 2 + 24 * l + 32)
                nc.vector.tensor_tensor(modc[:, 0:16], bank[7][:, MOD_AT + 48:MOD_AT + 64], lc[:, LC_BA:LC_BA + 16], ALU.add)
            dve_modc(dve, modc_ready, 3 * l + 4, 40, lc[:, LC_BM + 24:LC_BM + 32], 12 * l + 11)
            if ahead:
                nc.vector.scalar_tensor_tensor(gcol[:, 0:KC], modc[:, 8:16], 1.0, lc[:, LC_NA:LC_NA + KC], ALU.add, ALU.mult)
            dve.wait_ge(split_free, SPLIT + 4 * m + L_PANELS)
            for kc in range(KC):
                nc.vector.scalar_tensor_tensor(x[:, kc, :], bank[kc // 2][:, (kc % 2) * T:(kc % 2 + 1) * T], modc[:, 40 + kc:41 + kc],
                                               x[:, kc, :], ALU.mult, ALU.add).then_inc(x_ready, 1)

        def dve_ff(dve, m, k0, j0, final=False, l=0, mods=None):
            def mod(at, half):
                inside = not isinstance(at, int)
                if mods == "ahead" and inside:
                    pair = 12 * l + 9 + at
                elif mods == "tail" and not inside:
                    pair = 12 * l + (10 if at < 2 else 11)
                else:
                    return
                if half == 0:
                    dve.wait_ge(macc_free, 2 * pair + 2)
                dve_mod(dve, pair, macc, half)

            def step(mm, jn, kf, par, kd, s, at):
                dve.wait_ge(ff_relu, 2 + jn + 1)
                nc.vector.tensor_tensor(fr[par], fr[par], fr[par], ALU.mult).then_inc(ff_sq, 1)
                for k in s[:1]:
                    split_lo(dve, mm, k)
                mod(at, par)
                dve.wait_ge(ff_his, jn + 1)
                nc.vector.tensor_tensor(ff_lo[:, par, :], fr[par], ff_hi[:, par, :].bitcast(F32), ALU.subtract).then_inc(ff_ready, 1)
                for k in s[1:]:
                    split_lo(dve, mm, k)

            ff_schedule(dve, m, k0, j0, step, final)

        M2 = L_PANELS // SPLIT * layers
        used2 = lambda eng, k: eng.wait_ge(split_free, SPLIT + 4 * M2 + k + 1)
        free2 = lambda eng, k: eng.wait_ge(gfree[k % 2], 7 * layers + k // 2 + 1)
        G2 = lambda k: bank[4 + k % 2]
        blocks2 = lambda ap: ap.rearrange("p (b t) -> p b t", b=2)
        XR = 16 * layers + 8

        dt_mm, dt_y, dt_n, dt_e, dt_pos, dt_ln, dt_done, dt_tr, dt_cols = [sem(n) for n in ("dt_mm", "dt_y", "dt_n", "dt_e", "dt_pos", "dt_ln", "dt_done", "dt_tr", "dt_cols")]
        pads_ready = sem("pads_ready")
        alog_e = sem("alog_e")
        d_stored = sem("d_stored")
        lc2_ready = sem("lc2_ready")
        dist_ready = sem("dist_ready")
        s2_sc = sem("s2_sc")
        s2_nm = sem("s2_nm")
        s2_exp = sem("s2_exp")
        s2_p = sem("s2_p")
        s2_tr = sem("s2_tr")
        s2_ev0, s2_ev1 = sem("s2_ev0"), sem("s2_ev1")
        s2_pv = sem("s2_pv")
        s2_hi, s2_lo = sem("s2_hi"), sem("s2_lo")
        conv_done = sem("conv_done")
        silu_done = sem("silu_done")
        cb_mm, cb_done = sem("cb_mm"), sem("cb_done")
        xt_mm0, xt_mm1, xt_done0, xt_done1 = sem("xt_mm0"), sem("xt_mm1"), sem("xt_done0"), sem("xt_done1")
        db_ready = [sem(f"db_ready{i}") for i in range(4)]
        e_mask = sem("e_mask")
        e_exp = sem("e_exp")
        e_mul = sem("e_mul")
        e_used = sem("e_used")
        y_out = sem("y_out")
        z_silu = sem("z_silu")
        y_gated = sem("y_gated")
        y_sq = sem("y_sq")
        y_ss = sem("y_ss")
        y_rs = sem("y_rs")
        y_fin = sem("y_fin")
        y_hi, y_lo = sem("y_hi"), sem("y_lo")
        gates_done = sem("gates_done")
        att_proj = sem("att_proj")
        mx_sum, mx_hi, mx_lo = sem("mx_sum"), sem("mx_hi"), sem("mx_lo")
        x2_ready = sem("x2_ready")
        ln_sum, ln_mean, ln_c, ln_sq, ln_ss, ln_rs, ln_t, ln_hi, ln_x, ln_lo = [
            sem(n) for n in ("ln_sum", "ln_mean", "ln_c", "ln_sq", "ln_ss", "ln_rs", "ln_t", "ln_hi", "ln_x", "ln_lo")]
        o_turned, o_copied = sem("o_turned"), sem("o_copied")

        at[0] = 0
        xb = area(24 * T, 24, T)
        zb_at = at[0]
        zb = area(16 * T, 16, T)
        xt_at = at[0]
        xt = area(8 * T, 2, TT, 2 * T)
        cb = area(4 * T, 2, TT, T)
        work_at = at[0]
        decays = area(12 * T)
        lc2_at = at[0]
        lc2 = area(LC2)
        dtt = area(P, TT, 64)
        gb = arena[:, xt_at:xt_at + 16 * T].rearrange("p (b t) -> p b t", b=16)
        sq2 = arena[:, xt_at + 16 * T:xt_at + 20 * T].rearrange("p (b t) -> p b t", b=4)
        rs2 = arena[:, xt_at + 20 * T:xt_at + 21 * T]
        v2 = arena[:, zb_at:zb_at + 6 * T].rearrange("p (t n) -> p t n", t=TT)
        pp = [arena[:, zb_at + (6 + 3 * i) * T:zb_at + (9 + 3 * i) * T] for i in range(2)]
        dist = arena[:, zb_at + 12 * T:zb_at + 16 * T + 2 * T].rearrange("p (t a s) -> p t a s", t=TT, a=3)
        pt2 = arena[:, xt_at + 2 * T:xt_at + 8 * T].rearrange("p (n t) -> p n t", n=6)
        up = [arena[:, work_at + i * 520:work_at + (i + 1) * 520].rearrange("p (b t) -> p b t", b=2) for i in range(2)]
        dw = [arena[0:64, work_at + 1040 + i * T:work_at + 1040 + (i + 1) * T] for i in range(6)]
        qk = mixf[:, 0:12 * T].rearrange("p (b t) -> p b t", b=12)
        eb = [v[:, i * 6 * T:(i + 1) * 6 * T] for v in (mixf, decays) for i in range(2)]
        eb_far = [v[:, 0:4 * T].rearrange("p (h t) -> p h t", h=4) for v in eb]
        eb_near = [v[:, 4 * T:6 * T].rearrange("p (h t) -> p h t", h=4) for v in eb]
        m2 = zb[:, 0:8, :]
        mx = zb[:, 8:16, :]
        tb2 = xb[:, 0:8, :]
        obuf = xb[:, 8:16, :].rearrange("p b t -> p (b t)").rearrange("p (t d) -> p t d", t=TT)
        ea = small[0:64, 158:159]
        dens2, nm2 = small[:, 150:152], small[:, 152:154]
        dscr = nc.dram_tensor("dscr", (64, T), F32, kind="Internal").ap()
        ATT_SLOT = {0: 0, 1: 1, 3: 2, 4: 3, 6: 4, 7: 5, 9: 6, 10: 7}
        PV_SLOT = {2: 0, 5: 1, 8: 2, 11: 3}
        ALPHA = 2.0 ** 0.25
        slope = lambda h: 2.0 ** (-8.0 * (h + 1) / 12)

        def head2(p, j):
            h = 4 * p + j
            return h // 2, slice(64 * (h % 2), 64 * (h % 2) + 64), h

        def fetch(sp, e):
            hu, st = e // 2, e % 2
            for o, d, t0, t1 in ((eb_far, st, 0, T), (eb_near, 1 - st, st * P, (st + 1) * P)):
                src = dscr[32 * d + 4 * hu:32 * d + 4 * hu + 4, t0:t1].partition_broadcast(P)
                sp.dma_start(o[e % 4], src).then_inc(db_ready[e % 4], 16)

        def finish(sp):
            for k in range(2, 6):
                load(sp, M2, k)
            with sp.Fori(0, 4) as i:
                for k in (6, 7, 8, 9):
                    load(sp, M2 + i, k)
            load(sp, M2, 22)
            load(sp, M2, 23)
            sp.wait_ge(d_stored, 16)
            sp.wait_ge(s2_sc, 8)
            fetch(sp, 0)
            fetch(sp, 1)
            load(sp, M2, 24)
            load(sp, M2, 25)
            sp.wait_ge(conv_done, 12)
            fetch(sp, 2)
            fetch(sp, 3)
            for hu in range(8):
                load(sp, M2, 26 + hu)
                for e in (2 * hu + 4, 2 * hu + 5):
                    if e < 16:
                        sp.wait_ge(e_used, e - 3)
                        fetch(sp, e)
            with sp.Fori(7, 19) as i:
                for k in (6, 7, 8, 9):
                    load(sp, M2 + i, k)
            sp.wait_ge(o_copied, 4)
            sp.dma_start(out.rearrange("b (t p) d -> p (b t) d", p=P), obuf).then_inc(out_written, 16)
            sp.wait_ge(out_written, 16)
            sp.wait_ge(d_stored, 16)

        def pool_second(pool):
            pool.wait_ge(x_ready, 16 * layers)
            pool.dma_start(lc2, a["lc2"]).then_inc(lc2_ready, 16)
            pool.wait_ge(x_ready, XR)
            pool.dma_start(dist.rearrange("p t a s -> p (t a s)"), a["dist"]).then_inc(dist_ready, 16)
            for i in range(2):
                for c0 in (0, 258):
                    last = nc.gpsimd.memset(up[i][:, :, c0:c0 + 2], 0.0)
            last.then_inc(pads_ready, 1)
            pool.wait_ge(dt_done, 1)
            pool.dma_start(dscr, dw[5]).then_inc(d_stored, 16)

        def pe_second(pe):
            arrive = lambda kc: pe.wait_ge(act_ready, 16 * layers + kc + 1)

            def panel2(k, arr=None):
                free2(pe, k)
                pe_used(pe, pe_panel(pe, M2, k, G2(k), act_hi, act_lo, arr))

            for k in range(6):
                panel2(k, arrive if k == 0 else None)
            for k in range(6, 9):
                free2(pe, k)
                pe.wait_ge(lo_done, 4 * M2 + k + 1)
                for tt in range(TT):
                    ts = slice(tt * P, (tt + 1) * P)
                    for kc in range(KC):
                        last = mm3(G2(k)[:, tt * T:(tt + 1) * T], act_hi[:, kc, ts], act_lo[:, kc, ts],
                                   w_hi[slot(k)][:, kc * 256:(kc + 1) * 256], w_lo[slot(k)][:, kc * 256:(kc + 1) * 256], kc == 0, kc == KC - 1)
                pe_used(pe, last)
            pe.wait_ge(lc2_ready, 16)
            for kc in range(KC):
                last = nc.tensor.matmul(bank[6][0:64, 0:T], lc2[:, L2_WDT + 64 * kc:L2_WDT + 64 * kc + 64], x[:, kc, :],
                                        start=kc == 0, stop=kc == KC - 1)
            last.then_inc(dt_mm, 1)
            scores2(pe, 0)
            scores2(pe, 1)
            for i in range(12):
                panel2(9 + i)
                if i == 0:
                    pe.wait_ge(dt_done, 1)
                    for tt in range(TT):
                        last = nc.tensor.transpose(bank[7][:, tt * 64:(tt + 1) * 64], dw[1][:, tt * P:(tt + 1) * P], ident[0:64, 0:64])
                    last.then_inc(dt_tr, 1)
                if i in ATT_SLOT:
                    u = ATT_SLOT[i]
                    pe.wait_ge(s2_p, u + 1)
                    if u:
                        pe.wait_ge(s2_ev0, u)
                        pe.wait_ge(s2_ev1, u)
                    else:
                        pe.wait_ge(dt_cols, 1)
                    if u in (4,):
                        pe.wait_ge(s2_lo, u // 4)
                    for n in range(6):
                        last = nc.tensor.transpose(bank[6 + n // 4][:, (n % 4) * P:(n % 4 + 1) * P], pp[u % 2][:, n * P:(n + 1) * P], ident)
                    last.then_inc(s2_tr, 1)
                    if u + 2 < 8:
                        pe.wait_ge(s2_nm, u + 1)
                        scores2(pe, u + 2)
                if i in PV_SLOT:
                    j = PV_SLOT[i]
                    pe.wait_ge(s2_ev0, 2 * j + 2)
                    pe.wait_ge(s2_ev1, 2 * j + 2)
                    o = bank[7][64 * (j % 2):64 * (j % 2) + 64, T:2 * T]
                    for n in range(6):
                        h = 4 * (n // 2) + j
                        last = nc.tensor.matmul(o, v2[:, n % 2, 64 * h:64 * h + 64], pt2[:, n, :], start=n == 0, stop=n == 5)
                    last.then_inc(s2_pv, 1)

            def prepare(g):
                if g == 0:
                    pe.wait_ge(s2_lo, 2)
                    pe.wait_ge(silu_done, 3)
                else:
                    pe.wait_ge(xt_done1, g)
                for st in range(TT):
                    last = nc.tensor.matmul(bank[7][:, st * T:(st + 1) * T], xb[:, 16 + g, st * P:(st + 1) * P], xb[:, 20 + g, :],
                                            start=True, stop=True)
                last.then_inc(cb_mm, 1)
                if g:
                    pe.wait_ge(xt_done0, g)
                for st in range(TT):
                    if st:
                        pe.wait_ge(cb_done, g + 1)
                    for b in range(4):
                        last = nc.tensor.transpose(bank[6 + st][:, b * P:(b + 1) * P], xb[:, 4 * g + b, st * P:(st + 1) * P], ident)
                    last.then_inc((xt_mm0, xt_mm1)[st], 1)

            prepare(0)
            for hu in range(8):
                g = hu // 2
                panel2(21 + hu)
                if hu % 2 and g < 3:
                    prepare(g + 1)
                if hu == 0 or hu % 2 == 0:
                    pe.wait_ge(xt_done0, g + 1)
                    pe.wait_ge(xt_done1, g + 1)
                if hu >= 4:
                    pe.wait_ge(y_out, hu - 3)
                for st in range(TT):
                    e = 2 * hu + st
                    pe.wait_ge(e_mul, e + 1)
                    for h in range(4):
                        o = bank[hu % 4][64 * (h % 2):64 * (h % 2) + 64, (h // 2) * T:(h // 2 + 1) * T]
                        w = xt[:, g % 2, st, 64 * (4 * (hu % 2) + h):64 * (4 * (hu % 2) + h) + 64]
                        last = nc.tensor.matmul(o, w, eb_far[e % 4][:, h, :], start=st == 0 and h < 2, stop=st == 1, skip_group_check=True)
                    last.then_inc(e_used, 1)
            for i in range(8):
                panel2(29 + i)
                if i % 2:
                    n = i // 2
                    pe.wait_ge(y_sq, n + 1)
                    if n:
                        pe.wait_ge(y_rs, n)
                    else:
                        pe.wait_ge(xt_done0, 4)
                    for b in range(4):
                        last = nc.tensor.matmul(bank[6][:, 0:T], ones, sq2[:, b, :], start=b == 0, stop=b == 3)
                    last.then_inc(y_ss, 1)
            free2(pe, 37)
            free2(pe, 38)
            pe.wait_ge(y_rs, 4)
            pe.wait_ge(xt_done1, 4)
            pe.wait_ge(s2_lo, 2)
            pe_used(pe, pe_panel_rows(pe, M2, 37, bank[4:8], lambda kk: ff_hi[:, 0, kk * T:(kk + 1) * T],
                                      lambda kk: ff_lo[:, 0, kk * T:(kk + 1) * T], True, True))
            pe.wait_ge(y_out, 8)
            for n in range(8):
                if n % 2 == 0:
                    pe.wait_ge(y_lo, n // 2 + 1)
                hi, lo = (mix_hi, mix_lo) if n < 4 else (act_hi, act_lo)
                c = 2 * n % 8
                pe_used(pe, pe_panel_rows(pe, M2, 38 + n, bank[0:4], lambda kk: hi[:, c + kk, :], lambda kk: lo[:, c + kk, :], n == 0, n == 7))
            pe.wait_ge(att_proj, 4)
            for n in range(4):
                if n == 2:
                    pe.wait_ge(x2_ready, 2)
                if n == 3:
                    pe.wait_ge(x2_ready, 4)
                pe_used(pe, pe_panel(pe, M2, 46 + n, bank[4 + n % 2], mix_hi, mix_lo,
                                     (lambda kc: pe.wait_ge(mx_lo, kc // 2 + 1)) if n == 0 else None))
            pe_layer_norm(pe, 0)
            pe_ff(pe, layers, M2, lambda kc: pe.wait_ge(ln_lo, kc + 1), 16 * layers, 50)
            pe_layer_norm(pe, 1)
            for c in range(4):
                for kc in (2 * c, 2 * c + 1):
                    pe.wait_ge(ln_x, 8 + kc + 1)
                    for tt in range(TT):
                        last = nc.tensor.transpose(bank[c][:, tt * T + (kc % 2) * P:tt * T + (kc % 2 + 1) * P], x[:, kc, tt * P:(tt + 1) * P], ident)
                last.then_inc(o_turned, 1)

        def scores2(pe, u):
            j, tt = u // 2, u % 2
            for p in range(3):
                b, r, _ = head2(p, j)
                o = bank[2 * (u % 2) + p // 2][:, (p % 2) * T:(p % 2 + 1) * T]
                last = nc.tensor.matmul(o, qk[r, b, tt * P:(tt + 1) * P], qk[r, 6 + b, :], start=True, stop=True)
            last.then_inc(s2_sc, 1)

        def pe_layer_norm(pe, q):
            for kc in range(KC):
                pe.wait_ge(x2_ready, 8 * q + kc + 1)
                last = nc.tensor.matmul(bank[6][:, 0:T], ones, x[:, kc, :], start=kc == 0, stop=kc == KC - 1)
            last.then_inc(ln_sum, 1)
            for kc in range(KC):
                pe.wait_ge(ln_sq, 8 * q + kc + 1)
                last = nc.tensor.matmul(bank[7][:, 0:T], ones, tb2[:, kc, :], start=kc == 0, stop=kc == KC - 1)
            last.then_inc(ln_ss, 1)

        def act_second(act):
            link = Chain(act, act_links, 0)
            link.base = layers * ACT_LINKS
            for kc in range(KC):
                act.wait_ge(x_ready, XR - 8 + kc + 1)
                nc.scalar.activation(act_hi[:, kc, :], x[:, kc, :], ACT.Copy).then_inc(act_his, 1)
            for k in (1, 2, 3):
                split_hi(act, M2, k)
            for k in range(9):
                used2(act, k)
                if k < 6:
                    if k == 0:
                        act.wait_ge(x_ready, XR)
                    nc.scalar.activation(qk[:, 2 * k:2 * k + 2, :], blocks2(G2(k)[:, :]), ACT.Copy, scale=0.125 if k < 3 else 1.0)\
                        .then_inc(gfree[k % 2], 1)
                split_hi(act, M2, k + 4)
            act.wait_ge(dt_mm, 1)
            nc.scalar.activation(dw[0], bank[6][0:64, 0:T], ACT.Identity, bias=lc2[0:64, L2_DTB:L2_DTB + 1]).then_inc(dt_y, 1)
            nc.scalar.activation(ea, lc2[0:64, L2_ALOG:L2_ALOG + 1], ACT.Exp).then_inc(alog_e, 1)
            act.wait_ge(dt_n, 1)
            nc.scalar.activation(dw[1], dw[1], ACT.Exp).then_inc(dt_e, 1)
            act.wait_ge(dt_pos, 1)
            nc.scalar.activation(dw[1], dw[0], ACT.Ln).then_inc(dt_ln, 1)

            def exp2(u):
                act.wait_ge(s2_nm, u + 1)
                nc.scalar.activation(pp[u % 2], pp[u % 2], ACT.Exp, bias=nm2[:, u % 2:u % 2 + 1], accum_out=dens2[:, u % 2:u % 2 + 1])\
                    .then_inc(s2_exp, 1)

            exp2(0)
            act.wait_ge(pads_ready, 1)
            for i in range(12):
                if i in ATT_SLOT and ATT_SLOT[i] + 1 < 8:
                    exp2(ATT_SLOT[i] + 1)
                used2(act, 9 + i)
                if i >= 2:
                    act.wait_ge(conv_done, i - 1)
                nc.scalar.activation(up[i % 2][:, :, 2:2 + T], blocks2(G2(9 + i)[:, :]), ACT.Copy).then_inc(gfree[(9 + i) % 2], 1)
                split_hi(act, M2, 13 + i)
                if i in ATT_SLOT:
                    u = ATT_SLOT[i]
                    act.wait_ge(s2_tr, u + 1)
                    if u % 2 == 0 and u:
                        act.wait_ge(s2_pv, u // 2)
                    nc.scalar.activation(pt2[:, 0:4, (u % 2) * P:(u % 2 + 1) * P], bank[6][:, :].rearrange("p (n t) -> p n t", n=4), ACT.Copy)\
                        .then_inc(s2_ev0, 1)
                if i in PV_SLOT and PV_SLOT[i] % 2:
                    b = PV_SLOT[i] // 2
                    act.wait_ge(s2_pv, 2 * b + 2)
                    nc.scalar.activation(ff_hi[:, 0, b * T:(b + 1) * T], bank[7][:, T:2 * T], ACT.Copy).then_inc(s2_hi, 1)
            act.wait_ge(conv_done, 12)
            for n in (2, 0, 1):
                nc.scalar.activation(xb[:, 8 * n:8 * n + 8, :], xb[:, 8 * n:8 * n + 8, :], ACT.Silu).then_inc(silu_done, 1)

            def copies(g):
                act.wait_ge(cb_mm, g + 1)
                nc.scalar.activation(cb[:, g % 2, :, :], blocks2(bank[7][:, :]), ACT.Copy).then_inc(cb_done, 1)
                act.wait_ge(xt_mm0, g + 1)
                nc.scalar.activation(xt[:, g % 2, 0, :], bank[6][:, :], ACT.Copy).then_inc(xt_done0, 1)
                act.wait_ge(xt_mm1, g + 1)
                nc.scalar.activation(xt[:, g % 2, 1, :], bank[7][:, :], ACT.Copy).then_inc(xt_done1, 1)

            act.wait_ge(s2_pv, 4)
            copies(0)

            def decay(e):
                act.wait_ge(e_mask, e + 1)
                hu, st = e // 2, e % 2
                for h in range(4):
                    far, near = [dtt[:, st, 32 * d + 4 * hu + h:32 * d + 4 * hu + h + 1] for d in (st, 1 - st)]
                    nc.scalar.activation(eb_far[e % 4][:, h, :], eb_far[e % 4][:, h, :], ACT.Exp, bias=far)
                    last = nc.scalar.activation(eb_near[e % 4][:, h, :], eb_near[e % 4][:, h, :], ACT.Exp, bias=near)
                last.then_inc(e_exp, 1)

            act.wait_ge(dt_cols, 1)
            decay(0)
            decay(1)
            for hu in range(8):
                used2(act, 21 + hu)
                nc.scalar.activation(zb[:, 2 * hu:2 * hu + 2, :], blocks2(G2(21 + hu)[:, :]), ACT.Copy).then_inc(gfree[(21 + hu) % 2], 1)
                if hu < 7:
                    decay(2 * hu + 2)
                split_hi(act, M2, 25 + hu)
                if hu % 2 and hu < 7:
                    if hu > 2:
                        act.wait_ge(e_used, 4 * (hu // 2))
                    copies(hu // 2 + 1)
                if hu < 7:
                    decay(2 * hu + 3)
            act.wait_ge(gfree[0], 7 * layers + 28 // 2 + 1 + 1)
            act.wait_ge(gfree[1], 7 * layers + 28 // 2 + 1)
            for n in range(2):
                nc.scalar.activation(zb[:, 8 * n:8 * n + 8, :], zb[:, 8 * n:8 * n + 8, :], ACT.Silu).then_inc(z_silu, 1)
            act.wait_ge(e_used, 16)
            for i in range(8):
                used2(act, 29 + i)
                for c in range(2):
                    b = 2 * i + c
                    last = nc.scalar.activation(gb[:, b, :], G2(29 + i)[:, c * T:(c + 1) * T], ACT.Identity, bias=lc2[:, L2_BG + b:L2_BG + b + 1])
                last.then_inc(gfree[(29 + i) % 2], 1)
                split_hi(act, M2, 33 + i)
                n = i // 2
                g = (2, 3, 0, 1)[n]
                if i % 2 == 0:
                    act.wait_ge(y_gated, n + 1)
                    if n:
                        act.wait_ge(y_ss, n)
                    nc.scalar.activation(sq2, xb[:, 4 * g:4 * g + 4, :], ACT.Square).then_inc(y_sq, 1)
                else:
                    act.wait_ge(y_ss, n + 1)
                    if n:
                        act.wait_ge(y_fin, n)
                    rsqrt(link, rs2, bank[6][:, 0:T], 1.0 / 512, cst[:, C_LEPS:C_LEPS + 1]).then_inc(y_rs, 1)
                    if n < 2:
                        act.wait_ge(y_fin, n + 1)
                        nc.scalar.activation(mix_hi[:, 4 * n:4 * n + 4, :], xb[:, 4 * g:4 * g + 4, :], ACT.Copy).then_inc(y_hi, 1)
            for n in (2, 3):
                act.wait_ge(y_fin, n + 1)
                nc.scalar.activation(act_hi[:, 4 * n - 8:4 * n - 4, :], xb[:, 4 * n - 8:4 * n - 4, :], ACT.Copy).then_inc(y_hi, 1)
            act.wait_ge(gfree[0], 7 * layers + 19 + 1)
            act.wait_ge(gfree[1], 7 * layers + 18 + 1)
            for n in (1, 0):
                nc.scalar.activation(gb[:, 8 * n:8 * n + 8, :], gb[:, 8 * n:8 * n + 8, :], ACT.Sigmoid).then_inc(gates_done, 1)
            for k in range(41, 50):
                split_hi(act, M2, k)
            for n in range(4):
                act.wait_ge(mx_sum, n + 1)
                nc.scalar.activation(mix_hi[:, 2 * n:2 * n + 2, :], mx[:, 2 * n:2 * n + 2, :], ACT.Copy).then_inc(mx_hi, 1)
            act_layer_norm(act, 0, link, L2_LN1B, (50, 51, 52))
            act_ff(act, layers, M2, 50, 16 * layers, final=True)
            act_layer_norm(act, 1, link, L2_LN2B, ())
            for c in range(4):
                if c % 2 == 0:
                    act.wait_ge(o_turned, c + 1)
                    nc.scalar.activation(obuf[:, :, c * T:(c + 1) * T], blocks2(bank[c][:, :]), ACT.Copy).then_inc(o_copied, 1)

        def act_layer_norm(act, q, link, bias, ks):
            act.wait_ge(ln_sum, q + 1)
            nc.scalar.activation(rs[:, :], bank[6][:, 0:T], ACT.Copy, scale=-1.0 / D).then_inc(ln_mean, 1)
            for kc in range(KC):
                act.wait_ge(ln_c, 8 * q + kc + 1)
                nc.scalar.activation(tb2[:, kc, :], x[:, kc, :], ACT.Square).then_inc(ln_sq, 1)
            for k in ks:
                split_hi(act, M2, k)
            act.wait_ge(ln_ss, q + 1)
            rsqrt(link, rs[:, :], bank[7][:, 0:T], 1.0 / D, cst[:, C_LEPS:C_LEPS + 1]).then_inc(ln_rs, 1)
            for kc in range(KC):
                act.wait_ge(ln_t, 8 * q + kc + 1)
                b = lc2[:, bias + kc:bias + kc + 1]
                if q == 0:
                    nc.scalar.activation(act_hi[:, kc, :], tb2[:, kc, :], ACT.Identity, bias=b).then_inc(ln_hi, 1)
                nc.scalar.activation(x[:, kc, :], tb2[:, kc, :], ACT.Identity, bias=b).then_inc(ln_x, 1)

        def dve_second(dve):
            link = Chain(dve, dve_links, 0)
            link.base = layers * DVE_LINKS
            for kc in range(KC):
                dve.wait_ge(act_his, 16 * layers + kc + 1)
                nc.vector.tensor_tensor(act_lo[:, kc, :], x[:, kc, :], act_hi[:, kc, :].bitcast(F32), ALU.subtract).then_inc(act_ready, 1)
            for k in (1, 2, 3):
                split_lo(dve, M2, k)
            for k in range(9):
                if k >= 6:
                    used2(dve, k)
                    nc.vector.tensor_copy(v2[:, :, (k - 6) * T:(k - 5) * T], blocks2(G2(k)[:, :])).then_inc(gfree[k % 2], 1)
                split_lo(dve, M2, k + 4)
            dve.wait_ge(dt_y, 1)
            link(nc.vector.scalar_tensor_tensor(dw[1], dw[0], -1.0, dw[0], ALU.mult, ALU.min))
            dve.sem_inc(dt_n, 1)
            dve.wait_ge(dt_e, 1)
            link(nc.vector.tensor_scalar(dw[2], dw[1], 2.0, None, ALU.add))
            link(nc.vector.reciprocal(dw[2], dw[2]))
            link(nc.vector.tensor_tensor(dw[3], dw[1], dw[2], ALU.mult))
            link(nc.vector.tensor_tensor(dw[4], dw[3], dw[3], ALU.mult))
            link(nc.vector.tensor_scalar(dw[2], dw[4], 1.0 / 15, None, ALU.mult))
            for c in (13, 11, 9, 7, 5, 3):
                link(nc.vector.scalar_tensor_tensor(dw[2], dw[2], 1.0 / c, dw[4], ALU.add, ALU.mult))
            link(nc.vector.scalar_tensor_tensor(dw[2], dw[2], 1.0, dw[3], ALU.add, ALU.mult))
            link(nc.vector.tensor_scalar(dw[0], dw[0], 0.0, None, ALU.max))
            link(nc.vector.scalar_tensor_tensor(dw[2], dw[2], 2.0, dw[0], ALU.mult, ALU.add))
            nc.vector.tensor_scalar(dw[0], dw[2], 1e-37, None, ALU.max).then_inc(dt_pos, 1)
            dve.wait_ge(alog_e, 1)
            link(nc.vector.tensor_scalar(dw[3], dw[2], ea, -1.0, ALU.mult, ALU.mult))
            link(nc.vector.tensor_tensor_scan(dw[4], cst[0:64, C_ONE:C_ONE + 1].to_broadcast([64, T]), dw[3], 0.0, ALU.mult, ALU.add))
            link(nc.vector.scalar_tensor_tensor(dw[4], dw[3], cst[0:64, C_NM:C_NM + 1], dw[4], ALU.mult, ALU.add))
            link(nc.vector.tensor_scalar(dw[5], dw[4], cst[0:64, C_SG:C_SG + 1], None, ALU.mult))
            dve.wait_ge(dt_ln, 1)
            nc.vector.tensor_tensor(dw[1], dw[1], dw[5], ALU.subtract).then_inc(dt_done, 1)
            dve.wait_ge(dist_ready, 16)

            def biased(u):
                j, tt = u // 2, u % 2
                dve.wait_ge(s2_sc, u + 1)
                if u >= 2:
                    dve.wait_ge(s2_tr, u - 1)
                for p in range(3):
                    _, _, h = head2(p, j)
                    ins = nc.vector.scalar_tensor_tensor(pp[u % 2][:, p * T:(p + 1) * T], dist[:, tt, p, :], -slope(h),
                                                         bank[2 * (u % 2) + p // 2][:, (p % 2) * T:(p % 2 + 1) * T], ALU.mult, ALU.add)
                link(ins)
                nc.vector.tensor_reduce(nm2[:, u % 2:u % 2 + 1], pp[u % 2], AX.X, ALU.max, negate=True).then_inc(s2_nm, 1)

            biased(0)
            for i in range(12):
                if i in ATT_SLOT:
                    u = ATT_SLOT[i]
                    if u + 1 < 8:
                        biased(u + 1)
                    dve.wait_ge(s2_exp, u + 1)
                    link(nc.vector.reciprocal(dens2[:, u % 2:u % 2 + 1], dens2[:, u % 2:u % 2 + 1]))
                    nc.vector.tensor_scalar(pp[u % 2], pp[u % 2], dens2[:, u % 2:u % 2 + 1], None, ALU.mult).then_inc(s2_p, 1)
                if i == 0:
                    dve.wait_ge(dt_tr, 1)
                    nc.vector.tensor_copy(dtt.rearrange("p t h -> p (t h)"), bank[7][:, 0:P]).then_inc(dt_cols, 1)
                dve.wait_ge(gfree[(9 + i) % 2], 7 * layers + (9 + i) // 2 + 2)
                for tap in range(5):
                    for c in range(2):
                        b = 2 * i + c
                        src, w = up[i % 2][:, c, tap:tap + T], lc2[:, L2_CW + 24 * tap + b:L2_CW + 24 * tap + b + 1]
                        if tap == 0:
                            ins = nc.vector.tensor_scalar(xb[:, b, :], src, w, lc2[:, L2_CB + b:L2_CB + b + 1], ALU.mult, ALU.add)
                        else:
                            dve.wait_ge(dve_links, link.base + link.n - 1)
                            ins = nc.vector.scalar_tensor_tensor(xb[:, b, :], src, w, xb[:, b, :], ALU.mult, ALU.add)
                        if tap < 4:
                            ins.then_inc(dve_links, 1)
                            link.n += 1
                        elif c == 1:
                            ins.then_inc(conv_done, 1)
                        else:
                            ins.then_inc(dve_links, 1)
                            link.n += 1
                split_lo(dve, M2, 13 + i)
                if i in ATT_SLOT:
                    u = ATT_SLOT[i]
                    dve.wait_ge(s2_tr, u + 1)
                    if u % 2 == 0 and u:
                        dve.wait_ge(s2_pv, u // 2)
                    nc.vector.tensor_copy(pt2[:, 4:6, (u % 2) * P:(u % 2 + 1) * P], bank[7][:, 0:T].rearrange("p (n t) -> p n t", n=2))\
                        .then_inc(s2_ev1, 1)
                if i in PV_SLOT and PV_SLOT[i] % 2:
                    b = PV_SLOT[i] // 2
                    dve.wait_ge(s2_hi, b + 1)
                    nc.vector.tensor_tensor(ff_lo[:, 0, b * T:(b + 1) * T], bank[7][:, T:2 * T], ff_hi[:, 0, b * T:(b + 1) * T].bitcast(F32),
                                            ALU.subtract).then_inc(s2_lo, 1)

            def mask(e):
                st = e % 2
                far, near = eb_far[e % 4][:, :, st * P:(st + 1) * P], eb_near[e % 4]
                dve.wait_ge(db_ready[e % 4], 32 * (e // 4 + 1))
                mf, mb = [cst[:, c:c + P].unsqueeze(1).to_broadcast([P, 4, P]) for c in (C_MF, C_MB)]
                m_far, m_near = (mf, mb) if st == 0 else (mb, mf)
                nc.vector.tensor_tensor(far, far, m_far, ALU.add)
                nc.vector.tensor_tensor(near, near, m_near, ALU.add).then_inc(e_mask, 1)

            def weigh2(e):
                st, g = e % 2, e // 4
                if e % 4 == 0:
                    dve.wait_ge(cb_done, g + 1)
                dve.wait_ge(e_exp, e + 1)
                own = eb_far[e % 4][:, :, st * P:(st + 1) * P]
                link(nc.vector.tensor_tensor(own, own, eb_near[e % 4], ALU.add))
                nc.vector.tensor_tensor(eb_far[e % 4], eb_far[e % 4], cb[:, g % 2, st, :].unsqueeze(1).to_broadcast([P, 4, T]), ALU.mult)\
                    .then_inc(e_mul, 1)

            def take_y(hu):
                dve.wait_ge(e_used, 2 * hu + 2)
                for c in range(2):
                    b = 2 * hu + c
                    last = nc.vector.scalar_tensor_tensor(xb[:, b, :], xb[:, b, :], lc2[:, L2_DS + b:L2_DS + b + 1],
                                                          bank[hu % 4][:, c * T:(c + 1) * T], ALU.mult, ALU.add)
                last.then_inc(y_out, 1)

            mask(0)
            mask(1)
            for hu in range(8):
                weigh2(2 * hu)
                if hu < 7:
                    mask(2 * hu + 2)
                weigh2(2 * hu + 1)
                if hu < 7:
                    mask(2 * hu + 3)
                if hu:
                    dve.wait_ge(xt_mm1, (hu - 1) // 2 + 1)
                    take_y(hu - 1)
                split_lo(dve, M2, 25 + hu)
            take_y(7)
            for n in range(4):
                g = (2, 3, 0, 1)[n]
                dve.wait_ge(z_silu, 2)
                dve.wait_ge(y_out, 8)
                nc.vector.tensor_tensor(xb[:, 4 * g:4 * g + 4, :], xb[:, 4 * g:4 * g + 4, :], zb[:, 4 * g:4 * g + 4, :], ALU.mult).then_inc(y_gated, 1)
                split_lo(dve, M2, 33 + 2 * n)
                dve.wait_ge(y_rs, n + 1)
                for b in range(4 * g, 4 * g + 4):
                    last = nc.vector.scalar_tensor_tensor(xb[:, b, :], xb[:, b, :], lc2[:, L2_SN + b:L2_SN + b + 1], rs2, ALU.mult, ALU.mult)
                last.then_inc(y_fin, 1)
                split_lo(dve, M2, 34 + 2 * n)
                if n < 2:
                    dve.wait_ge(y_hi, n + 1)
                    nc.vector.tensor_tensor(mix_lo[:, 4 * n:4 * n + 4, :], xb[:, 4 * g:4 * g + 4, :], mix_hi[:, 4 * n:4 * n + 4, :].bitcast(F32),
                                            ALU.subtract).then_inc(y_lo, 1)
            for n in (0, 1):
                dve.wait_ge(y_hi, n + 3)
                nc.vector.tensor_tensor(act_lo[:, 4 * n:4 * n + 4, :], xb[:, 4 * n:4 * n + 4, :], act_hi[:, 4 * n:4 * n + 4, :].bitcast(F32),
                                        ALU.subtract).then_inc(y_lo, 1)
            used2(dve, 37)
            dve.wait_ge(gates_done, 1)
            for n in range(4):
                nc.vector.tensor_tensor(m2[:, 2 * n:2 * n + 2, :], blocks2(bank[4 + n][:, :]), gb[:, 8 + 2 * n:10 + 2 * n, :], ALU.mult).then_inc(att_proj, 1)
            for k in range(41, 50):
                split_lo(dve, M2, k)
            used2(dve, 45)
            dve.wait_ge(gates_done, 2)
            for n in range(4):
                v = slice(2 * n, 2 * n + 2)
                link(nc.vector.tensor_tensor(mx[:, v, :], blocks2(bank[n][:, :]), gb[:, v, :], ALU.mult))
                nc.vector.tensor_tensor(mx[:, v, :], mx[:, v, :], m2[:, v, :], ALU.add).then_inc(mx_sum, 1)
                if n:
                    mixed2(dve, n - 1)
            mixed2(dve, 3)
            for n in range(4):
                used2(dve, 46 + n)
                for c in range(2):
                    kc = 2 * n + c
                    nc.vector.scalar_tensor_tensor(x[:, kc, :], x[:, kc, :], ALPHA, bank[4 + n % 2][:, c * T:(c + 1) * T], ALU.mult, ALU.add)\
                        .then_inc(x2_ready, 1)
            dve_layer_norm(dve, 0, L2_LN1G, L2_LN1B, (50, 51, 52))
            dve_ff(dve, M2, 50, 16 * layers, final=True)
            used2(dve, 81)
            for kc in range(KC):
                nc.vector.scalar_tensor_tensor(x[:, kc, :], x[:, kc, :], ALPHA, bank[kc // 2][:, (kc % 2) * T:(kc % 2 + 1) * T], ALU.mult, ALU.add)\
                    .then_inc(x2_ready, 1)
            dve_layer_norm(dve, 1, L2_LN2G, L2_LN2B, ())
            for c in range(4):
                if c % 2:
                    dve.wait_ge(o_turned, c + 1)
                    nc.vector.tensor_copy(obuf[:, :, c * T:(c + 1) * T], blocks2(bank[c][:, :])).then_inc(o_copied, 1)

        def mixed2(dve, n):
            v = slice(2 * n, 2 * n + 2)
            dve.wait_ge(mx_hi, n + 1)
            nc.vector.tensor_tensor(mix_lo[:, v, :], mx[:, v, :], mix_hi[:, v, :].bitcast(F32), ALU.subtract).then_inc(mx_lo, 1)

        def dve_layer_norm(dve, q, gain, bias, ks):
            dve.wait_ge(ln_mean, q + 1)
            for kc in range(KC):
                nc.vector.tensor_tensor(x[:, kc, :], x[:, kc, :], rs[:, :], ALU.add).then_inc(ln_c, 1)
            for k in ks:
                split_lo(dve, M2, k)
            dve.wait_ge(ln_rs, q + 1)
            for kc in range(KC + 1):
                if kc < KC:
                    nc.vector.scalar_tensor_tensor(tb2[:, kc, :], x[:, kc, :], lc2[:, gain + kc:gain + kc + 1], rs[:, :], ALU.mult, ALU.mult)\
                        .then_inc(ln_t, 1)
                if kc and q == 0:
                    c = kc - 1
                    dve.wait_ge(ln_hi, c + 1)
                    nc.vector.scalar_tensor_tensor(act_lo[:, c, :], tb2[:, c, :], lc2[:, bias + c:bias + c + 1], act_hi[:, c, :].bitcast(F32),
                                                   ALU.add, ALU.subtract).then_inc(ln_lo, 1)

        block = ctx.enter_context(nc.Block())

        @block.sync
        def _(sp):
            sp.dma_start(x_in, a["x"].rearrange("b (t p) d -> p (b t) d", p=P)).then_inc(x_loaded, 16)
            sp.dma_start(cst[:, :], a["cst"]).then_inc(cst_loaded, 16)
            for mp in range(8):
                load_mod(sp, 0, mp)
            for n in range(RAW):
                sp.dma_start(raw[:, n, :], a["panels"][n]).then_inc(raw_ready[n], 16)
            with sp.Fori(0, layers - 1) as l:
                sp_layer(sp, l, True)
            sp_layer(sp, layers - 1, False)
            finish(sp)

        @block.gpsimd
        def _(pool):
            link = Chain(pool, pool_links, 7)
            pool.dma_start(ccol[:, :], a["ccol"]).then_inc(c_loaded, 16)
            nc.gpsimd.memset(ub, 0.0)
            nc.gpsimd.memset(wb[0], 0.0)
            link(nc.gpsimd.memset(wb[1], 0.0))
            link.first = link.n
            with pool.Fori(0, layers) as l:
                link.layer(l)
                pool.wait_ge(x_ready, 16 * l + 8)
                pool.dma_start(lc[:, :], a["lcs"][l]).then_inc(lc_ready, 16)
                pool_rope(pool, l)
                pool_window(pool, l, link)
                link.end()
            pool_second(pool)

        @block.tensor
        def _(pe):
            pe.sem_inc(split_free, SPLIT)
            pe.sem_inc(mod_used, 2)
            pe.sem_inc(macc_free, 2)
            pe.sem_inc(gfree[0], 1)
            pe.sem_inc(gfree[1], 1)
            pe.sem_inc(ff_relu, 2)
            pe.sem_inc(ff_ready, 2)
            pe.wait_ge(x_loaded, 16)
            pe.wait_ge(cst_loaded, 16)
            for kc in range(KC):
                for tt in range(TT):
                    o = bank[kc // 2][:, (kc % 2) * T + tt * P:(kc % 2) * T + (tt + 1) * P]
                    last = nc.tensor.transpose(o, x_in[:, tt, kc * P:(kc + 1) * P], ident)
                last.then_inc(x_turned, 1)
            for n in range(4):
                pe_mod(pe, n, macc, MOD_AT + 48 + 4 * n)
            with pe.Fori(0, layers - 1) as l:
                pe_layer(pe, l, True)
            pe_layer(pe, layers - 1, False)
            pe_second(pe)

        @block.scalar
        def _(act):
            link = Chain(act, act_links, ACT_LINKS)
            act.wait_ge(cst_loaded, 16)
            nc.scalar.activation(idb[:, :], ident, ACT.Copy).then_inc(masks_ready, 1)
            nc.scalar.activation(causb[:, :], cst[:, C_CAUS:C_CAUS + P], ACT.Copy).then_inc(masks_ready, 1)
            nc.scalar.activation(cmpmb[:, :], cst[:, C_CMPM:C_CMPM + 32], ACT.Copy).then_inc(masks_ready, 1)
            act.wait_ge(c_loaded, 16)
            nc.scalar.activation(cact[:, :], ccol[:, 0:KC], ACT.Silu).then_inc(cact_ready, 1)
            split_hi(act, 0, 0)
            with act.Fori(0, layers - 1) as l:
                link.layer(l)
                act_layer(act, l, link, True)
                link.end()
            link.layer(layers - 1)
            act_layer(act, layers - 1, link, False)
            link.end()
            act_second(act)

        @block.vector
        def _(dve):
            link = Chain(dve, dve_links, DVE_LINKS)
            for kc in range(KC):
                dve.wait_ge(x_turned, kc // 2 * 2 + 2)
                nc.vector.tensor_copy(x[:, kc, :], bank[kc // 2][:, (kc % 2) * T:(kc % 2 + 1) * T]).then_inc(x_ready, 1)
            dve.wait_ge(c_loaded, 16)
            dve.wait_ge(cact_ready, 1)
            for pair in range(4):
                dve.wait_ge(macc_free, 2 * pair + 2)
                for half in range(2):
                    dve_mod(dve, pair, macc, half)
            dve_modc(dve, modc_ready, 1, 48, ccol[:, 2 * KC:2 * KC + 16], 3)
            nc.vector.scalar_tensor_tensor(gcol[:, 0:KC], modc[:, 8:16], 1.0, ccol[:, KC:2 * KC], ALU.add, ALU.mult).then_inc(gcol_ready, 1)
            dve.wait_ge(gcol_ready, 1)
            split_lo(dve, 0, 0)
            with dve.Fori(0, layers - 1) as l:
                link.layer(l)
                dve_layer(dve, l, link, True)
                link.end()
            link.layer(layers - 1)
            dve_layer(dve, layers - 1, link, False)
            link.end()
            dve_second(dve)


def col_panel(w, cols):
    return w[:, cols].reshape(KC, P, 256).transpose(1, 0, 2).reshape(P, PANEL)


def row_panel(w, j):
    return w[256 * j:256 * j + 256].reshape(2, P, D).transpose(1, 0, 2).reshape(P, PANEL)


def as_cols(v):
    return v.reshape(-1, P).T


def ff_panels(up, down):
    ups = [col_panel(up, slice(256 * j, 256 * j + 256)) for j in range(FF_STEPS)]
    downs = [row_panel(down, j) for j in range(FF_STEPS)]
    got = [ups[0]]
    for j in range(FF_STEPS - 1):
        got += [ups[j + 1], downs[j]]
    return got + [downs[-1]]


def lay_out(i):
    panels, lcs = [], []
    for l in range(DEPTH):
        w = i["w_in"][l]
        heads = [np.r_[512 + 64 * b:576 + 64 * b, 768 + 64 * b:832 + 64 * b] for b in range(4)]
        for cols in (slice(1024, 1280), slice(1280, 1536), slice(1536, 1792),
                     np.concatenate(heads[:2])):
            panels.append(col_panel(w, cols))
        panels.append(i["cmp_w1"][l].reshape(2, 16, 2, 64, 64).transpose(2, 3, 1, 0, 4).reshape(P, PANEL))
        panels += [col_panel(w, cols) for cols in (np.concatenate(heads[2:]), slice(0, 256), slice(256, 512))]
        rows = np.concatenate([np.arange(512), np.concatenate(heads)])
        panels += [col_panel(i["w_out"][l][rows], slice(256 * j, 256 * j + 256)) for j in range(4)]
        panels += ff_panels(i["w_ff1"][l], i["w_ff2"][l])
        following = (as_cols(i["b_mod"][l + 1])[:, :16], as_cols(i["norm1"][l + 1])) if l + 1 < DEPTH else (np.zeros((P, 24), np.float32),)
        twice = lambda v: np.concatenate([v, v])[:, None]
        lcs.append(np.concatenate([
            as_cols(i["b_mod"][l])[:, 16:], *following, as_cols(i["norm2"][l]), as_cols(i["pool_scale"][l]),
            twice(i["q_norm"][l]), *[twice(i["k_norm"][l, n]) for n in range(3)],
            i["cmp_pe"][l].reshape(2, 16, 2, 64).transpose(2, 3, 1, 0).reshape(P, 32),
            i["cmp_w2"][l].reshape(P, 64), i["pool_w"][l].transpose(1, 0, 2).reshape(P, 512),
            w[:, 1792:1816].reshape(KC, P, 24).transpose(1, 0, 2).reshape(P, 192)], axis=1))
    modw = np.stack([col_panel(i["w_mod"][l], slice(256 * j, 256 * j + 256)) for l in range(DEPTH) for j in range(MOD_PANELS)])
    w = i["w_in_2"]
    z, xbc, dt_f, _, q, k, v, gates = [int(n) for n in N_SPLITS[:-1]]
    cols = [n + 256 * j for n, count in ((q, 3), (k, 3), (v, 3), (xbc, 12), (z, 8), (gates, 8)) for j in range(count)]
    panels += [col_panel(w, slice(c, c + 256)) for c in cols]
    panels.append(row_panel(i["w_proj_attn_2"], 0))
    panels += [row_panel(i["w_proj_ssd_2"], j) for j in (4, 5, 6, 7, 0, 1, 2, 3)]
    panels += [col_panel(i["w_out_2"], slice(256 * j, 256 * j + 256)) for j in range(4)]
    panels += ff_panels(i["w_up_2"], i["w_down_2"])
    in_rows = lambda *v: np.concatenate([*v, np.zeros(P - 2 * N_HEADS, np.float32)])[:, None]
    lc2 = np.concatenate([
        w[:, dt_f:dt_f + 64].reshape(KC, P, 64).transpose(1, 0, 2).reshape(P, 512),
        in_rows(i["dt_bias_f_2"], i["dt_bias_b_2"]), in_rows(i["a_log_f_2"], i["a_log_b_2"]),
        *[as_cols(i["conv_w_2"][tap]) for tap in range(D_CONV)], as_cols(i["conv_b_2"]),
        as_cols(np.repeat(i["d_skip_2"], 64)), as_cols(i["ssd_norm_w_2"]), as_cols(i["b_gate_2"]),
        as_cols(i["ln1_g_2"]), as_cols(i["ln1_b_2"]), as_cols(i["ln2_g_2"]), as_cols(i["ln2_b_2"])], axis=1)
    first = np.concatenate([as_cols(i["c"][0]), as_cols(i["norm1"][0]), as_cols(i["b_mod"][0])[:, :16]], axis=1)
    return dict(x=i["x"], ccol=first, cst=constants(), lcs=np.stack(lcs), modw=modw, panels=np.stack(panels),
                lc2=lc2, dist=distances())


SETTINGS = dict(target_bir_lowering=False, num_devices=1, dynamic_dma_scratch_size=4096)


def kernel(**inputs):
    import numpy as _np
    import concourse.bacc as _bacc
    from concourse import mybir as _mybir
    from concourse.bass_utils import run_bass_kernel_spmd as _run

    laid_out = lay_out({name: _np.asarray(v) for name, v in inputs.items()})
    nc = _bacc.Bacc("TRN2", **SETTINGS)
    arrays, views = {}, {}
    for name, v in laid_out.items():
        arrays[f"in_{name}"] = _np.ascontiguousarray(v)
        views[name] = nc.dram_tensor(f"in_{name}", v.shape, _mybir.dt.float32, kind="ExternalInput").ap()
    out = nc.dram_tensor("out", (1, T, D), _mybir.dt.float32, kind="ExternalOutput").ap()
    build(nc, views, out)
    return _run(nc, [arrays], core_ids=[0]).results[0]["out"]
```

```python
from contextlib import ExitStack

import numpy as np
import concourse.bass as bass
from concourse import mybir

F32 = mybir.dt.float32
F32R = mybir.dt.float32r
BF16 = mybir.dt.bfloat16
ALU = mybir.AluOpType
ACT = mybir.ActivationFunctionType
AX = mybir.AxisListType

P = 128
T = 256
TT = T // P
D = 1024
KC = D // P
DEPTH = 2
EPS = 1e-6
LN_EPS = 1e-5
NEG = -1e30

PANEL = KC * 256
RAW = 2
SPLIT = 4
L_K0K1, L_K2V0, L_V1V2, L_Q0, L_CMP, L_Q1, L_U0, L_U1, L_OUT, L_FF = 0, 1, 2, 3, 4, 5, 6, 7, 8, 12
L_PANELS = 44
FF_STEPS = 16
MOD_PANELS = 24

LC_BM, LC_BA, LC_NA, LC_N2, LC_PS, LC_QN, LC_KN, LC_PE, LC_W2, LC_PW, LC_GW, LC = 0, 32, 48, 56, 64, 68, 69, 72, 104, 168, 680, 872

C_ID, C_BD, C_ROT, C_ONE, C_COS, C_SIN, C_CCOS, C_CSIN, C_CAUS, C_CMPM, C_VALID, C_EPS, C_LEPS, C_MF, C_MB, C_SG, C_NM, C_RC, CN = (
    0, 128, 256, 384, 512, 768, 1024, 1040, 1056, 1184, 1216, 1217, 1218, 1219, 1347, 1475, 1476, 1477, 2501)
N_CMP = (T - 32) // 16 + 1


D_INNER, N_HEADS, CONV_DIM, D_CONV = 2048, 32, 3072, 5
N_SPLITS = np.cumsum([0, D_INNER, CONV_DIM, N_HEADS, N_HEADS, 768, 768, 768, 2 * D])
L2_WDT, L2_DTB, L2_ALOG, L2_CW, L2_CB, L2_DS, L2_SN, L2_BG, L2_LN1G, L2_LN1B, L2_LN2G, L2_LN2B, LC2 = (
    0, 512, 513, 514, 634, 658, 674, 690, 706, 714, 722, 730, 738)
FAR = 1e30


def distances():
    t = np.arange(T).reshape(TT, P).T[:, :, None, None]
    s = np.arange(T)[None, None, None, :]
    dil = np.array((1, 4, 16))[None, None, :, None]
    dd = np.abs(t - s)
    return np.where((dd % dil == 0) & (dd <= 64 * dil), dd, FAR).astype(np.float32).reshape(P, TT * 3 * T)


def constants():
    c = np.zeros((P, CN), np.float32)
    p = np.arange(P)[:, None]
    f = np.arange(P)[None, :]
    c[:, C_ID:C_ID + P] = p == f
    c[:, C_BD:C_BD + P] = p // 64 == f // 64
    c[:, C_ROT:C_ROT + P] = np.where((f % 64 < 32) & (p == f + 32), -1.0, np.where((f % 64 >= 32) & (p == f - 32), 1.0, 0.0))
    c[:, C_ONE:C_ONE + P] = 1.0
    inv = np.float32(10000.0) ** (-(np.arange(32, dtype=np.float32)) * np.float32(2.0) / np.float32(64))
    inv = np.tile(inv.astype(np.float32), 4)[:, None]
    ang = (np.arange(T, dtype=np.float32)[None, :] * inv).astype(np.float32)
    c[:, C_COS:C_COS + T], c[:, C_SIN:C_SIN + T] = np.cos(ang), np.sin(ang)
    end = np.arange(N_CMP) * 16 + 31
    ang = (end.astype(np.float32)[None, :] * inv).astype(np.float32)
    c[:, C_CCOS:C_CCOS + N_CMP], c[:, C_CSIN:C_CSIN + N_CMP] = np.cos(ang), np.sin(ang)
    c[:, C_CAUS:C_CAUS + P] = np.where(f > p, NEG, 0.0)
    for tt in range(TT):
        c[:, C_CMPM + 16 * tt:C_CMPM + 16 * tt + N_CMP] = np.where(end[None, :] > p + P * tt, NEG, 0.0)
    c[:, C_VALID] = np.arange(P) >= 31
    c[:, C_EPS] = EPS
    c[:, C_LEPS] = LN_EPS
    c[:, C_MF:C_MF + P] = np.where(p > f, NEG, 0.0)
    c[:, C_MB:C_MB + P] = np.where(f > p, NEG, 0.0)
    c[:, C_SG] = np.where(np.arange(P) % 64 < 32, 1.0, -1.0)
    c[:, C_NM] = np.where(np.arange(P) % 64 < 32, 0.0, -1.0)
    for g, w in enumerate((2, 4, 8, 16)):
        c[:, C_RC + g * T:C_RC + (g + 1) * T] = 1.0 / np.minimum(np.arange(T) + 1, w)
    return c


def build(nc, a, out, layers=DEPTH):
    ctx = ExitStack()

    def sb(name, shape, dt=F32):
        return ctx.enter_context(nc.sbuf_tensor(name, shape, dt))

    def sem(name):
        return ctx.enter_context(nc.semaphore(name))

    with ctx:
        raw = sb("raw", [P, RAW, PANEL])
        w_hi = [sb(f"w_hi{i}", [P, PANEL], F32R) for i in range(SPLIT)]
        w_lo = [sb(f"w_lo{i}", [P, PANEL], F32R) for i in range(SPLIT)]
        x = sb("x", [P, KC, T])
        act_hi, act_lo = sb("act_hi", [P, KC, T], F32R), sb("act_lo", [P, KC, T], F32R)
        with nc.sbuf_tensor("mixf", [P, 2 * KC * T], F32) as mixf:
            pass
        mix_hi, mix_lo = sb("mix_hi", [P, KC, T], F32R), sb("mix_lo", [P, KC, T], F32R)
        ff_hi, ff_lo = sb("ff_hi", [P, 2, 2 * T], F32R), sb("ff_lo", [P, 2, 2 * T], F32R)
        cst = sb("cst", [P, CN])
        lc = sb("lc", [P, LC])
        idb = sb("idb", [P, P], BF16)
        causb = sb("causb", [P, P], BF16)
        cmpmb = sb("cmpmb", [P, 32], BF16)
        ccol = sb("ccol", [P, 2 * KC + 16])
        cact = sb("cact", [P, KC])
        modc = sb("modc", [P, 48])
        macc = sb("macc", [P, 2, 256])
        gcol = sb("gcol", [P, 2 * KC])
        rs = sb("rs", [P, T])
        small = sb("small", [P, 160])
        ARENA = 17920
        arena = sb("arena", [P, ARENA])
        at = [0]

        def area(n, *dims):
            v = arena[:, at[0]:at[0] + n]
            at[0] += n
            assert at[0] <= ARENA, at[0]
            if len(dims) == 2:
                v = v.rearrange("p (a b) -> p a b", a=dims[0])
            if len(dims) == 3:
                v = v.rearrange("p (a b c) -> p a b c", a=dims[0], b=dims[1])
            return v

        bank = [ctx.enter_context(nc.psum_tensor(f"bank{i}", [P, 512], F32)) for i in range(8)]

        def win(ap, start, n_part, dims, col=0):
            full = ap[start:start + n_part, col:col + 1]
            return bass.AP(full.tensor, full.offset, [[full.ap[0][0], n_part], *dims])

        x_loaded, cst_loaded, c_loaded = sem("x_loaded"), sem("cst_loaded"), sem("c_loaded")
        masks_ready = sem("masks_ready")
        cact_ready = sem("cact_ready")
        gcol_ready = sem("gcol_ready")
        x_turned = sem("x_turned")
        x_ready = sem("x_ready")
        lc_ready = sem("lc_ready")
        sq_done = sem("sq_done")
        ss_done = sem("ss_done")
        rs_done = sem("rs_done")
        t_done = sem("t_done")
        act_his = sem("act_his")
        act_ready = sem("act_ready")
        raw_ready = [sem(f"raw_ready{i}") for i in range(RAW)]
        hi_done = sem("hi_done")
        lo_done = sem("lo_done")
        split_free = sem("split_free")
        modraw = [sem(f"modraw{i}") for i in range(2)]
        modraw_x = [sem(f"modraw_x{i}") for i in range(2)]
        mod_used = sem("mod_used")
        macc_free = sem("macc_free")
        mod_links = sem("mod_links")
        modc_ready = sem("modc_ready")
        gfull = sem("gfull")
        gfree = [sem(f"gfree{i}") for i in range(2)]
        nr_sq = sem("nr_sq")
        nr_mm = sem("nr_mm")
        nr_rs = sem("nr_rs")
        nr_yc = sem("nr_yc")
        nr_out = sem("nr_out")
        tb_k, tb_v, tb_pe, tb_hi, tb_lo = sem("tb_k"), sem("tb_v"), sem("tb_pe"), sem("tb_hi"), sem("tb_lo")
        cmp_h, cmp_e, cmp_s, cmp_w2, cmp_y = sem("cmp_h"), sem("cmp_e"), sem("cmp_s"), sem("cmp_w2"), sem("cmp_y")
        gw_hi, gw_lo = sem("gw_hi"), sem("gw_lo")
        u_copied = sem("u_copied")
        pooled_ready = sem("pooled_ready")
        at_sc = sem("at_sc")
        at_nm = sem("at_nm")
        at_exp = sem("at_exp")
        at_p = sem("at_p")
        at_tr = sem("at_tr")
        at_ev0, at_ev1 = sem("at_ev0"), sem("at_ev1")
        at_pv = sem("at_pv")
        mix_his = sem("mix_his")
        out_done = sem("out_done")
        ff_full = sem("ff_full")
        ff_relu = sem("ff_relu")
        ff_sq = sem("ff_sq")
        ff_his = sem("ff_his")
        ff_ready = sem("ff_ready")
        rows_done = sem("rows_done")
        dve_links, act_links, pool_links = sem("dve_links"), sem("act_links"), sem("pool_links")
        out_written = sem("out_written")

        class Chain:

            def __init__(self, eng, s, per_layer):
                self.eng, self.s, self.per, self.base, self.n, self.first = eng, s, per_layer, 0, 0, 0

            def __call__(self, ins):
                ins.then_inc(self.s, 1)
                self.n += 1
                self.eng.wait_ge(self.s, self.base + self.n)

            def layer(self, l):
                self.base, self.n = l * self.per + self.first, 0

            def end(self):
                assert self.n == self.per, (self.eng, self.n)

        at[0] = 0
        modw = area(2 * PANEL, 2, PANEL)
        mod_sums = arena[:, at[0]:at[0] + 12 * 256].rearrange("p (n c) -> p n c", n=12)
        tbuf = area(KC * T, KC, T)
        ybuf = [area(2 * T, 2, T) for _ in range(3)]
        first_sums = arena[:, at[0] - 6 * T:at[0]].rearrange("p (n c) -> p n c", n=6)
        q_at = at[0]
        qr = area(4 * T, 4, T)
        kr = area(2 * T, 2, T)
        vt = area(TT * T, TT, T)
        tb = area(960, 16, 60)
        pbuf = [area(800) for _ in range(2)]
        pts = [area(1024) for _ in range(2)]
        fr = [v[:, 0:2 * T] for v in pts]
        modw_x = arena[:, q_at + TT * D:q_at + TT * D + 2 * PANEL].rearrange("p (b n) -> p b n", b=2)
        assert q_at + TT * D + 2 * PANEL <= at[0]
        ub = area(4 * (T + 16), 4, T + 16)
        wb = [area(4 * (T + 16), 4, T + 16) for _ in range(2)]
        tbh, tbl = [v[:, :, :].rearrange("p a b -> p (a b)")[:, 0:960].rearrange("p (j n) -> p j n", j=16) for v in (ff_hi, ff_lo)]
        gwh, gwl = sb("gwh", [P, KC, 24], F32R), sb("gwl", [P, KC, 24], F32R)
        kcmp = small[:, 0:15]
        vcmp = sb("vcmp", [16, P])
        hs = small[:, 16:76]
        ce = small[:, 76:136]
        ycmp = small[:, 136:151]
        gts = sb("gts", [P, TT, 24])
        sqc = sb("sqc", [P, 48])
        ln_out = sb("ln_out", [P, 1])
        dens = sb("dens", [P, 2, 6])
        nm = sb("nm", [P, 2, 6])
        fac = sb("fac", [P, 2, 6])

        ident = cst[:, C_ID:C_ID + P]
        ones = cst[:, C_ONE:C_ONE + P]
        x_in = arena[:, q_at:q_at + TT * D].rearrange("p (t d) -> p t d", t=TT)


        def slot(k):
            return k % SPLIT

        n_panels = a["panels"].shape[0]

        def load(sp, m, k):
            sp.wait_ge(lo_done, 4 * m + k - RAW + 1)
            sp.dma_start(raw[:, k % RAW, :], a["panels"][4 * m + k]).then_inc(raw_ready[k % RAW], 16)

        def load_mod(sp, l, u):
            sp.wait_ge(mod_used, MOD_PANELS * l + u + 1)
            sp.dma_start(modw[:, u % 2, :], a["modw"][MOD_PANELS * l + u]).then_inc(modraw[u % 2], 16)

        def sp_layer(sp, l, ahead):
            m = 11 * l
            for k in range(2, 8):
                load(sp, m, k)
            load_mod(sp, l, 8)
            load_mod(sp, l, 9)
            for k in range(8, 13):
                load(sp, m, k)
            load_mod(sp, l, 10)
            load_mod(sp, l, 11)
            load(sp, m, 13)
            for mp in range(12, 18):
                load_mod(sp, l, mp)
            load(sp, m, 14)
            for mp in (18, 19):
                load_mod(sp, l, mp)
            load(sp, m, 15)
            if not ahead:
                load_mod(sp, l, 20)
                load_mod(sp, l, 21)
            for k in (16, 17, 18):
                load(sp, m, k)
            with sp.Fori(1, FF_STEPS // 2 - 1) as i:
                load(sp, m + i, 15)
                if ahead:
                    for mp in range(2):
                        sp.wait_ge(mod_used, MOD_PANELS * l + 18 + 2 * i + mp + 1)
                        sp.dma_start(modw[:, mp, :], a["modw"][MOD_PANELS * l + 18 + 2 * i + mp]).then_inc(modraw[mp], 16)
                for k in (16, 17, 18):
                    load(sp, m + i, k)
            e = m + FF_STEPS // 2 - 1
            load(sp, e, 15)
            if not ahead:
                load_mod(sp, l, 22)
                load_mod(sp, l, 23)
            load(sp, e, 16)
            load(sp, e, 17)

        def split_hi(act, m, k):
            act.wait_ge(raw_ready[k % RAW], 16 * (2 * m + k // 2 + 1))
            act.wait_ge(split_free, 4 * m + k + 1)
            nc.scalar.activation(w_hi[slot(k)][:, :], raw[:, k % RAW, :], ACT.Copy).then_inc(hi_done, 1)

        def split_lo(dve, m, k):
            dve.wait_ge(hi_done, 4 * m + k + 1)
            nc.vector.tensor_tensor(w_lo[slot(k)][:, :], raw[:, k % RAW, :], w_hi[slot(k)][:, :].bitcast(F32),
                                    ALU.subtract).then_inc(lo_done, 1)

        def mm3(o, wh, wl, xh, xl, start, stop, skip=False):
            nc.tensor.matmul(o, wh, xh, start=start, stop=False, skip_group_check=skip)
            nc.tensor.matmul(o, wh, xl, start=False, stop=False, skip_group_check=skip)
            return nc.tensor.matmul(o, wl, xh, start=False, stop=stop, skip_group_check=skip)

        def pool_rope(pool, l):
            for j in range(3):
                pool.wait_ge(nr_mm, 4 * l + j + 1)
                y = ybuf[j]
                nc.gpsimd.tensor_tensor(y, y, cst[:, C_COS:C_COS + T].unsqueeze(1).to_broadcast([P, 2, T]), ALU.mult).then_inc(nr_yc, 1)

        def pool_window(pool, l, link):
            pool.wait_ge(u_copied, 2 * l + 2)
            b, c = wb

            def cols(t, g0, off=0, step=1):
                return t[:, g0:4:step, 16 - off:16 - off + T]

            link(nc.gpsimd.tensor_tensor(cols(b, 0), cols(ub, 0), cols(ub, 0, 1), ALU.add))
            link(nc.gpsimd.tensor_tensor(cols(c, 1), cols(b, 1), cols(b, 1, 2), ALU.add))
            link(nc.gpsimd.tensor_tensor(cols(b, 2), cols(c, 2), cols(c, 2, 4), ALU.add))
            link(nc.gpsimd.tensor_tensor(cols(c, 3), cols(b, 3), cols(b, 3, 8), ALU.add))
            rc = cst[:, C_RC:C_RC + 4 * T].rearrange("p (g t) -> p g t", g=4)
            for t, g0 in ((b, 0), (c, 1)):
                link(nc.gpsimd.tensor_tensor(cols(t, g0, 0, 2), cols(t, g0, 0, 2), rc[:, g0:4:2, :], ALU.mult))
                last = nc.gpsimd.tensor_tensor(cols(t, g0, 0, 2), cols(t, g0, 0, 2), cols(ub, g0, 0, 2), ALU.subtract)
                if g0 == 0:
                    link(last)
            last.then_inc(pooled_ready, 1)


        def pe_gfree(pe, l, g):
            pe.wait_ge(gfree[g % 2], 7 * l + g // 2 + 1)

        def pe_panel(pe, m, k, o, xh, xl, arrive=None):
            pe.wait_ge(lo_done, 4 * m + k + 1)
            wh, wl = w_hi[slot(k)], w_lo[slot(k)]
            for c in range(2):
                for kc in range(KC):
                    if c == 0 and arrive:
                        arrive(kc)
                    s = kc * 256 + c * P
                    last = mm3(o[:, c * T:(c + 1) * T], wh[:, s:s + P], wl[:, s:s + P], xh[:, kc, :], xl[:, kc, :],
                               kc == 0, kc == KC - 1)
            return last

        def pe_panel_rows(pe, m, k, o, xh, xl, first, last_panel, parts=False):
            pe.wait_ge(lo_done, 4 * m + k + 1)
            wh, wl = w_hi[slot(k)], w_lo[slot(k)]
            for n in range(16):
                c, kk = (n // 2, n % 2) if parts else (n % 8, n // 8)
                s = kk * D + c * P
                last = mm3(o[c // 2][:, (c % 2) * T:(c % 2 + 1) * T], wh[:, s:s + P], wl[:, s:s + P], xh(kk), xl(kk),
                           first and kk == 0 and c % 2 == 0, last_panel and kk == 1, skip=True)
                if parts and n in (3, 7, 11):
                    last.then_inc(rows_done, 1)
            return last

        def pe_used(pe, last):
            last.then_inc(split_free, 1)

        MOD_AT = 440

        def pe_mod(pe, pair, src, col):
            pe.wait_ge(mod_used, 2 + 2 * pair + 2)
            for n in range(2):
                for c in range(2):
                    last = nc.tensor.matmul(bank[7][:, bass.ds(col + 2 * n + c, 1)], src[:, n, c * P:(c + 1) * P], ones[:, 0:1],
                                            start=True, stop=True)
            last.then_inc(macc_free, 2)

        def pe_norm_sum(pe, q):
            for kc in range(KC):
                pe.wait_ge(sq_done, KC * q + kc + 1)
                last = nc.tensor.matmul(bank[6][:, 0:T], ones, tbuf[:, kc, :], start=kc == 0, stop=kc == KC - 1)
            last.then_inc(ss_done, 1)

        def pe_layer(pe, l, ahead):
            m = 11 * l

            def arrive(kc):
                pe.wait_ge(act_ready, 16 * l + kc + 1)

            def turn(j):
                if j == 0:
                    pe.wait_ge(nr_sq, 5 * l + 2)
                    pe.wait_ge(gfree[0], 7 * l + 2)
                    pe.wait_ge(gfree[1], 7 * l + 2)
                else:
                    pe.wait_ge(nr_sq, 5 * l + 2 + j)
                    pe.wait_ge(gfree[(j + 1) % 2], 7 * l + 4)
                if j == 2:
                    pe.wait_ge(nr_out, 4 * l + 2)
                o = (0, 2, 2)[j]
                nc.tensor.matmul(bank[o][:, :], cst[:, C_BD:C_BD + P], tbuf[:, 2 * j:2 * j + 2, :], start=True, stop=True)
                nc.tensor.matmul(bank[o + 1][:, :], cst[:, C_ROT:C_ROT + P], ybuf[j], start=True, stop=True).then_inc(nr_mm, 1)

            G = lambda g: bank[4 + g % 2]
            for g, k in ((0, L_K0K1), (1, L_K2V0)):
                pe_gfree(pe, l, g)
                pe_used(pe, pe_panel(pe, m, k, G(g), act_hi, act_lo, arrive if g == 0 else None))
            pe_gfree(pe, l, 2)
            pe.wait_ge(lo_done, 4 * m + L_V1V2 + 1)
            wh, wl = w_hi[slot(L_V1V2)], w_lo[slot(L_V1V2)]
            for tt in range(TT):
                for kc in range(KC):
                    ts = slice(tt * P, (tt + 1) * P)
                    last = mm3(G(2)[:, tt * T:(tt + 1) * T], act_hi[:, kc, ts], act_lo[:, kc, ts],
                               wh[:, kc * 256:(kc + 1) * 256], wl[:, kc * 256:(kc + 1) * 256], kc == 0, kc == KC - 1)
            pe_used(pe, last)
            pe_gfree(pe, l, 3)
            pe.wait_ge(lc_ready, 16 * l + 16)
            pe.wait_ge(gw_lo, l + 1)
            for tt in range(TT):
                for kc in range(KC):
                    ts = slice(tt * P, (tt + 1) * P)
                    last = mm3(G(3)[:, tt * 24:(tt + 1) * 24], act_hi[:, kc, ts], act_lo[:, kc, ts], gwh[:, kc, :], gwl[:, kc, :],
                               kc == 0, kc == KC - 1)
            last.then_inc(gfull, 1)
            pe_gfree(pe, l, 4)
            pe_used(pe, pe_panel(pe, m, L_Q0, G(4), act_hi, act_lo))
            turn(0)
            pe.wait_ge(tb_lo, l + 1)
            pe.wait_ge(lo_done, 4 * m + L_CMP + 1)
            for jj in range(16):
                s = slice(jj * P, (jj + 1) * P)
                last = mm3(bank[6][:, 0:60], w_hi[slot(L_CMP)][:, s], w_lo[slot(L_CMP)][:, s], tbh[:, jj, :], tbl[:, jj, :],
                           jj == 0, jj == 15)
            pe_used(pe, last)
            turn(1)
            pe_gfree(pe, l, 5)
            pe_used(pe, pe_panel(pe, m, L_Q1, G(5), act_hi, act_lo, lambda kc: pe.wait_ge(cmp_s, l + 1) if kc == KC - 1 else None))
            w2 = lc[:, LC_W2:LC_W2 + 64]
            nc.tensor.matmul(bank[6][0:64, 64:79], w2[0:64, :], hs[0:64, 0:15], start=True, stop=True)
            nc.tensor.matmul(bank[6][64:128, 64:79], w2[0:64, :], hs[0:64, 15:30], start=True, stop=True)
            for v in range(2):
                last = nc.tensor.matmul(bank[6][0:15, 128 + 64 * v:192 + 64 * v], hs[64:128, 30 + 15 * v:45 + 15 * v],
                                        w2[64:128, :], start=True, stop=True)
            last.then_inc(cmp_w2, 1)
            pe_gfree(pe, l, 6)
            pe_used(pe, pe_panel(pe, m, L_U0, G(6), act_hi, act_lo))
            turn(2)
            pe.wait_ge(nr_sq, 5 * l + 5)
            pe.wait_ge(cmp_y, l + 1)
            nc.tensor.matmul(bank[6][:, 256:271], cst[:, C_BD:C_BD + P], sqc[:, 0:15], start=True, stop=True)
            nc.tensor.matmul(bank[6][:, 288:303], cst[:, C_ROT:C_ROT + P], ycmp, start=True, stop=True).then_inc(nr_mm, 1)
            pe.wait_ge(nr_out, 4 * l + 2)
            pe.wait_ge(masks_ready, 3)
            pe_scores(pe, l, 0, False)
            pe.wait_ge(nr_out, 4 * l + 3)
            pe_scores(pe, l, 1, False)
            pe.wait_ge(nr_out, 4 * l + 4)
            pe_scores(pe, l, 0, True)
            pe_scores(pe, l, 1, True)
            pe_gfree(pe, l, 7)
            pe_used(pe, pe_panel(pe, m, L_U1, G(7), act_hi, act_lo))
            pe.wait_ge(modc_ready, 3 * l + 1)
            for i in range(8):
                pe_turn(pe, l, i)
                if i + 2 < 8:
                    pe.wait_ge(at_exp, 8 * l + i + 1)
                    pe_scores(pe, l, i + 2, False)
                    pe_scores(pe, l, i + 2, True)
                pe_pv(pe, l, i)
            for n in range(4):
                pe_mod(pe, 12 * l + 4 + n, mod_sums[:, 2 * n:2 * n + 2, :], MOD_AT + 16 + 4 * n)
            pe.wait_ge(pooled_ready, l + 1)
            for g in range(4):
                if g % 2 == 0:
                    pe_gfree(pe, l, 12 + g // 2)
                src = wb[g % 2]
                last = nc.tensor.matmul(bank[4 + g // 2][:, (g % 2) * T:(g % 2 + 1) * T], lc[:, LC_PW + g * P:LC_PW + (g + 1) * P],
                                        src[:, g, 16:16 + T], start=True, stop=True)
                if g % 2:
                    last.then_inc(gfull, 1)
            for i in range(4):
                if i < 2:
                    pe.wait_ge(gfree[i], 7 * l + 8)
                    pe.wait_ge(gfree[1 - i], 7 * l + 8)
                else:
                    pe.wait_ge(x_ready, 16 * l + 8 + 2 * (i - 2) + 2)
                last = pe_panel(pe, m, L_OUT + i, bank[4 + i % 2], mix_hi, mix_lo)
                pe_used(pe, last)
            pe_norm_sum(pe, 2 * l + 1)
            pe.wait_ge(modc_ready, 3 * l + 2)
            for n in (4, 5):
                pe_mod(pe, 12 * l + 4 + n, mod_sums[:, 2 * n:2 * n + 2, :], MOD_AT + 16 + 4 * n)
            pe.wait_ge(modc_ready, 3 * l + 3)
            pe_ff(pe, l, m, lambda kc: pe.wait_ge(act_ready, 16 * l + KC + kc + 1), 16 * l, L_FF, "ahead" if ahead else "tail")
            if ahead:
                pe_norm_sum(pe, 2 * l + 2)

        def pe_ff(pe, l, m, arrive, j0, k0, mods=None):
            def up(mm, k, jn, par, arr=None):
                pe.wait_ge(ff_relu, jn + 1)
                last = pe_panel(pe, mm, k, bank[4 + par], act_hi, act_lo, arr)
                pe_used(pe, last)

            def down(mm, k, jn, par, first, final):
                pe.wait_ge(ff_ready, 2 + jn + 1)
                last = pe_panel_rows(pe, mm, k, bank[0:4], lambda kk: ff_hi[:, par, kk * T:(kk + 1) * T],
                                     lambda kk: ff_lo[:, par, kk * T:(kk + 1) * T], first, final, parts=final)
                pe_used(pe, last)

            up(m, k0, j0, 0, arrive)
            up(m, k0 + 1, j0 + 1, 1)
            down(m, k0 + 2, j0, 0, True, False)
            up(m, k0 + 3, j0 + 2, 0)
            down(m, k0 + 4, j0 + 1, 1, False, False)
            if mods == "tail":
                pe_mod(pe, 12 * l + 10, macc, MOD_AT + 40)
            with pe.Fori(1, FF_STEPS // 2 - 1) as i:
                up(m + i, k0 + 1, j0 + 2 * i + 1, 1)
                down(m + i, k0 + 2, j0 + 2 * i, 0, False, False)
                up(m + i, k0 + 3, j0 + 2 * i + 2, 0)
                down(m + i, k0 + 4, j0 + 2 * i + 1, 1, False, False)
                if mods == "ahead":
                    pe_mod(pe, 12 * l + 9 + i, macc, MOD_AT + 36 + 4 * i)
            e = m + FF_STEPS // 2 - 1
            up(e, k0 + 1, j0 + FF_STEPS - 1, 1)
            down(e, k0 + 2, j0 + FF_STEPS - 2, 0, False, False)
            if mods == "tail":
                pe_mod(pe, 12 * l + 11, macc, MOD_AT + 44)
            down(e, k0 + 3, j0 + FF_STEPS - 1, 1, False, True)

        def pe_scores(pe, l, i, cmp):
            b, g = i // 2, i % 2
            h = slice(64 * g, 64 * g + 64)
            s0, s1 = bank[2 * (i % 2)], bank[2 * (i % 2) + 1]
            if cmp:
                for tt in range(TT):
                    o = s0[:, 256 + 16 * tt:271 + 16 * tt]
                    nc.tensor.matmul(o, qr[h, b, tt * P:(tt + 1) * P], kcmp[h, :], start=True, stop=False)
                    last = nc.tensor.matmul(o, idb[:, :], cmpmb[:, 16 * tt:16 * tt + 15], start=False, stop=True)
                last.then_inc(at_sc, 1)
                return
            both = lambda ap, n: ap.rearrange("p (b s) -> p b s", b=2)[:, :, n:n + P]
            mask = causb[:, :].unsqueeze(1).to_broadcast([P, 2, P])
            nc.tensor.matmul(s0[:, 0:T], qr[h, b, 0:P], kr[h, :, 0:P], start=True, stop=False)
            nc.tensor.matmul(s0[:, 0:T], idb[:, :], mask, start=False, stop=True)
            nc.tensor.matmul(s1[:, :], qr[h, b, P:T], kr[h, :, :], start=True, stop=False, skip_group_check=True)
            nc.tensor.matmul(both(s1[:, :], P), idb[:, :], mask, start=False, stop=True, skip_group_check=True)

        def pe_turn(pe, l, i):
            pe.wait_ge(at_p, 8 * l + i + 1)
            if i:
                pe.wait_ge(at_ev0, 8 * l + i)
                pe.wait_ge(at_ev1, 8 * l + i)
            pb = pbuf[i % 2]
            for n in range(6):
                br, part = n // 3, n % 3
                src = pb[:, br * P:(br + 1) * P] if part == 0 else pb[:, 288 + br * T + (part - 1) * P:288 + br * T + part * P]
                nc.tensor.transpose(bank[6 + n // 4][:, (n % 4) * P:(n % 4 + 1) * P], src, ident)
            for tt in range(TT):
                last = nc.tensor.transpose(bank[7][0:15, T + tt * P:T + (tt + 1) * P], pb[:, 256 + 16 * tt:271 + 16 * tt], ident)
            last.then_inc(at_tr, 1)

        def pe_pv(pe, l, i):
            b, g = i // 2, i % 2
            o = bank[4 + b % 2][64 * g:64 * g + 64, 0:T]
            if g == 0:
                pe_gfree(pe, l, 8 + b)
            pe.wait_ge(at_ev0, 8 * l + i + 1)
            pe.wait_ge(at_ev1, 8 * l + i + 1)
            pt = pts[i % 2]
            for br in range(2):
                v = slice(br * P + 64 * g, br * P + 64 * g + 64)
                nc.tensor.matmul(o, vt[:, 0, v], pt[:, br * 384:br * 384 + T], start=br == 0, stop=False, skip_group_check=True)
                nc.tensor.matmul(o[:, P:T], vt[:, 1, v], pt[:, br * 384 + T:br * 384 + 384], start=False, stop=False, skip_group_check=True)
            nc.tensor.matmul(o, vcmp[0:15, 64 * g:64 * g + 64], pt[0:15, 768:1024], start=False, stop=True,
                             skip_group_check=True).then_inc(at_pv, 1)


        ACT_LINKS = 5

        def rsqrt(link, o, src, scale, eps):
            link(nc.scalar.activation(o, src, ACT.Ln, bias=eps, scale=scale))
            return nc.scalar.activation(o, o, ACT.Exp, scale=-0.5)

        def ln_table():
            nc.scalar.activation(ln_out[:, :], cst[:, C_EPS:C_EPS + 1], ACT.Ln)

        def act_squares(act, q):
            for kc in range(KC):
                act.wait_ge(x_ready, 8 * q + kc + 1)
                nc.scalar.activation(tbuf[:, kc, :], x[:, kc, :], ACT.Square).then_inc(sq_done, 1)
            ln_table()

        def act_norm(act, l, q, link, shift):
            act.wait_ge(ss_done, q + 1)
            rsqrt(link, rs[:, :], bank[6][:, 0:T], 1.0 / D, cst[:, C_EPS:C_EPS + 1]).then_inc(rs_done, 1)
            for kc in range(KC):
                act.wait_ge(t_done, 8 * q + kc + 1)
                nc.scalar.activation(act_hi[:, kc, :], tbuf[:, kc, :], ACT.Identity, bias=modc[:, shift + kc:shift + kc + 1])\
                    .then_inc(act_his, 1)

        def act_layer(act, l, link, ahead):
            m = 11 * l
            used = lambda k: act.wait_ge(split_free, SPLIT + 4 * m + k + 1)
            act_norm(act, l, 2 * l, link, 0)
            act.wait_ge(lc_ready, 16 * l + 16)
            nc.scalar.activation(gwh[:, :, :], lc[:, LC_GW:LC_GW + 192].rearrange("p (k n) -> p k n", k=KC), ACT.Copy).then_inc(gw_hi, 1)
            split_hi(act, m, 2)
            split_hi(act, m, 3)
            G = lambda g: bank[4 + g % 2]
            used(L_K0K1)
            nc.scalar.activation(tbuf[:, 0, :], G(0)[:, T:2 * T], ACT.Square).then_inc(nr_sq, 1)
            for g in range(2):
                for j2 in range(2):
                    src = win(G(0), 64 * g, 64, [[2, 16], [16, 15]], j2)
                    last = nc.scalar.activation(tb[64 * j2:64 * j2 + 64, :, 15 * g:15 * g + 15], src, ACT.Copy)
            last.then_inc(tb_k, 1)
            split_hi(act, m, 4)
            used(L_K2V0)
            nc.scalar.activation(tbuf[:, 1, :], G(1)[:, 0:T], ACT.Square).then_inc(nr_sq, 1)
            split_hi(act, m, 5)
            act.wait_ge(tb_pe, l + 1)
            nc.scalar.activation(tbh[:, :, :], tb, ACT.Copy).then_inc(tb_hi, 1)
            split_hi(act, m, 6)
            act.wait_ge(gfull, 3 * l + 1)
            nc.scalar.activation(gts[:, :, :], G(3)[:, 0:48].rearrange("p (t n) -> p t n", t=TT), ACT.Exp, scale=-1.0).then_inc(gfree[1], 1)
            used(L_Q0)
            nc.scalar.activation(tbuf[:, 2:4, :], G(4)[:, :].rearrange("p (b t) -> p b t", b=2), ACT.Square).then_inc(nr_sq, 1)
            split_hi(act, m, 7)

            def roots(*js):
                at = {3: (sqc[:, 16:31], bank[6][:, 256:271])}
                for j in range(3):
                    at[j] = (tbuf[:, 2 * j:2 * j + 2, :], bank[(0, 2, 2)[j]][:, :].rearrange("p (b t) -> p b t", b=2))
                for j in js:
                    act.wait_ge(nr_mm, 4 * l + j + 1)
                    last = nc.scalar.activation(at[j][0], at[j][1], ACT.Ln, bias=cst[:, C_EPS:C_EPS + 1], scale=1.0 / 64)
                link(last)
                for j in js:
                    nc.scalar.activation(at[j][0], at[j][0], ACT.Exp, scale=-0.5).then_inc(nr_rs, 1)

            used(L_CMP)
            nc.scalar.activation(ce, bank[6][:, 0:60], ACT.Exp, scale=-1.0).then_inc(cmp_e, 1)
            split_hi(act, m, 8)
            roots(0, 1)
            used(L_Q1)
            nc.scalar.activation(tbuf[:, 4:6, :], G(5)[:, :].rearrange("p (b t) -> p b t", b=2), ACT.Square).then_inc(nr_sq, 1)
            act.wait_ge(cmp_w2, l + 1)
            nc.scalar.activation(sqc[:, 0:15], bank[6][:, 64:79], ACT.Square).then_inc(nr_sq, 1)
            split_hi(act, m, 9)
            used(L_U0)
            nc.scalar.activation(ub[:, 0:2, 16:16 + T], G(6)[:, :].rearrange("p (b t) -> p b t", b=2), ACT.Copy).then_inc(gfree[0], 1)
            roots(2, 3)
            split_hi(act, m, 10)

            def exponentials(i):
                s0, s1, pb = bank[2 * (i % 2)], bank[2 * (i % 2) + 1], pbuf[i % 2]
                if i >= 2:
                    act.wait_ge(at_tr, 8 * l + i - 1)
                act.wait_ge(at_nm, 8 * l + i + 1)
                for n, (src, dst) in enumerate((
                        (s0[:, 0:P], pb[:, 0:P]), (s0[:, P:T], pb[:, P:T]),
                        (s0[:, 256:271], pb[:, 256:271]), (s0[:, 272:287], pb[:, 272:287]),
                        (s1[:, 0:T], pb[:, 288:288 + T]), (s1[:, T:2 * T], pb[:, 288 + T:288 + 2 * T]))):
                    last = nc.scalar.activation(dst, src, ACT.Exp, bias=nm[:, i % 2, n:n + 1], accum_out=dens[:, i % 2, n:n + 1])
                last.then_inc(at_exp, 1)

            exponentials(0)
            exponentials(1)
            used(L_U1)
            link(nc.scalar.activation(ub[:, 2:4, 16:16 + T], G(7)[:, :].rearrange("p (b t) -> p b t", b=2), ACT.Copy))
            act.sem_inc(gfree[1], 1)
            act.sem_inc(u_copied, 2)
            for i in range(8):
                act_pt(act, l, i)
                if i + 2 < 8:
                    exponentials(i + 2)
                if i == 1:
                    split_hi(act, m, 11)
                if i >= 2 and i % 2 == 0:
                    act_mixed(act, l, (i - 2) // 2)
            act_mixed(act, l, 3)
            for g in range(4):
                act.wait_ge(gfull, 3 * l + 2 + g // 2)
                nc.scalar.activation(mix_hi[:, g, :], bank[4 + g // 2][:, (g % 2) * T:(g % 2 + 1) * T], ACT.Copy,
                                     scale=lc[:, LC_PS + g:LC_PS + g + 1]).then_inc(mix_his, 1)
            for k in range(3):
                split_hi(act, m, 12 + k)
            act_squares(act, 2 * l + 1)
            act_norm(act, l, 2 * l + 1, link, 24)
            act_ff(act, l, m, L_FF, 16 * l)
            if ahead:
                act_squares(act, 2 * l + 2)

        def act_pt(act, l, i):
            act.wait_ge(at_tr, 8 * l + i + 1)
            if i >= 2:
                act.wait_ge(at_pv, 8 * l + i - 1)
            nc.scalar.activation(pts[i % 2][:, 0:512], bank[6][:, :], ACT.Copy).then_inc(at_ev0, 1)

        def act_mixed(act, l, b):
            act.wait_ge(at_pv, 8 * l + 2 * b + 2)
            nc.scalar.activation(mix_hi[:, 4 + b, :], bank[4 + b % 2][:, 0:T], ACT.Copy).then_inc(mix_his, 1)

        def act_ff(act, l, m, k0, j0, final=False):
            def step(mm, jn, kf, par, kd, s, at):
                act.wait_ge(split_free, SPLIT + 4 * mm + kf + 1)
                act.wait_ge(ff_ready, jn + 1)
                nc.scalar.activation(fr[par], bank[4 + par][:, :], ACT.Relu).then_inc(ff_relu, 1)
                if s[0] is not None:
                    split_hi(act, mm, s[0])
                act.wait_ge(ff_sq, jn + 1)
                if kd is not None:
                    act.wait_ge(split_free, SPLIT + 4 * mm + kd + 1)
                nc.scalar.activation(ff_hi[:, par, :], fr[par], ACT.Copy).then_inc(ff_his, 1)
                if s[1] is not None:
                    split_hi(act, mm, s[1])

            ff_schedule(act, m, k0, j0, step, final)

        def ff_schedule(eng, m, k0, j0, step, final):
            step(m, j0, k0, 0, None, (k0 + 3, k0 + 4), 0)
            step(m, j0 + 1, k0 + 1, 1, None, (k0 + 5, k0 + 6), 1)
            with eng.Fori(1, FF_STEPS // 2 - 1) as i:
                step(m + i, j0 + 2 * i, k0 - 1, 0, k0 - 2, (k0 + 3, k0 + 4), i)
                step(m + i, j0 + 2 * i + 1, k0 + 1, 1, k0, (k0 + 5, k0 + 6), i)
            e = m + FF_STEPS // 2 - 1
            step(e, j0 + FF_STEPS - 2, k0 - 1, 0, k0 - 2, (k0 + 3, None if final else k0 + 4), 14)
            step(e, j0 + FF_STEPS - 1, k0 + 1, 1, k0, (None, None if final else k0 + 5), 15)

        DVE_LINKS = 31

        def dve_mod(dve, pair, o, half, steps=(0, 8)):
            if steps[0] == 0:
                dve.wait_ge(modraw[half], 16 * pair if not isinstance(pair, int) or pair else 16)
            unit = modw[:, half, :].rearrange("p (b k n) -> p b k n", b=2, k=4)
            for n in range(8 * half + steps[0], 8 * half + steps[1]):
                kc, p = n // 2, n % 2
                if n == 9:
                    dve.wait_ge(mod_used, 2 + 2 * pair + 1)
                elif n >= 2:
                    dve.wait_ge(mod_links, 14 * pair + n - 1 - (n > 9))
                src, c = unit[:, p, kc % 4, :], cact[:, kc:kc + 1]
                if n < 2:
                    ins = nc.vector.tensor_scalar(o[:, p, :], src, c, None, ALU.mult)
                else:
                    ins = nc.vector.scalar_tensor_tensor(o[:, p, :], src, c, o[:, p, :], ALU.mult, ALU.add)
                ins.then_inc(mod_used if n % 8 == 7 else mod_links, 1)

        def dve_modc(dve, done, count, c0, bias, pair):
            dve.wait_ge(macc_free, 2 + 2 * pair + 2)
            n = bias.shape[1]
            c1 = 0 if c0 == 48 else c0
            nc.vector.tensor_tensor(modc[:, c1:c1 + n], bank[7][:, MOD_AT + c0:MOD_AT + c0 + n], bias, ALU.add).then_inc(done, 1)
            dve.wait_ge(done, count)

        def dve_norm(dve, q, g0, shift):
            dve.wait_ge(rs_done, q + 1)
            for kc in range(KC + 1):
                if kc < KC:
                    nc.vector.scalar_tensor_tensor(tbuf[:, kc, :], x[:, kc, :], gcol[:, g0 + kc:g0 + kc + 1], rs[:, :], ALU.mult, ALU.mult)\
                        .then_inc(t_done, 1)
                if kc:
                    c = kc - 1
                    dve.wait_ge(act_his, 8 * q + c + 1)
                    nc.vector.scalar_tensor_tensor(act_lo[:, c, :], tbuf[:, c, :], modc[:, shift + c:shift + c + 1],
                                                   act_hi[:, c, :].bitcast(F32), ALU.add, ALU.subtract).then_inc(act_ready, 1)

        def dve_layer(dve, l, link, ahead):
            m = 11 * l
            used = lambda k: dve.wait_ge(split_free, SPLIT + 4 * m + k + 1)
            G = lambda g: bank[4 + g % 2]
            two = lambda ap: ap.rearrange("p (b t) -> p b t", b=2)
            dve_norm(dve, 2 * l, 0, 0)
            for k in (2, 3):
                split_lo(dve, m, k)
            dve.wait_ge(gw_hi, l + 1)
            nc.vector.tensor_tensor(gwl[:, :, :], lc[:, LC_GW:LC_GW + 192].rearrange("p (k n) -> p k n", k=KC), gwh[:, :, :].bitcast(F32),
                                    ALU.subtract).then_inc(gw_lo, 1)
            used(L_K0K1)
            dve.wait_ge(tb_k, l + 1)
            nc.vector.tensor_scalar(ybuf[0][:, 0, :], G(0)[:, T:2 * T], lc[:, LC_KN + 1:LC_KN + 2], None, ALU.mult).then_inc(gfree[0], 1)
            split_lo(dve, m, 4)
            used(L_K2V0)
            dve.wait_ge(nr_sq, 5 * l + 2)
            for g in range(2):
                for j2 in range(2):
                    src = win(G(1), 64 * g, 64, [[2, 16], [16, 15]], T + j2)
                    last = nc.vector.tensor_copy(tb[64 * j2:64 * j2 + 64, :, 30 + 15 * g:45 + 15 * g], src)
            last.then_inc(tb_v, 1)
            nc.vector.tensor_scalar(ybuf[0][:, 1, :], G(1)[:, 0:T], lc[:, LC_KN + 2:LC_KN + 3], None, ALU.mult).then_inc(gfree[1], 1)
            dve.wait_ge(tb_v, l + 1)
            pe_bc = win(lc, 0, P, [[2, 16], [1, 2], [0, 30]], LC_PE)
            tb4 = tb.rearrange("p j (v n) -> p j v n", v=2)
            nc.vector.tensor_tensor(tb4, tb4, pe_bc, ALU.add).then_inc(tb_pe, 1)
            split_lo(dve, m, 5)
            used(L_V1V2)
            nc.vector.tensor_copy(vt, two(G(2)[:, :])).then_inc(gfree[0], 1)
            dve.wait_ge(tb_hi, l + 1)
            nc.vector.tensor_tensor(tbl[:, :, :], tb, tbh[:, :, :].bitcast(F32), ALU.subtract).then_inc(tb_lo, 1)
            split_lo(dve, m, 6)
            dve.wait_ge(gfree[1], 7 * l + 3)
            link(nc.vector.tensor_scalar(gts[:, :, :], gts[:, :, :], 1.0, None, ALU.add))
            link(nc.vector.reciprocal(gts[:, :, :], gts[:, :, :]))
            link(nc.vector.tensor_scalar(gts[:, 0, 0:24:3], gts[:, 0, 0:24:3], cst[:, C_VALID:C_VALID + 1], None, ALU.mult))

            def scaled(j):
                dve.wait_ge(nr_sq, 5 * l + 2 + j)
                nc.vector.tensor_scalar(ybuf[j], two(G(3 + j)[:, :]), lc[:, LC_QN:LC_QN + 1], 0.125, ALU.mult, ALU.mult).then_inc(gfree[(j + 1) % 2], 1)

            def rotated(j):
                dst = kr if j == 0 else qr[:, 2 * j - 2:2 * j, :]
                dve.wait_ge(nr_mm, 4 * l + j + 1)
                link(nc.vector.tensor_tensor(dst, two(bank[(1, 3, 3)[j]][:, :]), cst[:, C_SIN:C_SIN + T].unsqueeze(1).to_broadcast([P, 2, T]), ALU.mult))
                dve.wait_ge(nr_yc, 3 * l + j + 1)
                link(nc.vector.tensor_tensor(dst, dst, ybuf[j], ALU.add))
                dve.wait_ge(nr_rs, 4 * l + j + 1)
                nc.vector.tensor_tensor(dst, dst, tbuf[:, 2 * j:2 * j + 2, :], ALU.mult).then_inc(nr_out, 1)

            scaled(1)
            split_lo(dve, m, 7)
            dve.wait_ge(cmp_e, l + 1)
            link(nc.vector.tensor_scalar(ce, ce, 1.0, None, ALU.add))
            link(nc.vector.reciprocal(ce, ce))
            nc.vector.tensor_tensor(hs, bank[6][:, 0:60], ce, ALU.mult).then_inc(cmp_s, 1)
            split_lo(dve, m, 8)
            rotated(0)
            rotated(1)
            scaled(2)
            dve.wait_ge(cmp_w2, l + 1)
            dve.wait_ge(nr_sq, 5 * l + 5)
            nc.vector.tensor_copy(vcmp[0:15, :], bank[6][0:15, P:T])
            nc.vector.tensor_scalar(ycmp, bank[6][:, 64:79], lc[:, LC_KN:LC_KN + 1], None, ALU.mult).then_inc(cmp_y, 1)
            split_lo(dve, m, 9)
            rotated(2)
            dve.wait_ge(nr_mm, 4 * l + 4)
            link(nc.vector.tensor_tensor(ycmp, ycmp, cst[:, C_CCOS:C_CCOS + 15], ALU.mult))
            dve.wait_ge(nr_rs, 4 * l + 4)
            link(nc.vector.tensor_tensor(kcmp, bank[6][:, 288:303], cst[:, C_CSIN:C_CSIN + 15], ALU.mult))
            link(nc.vector.tensor_tensor(kcmp, kcmp, ycmp, ALU.add))
            nc.vector.tensor_tensor(kcmp, kcmp, sqc[:, 16:31], ALU.mult).then_inc(nr_out, 1)
            split_lo(dve, m, 10)

            def maxima(i):
                s0, s1, o = bank[2 * (i % 2)], bank[2 * (i % 2) + 1], nm[:, i % 2, :]
                dve.wait_ge(at_sc, 8 * l + i + 1)
                nc.vector.tensor_reduce(o[:, 0:2], two(s0[:, 0:T]), AX.X, ALU.max, negate=True)
                nc.vector.tensor_reduce(o[:, 2:4], win(s0, 0, P, [[16, 2], [1, 15]], T), AX.X, ALU.max, negate=True)
                nc.vector.tensor_reduce(o[:, 4:6], two(s1[:, :]), AX.X, ALU.max, negate=True).then_inc(at_nm, 1)

            def weigh(i):
                b, g = i // 2, i % 2
                pb, f, d = pbuf[i % 2], fac[:, i % 2, :], dens[:, i % 2, :]
                dve.wait_ge(at_exp, 8 * l + i + 1)
                link(nc.vector.reciprocal(f, d))
                h0 = 3 * (4 * g + b)
                nc.vector.tensor_tensor(f[:, 0:2], f[:, 0:2], gts[:, 0, h0 + 1:h0 + 3], ALU.mult)
                nc.vector.tensor_tensor(f[:, 2:4], f[:, 2:4], gts[:, :, h0], ALU.mult)
                link(nc.vector.tensor_tensor(f[:, 4:6], f[:, 4:6], gts[:, 1, h0 + 1:h0 + 3], ALU.mult))
                for n, (c0, w) in enumerate(((0, P), (P, P), (256, 15), (272, 15), (288, T), (288 + T, T))):
                    last = nc.vector.tensor_scalar(pb[:, c0:c0 + w], pb[:, c0:c0 + w], f[:, n:n + 1], None, ALU.mult)
                last.then_inc(at_p, 1)

            def copy_pt(i):
                dve.wait_ge(at_tr, 8 * l + i + 1)
                if i >= 2:
                    dve.wait_ge(at_pv, 8 * l + i - 1)
                nc.vector.tensor_copy(pts[i % 2][:, 512:768], bank[7][:, 0:T])
                nc.vector.tensor_copy(pts[i % 2][0:15, 768:1024], bank[7][0:15, T:2 * T]).then_inc(at_ev1, 1)

            def mixed(b):
                dve.wait_ge(mix_his, 8 * l + b + 1)
                nc.vector.tensor_tensor(mix_lo[:, 4 + b, :], bank[4 + b % 2][:, 0:T], mix_hi[:, 4 + b, :].bitcast(F32), ALU.subtract)\
                    .then_inc(gfree[b % 2], 1)

            def mod(half, steps=(0, 8)):
                pair = half // 2
                dve_mod(dve, 12 * l + 4 + pair, mod_sums[:, 2 * pair:2 * pair + 2, :], half % 2, steps=steps)

            maxima(0)
            maxima(1)
            weigh(0)
            for i in range(8):
                copy_pt(i)
                if i + 1 < 8:
                    weigh(i + 1)
                if i == 2:
                    split_lo(dve, m, 11)
                if i + 2 < 8:
                    maxima(i + 2)
                mod(i)
                if i >= 2 and i % 2 == 0:
                    mixed((i - 2) // 2)
            mixed(3)
            dve_modc(dve, modc_ready, 3 * l + 2, 16, lc[:, LC_BM:LC_BM + 16], 12 * l + 7)
            for g in range(4):
                dve.wait_ge(mix_his, 8 * l + 4 + g // 2 * 2 + 2)
                last = nc.vector.scalar_tensor_tensor(mix_lo[:, g, :], bank[4 + g // 2][:, (g % 2) * T:(g % 2 + 1) * T],
                                                      lc[:, LC_PS + g:LC_PS + g + 1], mix_hi[:, g, :].bitcast(F32), ALU.mult, ALU.subtract)
                if g % 2:
                    last.then_inc(gfree[g // 2], 1)
            for i in range(4):
                if i < 3:
                    mod(8 + i)
                    split_lo(dve, m, 12 + i)
                used(L_OUT + i)
                for c in range(2):
                    kc = 2 * i + c
                    nc.vector.scalar_tensor_tensor(x[:, kc, :], bank[4 + i % 2][:, c * T:(c + 1) * T], modc[:, 16 + kc:17 + kc], x[:, kc, :],
                                                   ALU.mult, ALU.add).then_inc(x_ready, 1)
            mod(11)
            dve_modc(dve, modc_ready, 3 * l + 3, 32, lc[:, LC_BM + 16:LC_BM + 24], 12 * l + 9)
            link(nc.vector.scalar_tensor_tensor(gcol[:, KC:2 * KC], modc[:, 32:40], 1.0, lc[:, LC_N2:LC_N2 + KC], ALU.add, ALU.mult))
            dve_norm(dve, 2 * l + 1, KC, 24)
            dve_ff(dve, m, L_FF, 16 * l, l=l, mods="ahead" if ahead else "tail")
            if ahead:
                dve.wait_ge(macc_free, 2 + 24 * l + 32)
                nc.vector.tensor_tensor(modc[:, 0:16], bank[7][:, MOD_AT + 48:MOD_AT + 64], lc[:, LC_BA:LC_BA + 16], ALU.add)
            dve_modc(dve, modc_ready, 3 * l + 4, 40, lc[:, LC_BM + 24:LC_BM + 32], 12 * l + 11)
            if ahead:
                nc.vector.scalar_tensor_tensor(gcol[:, 0:KC], modc[:, 8:16], 1.0, lc[:, LC_NA:LC_NA + KC], ALU.add, ALU.mult)
            for kc in range(KC):
                if kc == 6:
                    dve.wait_ge(split_free, SPLIT + 4 * m + L_PANELS)
                elif kc % 2 == 0:
                    dve.wait_ge(rows_done, 3 * l + kc // 2 + 1)
                nc.vector.scalar_tensor_tensor(x[:, kc, :], bank[kc // 2][:, (kc % 2) * T:(kc % 2 + 1) * T], modc[:, 40 + kc:41 + kc],
                                               x[:, kc, :], ALU.mult, ALU.add).then_inc(x_ready, 1)

        def dve_ff(dve, m, k0, j0, final=False, l=0, mods=None):
            def mod(at, half):
                inside = not isinstance(at, int)
                if mods == "ahead" and inside:
                    pair = 12 * l + 9 + at
                elif mods == "tail" and not inside:
                    pair = 12 * l + (10 if at < 2 else 11)
                else:
                    return
                if half == 0:
                    dve.wait_ge(macc_free, 2 * pair + 2)
                dve_mod(dve, pair, macc, half)

            def step(mm, jn, kf, par, kd, s, at):
                dve.wait_ge(ff_relu, 2 + jn + 1)
                nc.vector.tensor_tensor(fr[par], fr[par], fr[par], ALU.mult).then_inc(ff_sq, 1)
                if s[0] is not None:
                    split_lo(dve, mm, s[0])
                dve.wait_ge(ff_his, jn + 1)
                nc.vector.tensor_tensor(ff_lo[:, par, :], fr[par], ff_hi[:, par, :].bitcast(F32), ALU.subtract).then_inc(ff_ready, 1)
                mod(at, par)
                if s[1] is not None:
                    split_lo(dve, mm, s[1])

            ff_schedule(dve, m, k0, j0, step, final)

        M2 = L_PANELS // SPLIT * layers
        used2 = lambda eng, k: eng.wait_ge(split_free, SPLIT + 4 * M2 + k + 1)
        free2 = lambda eng, k: eng.wait_ge(gfree[k % 2], 7 * layers + k // 2 + 1)
        G2 = lambda k: bank[4 + k % 2]
        blocks2 = lambda ap: ap.rearrange("p (b t) -> p b t", b=2)
        XR = 16 * layers + 8

        dt_mm, dt_y, dt_n, dt_e, dt_pos, dt_ln, dt_done, dt_tr, dt_cols = [sem(n) for n in ("dt_mm", "dt_y", "dt_n", "dt_e", "dt_pos", "dt_ln", "dt_done", "dt_tr", "dt_cols")]
        pads_ready = sem("pads_ready")
        alog_e = sem("alog_e")
        d_stored = sem("d_stored")
        lc2_ready = sem("lc2_ready")
        dist_ready = sem("dist_ready")
        s2_sc = sem("s2_sc")
        s2_nm = sem("s2_nm")
        s2_exp = sem("s2_exp")
        s2_p = sem("s2_p")
        s2_tr = sem("s2_tr")
        s2_ev0, s2_ev1 = sem("s2_ev0"), sem("s2_ev1")
        s2_pv = sem("s2_pv")
        s2_hi, s2_lo = sem("s2_hi"), sem("s2_lo")
        conv_done = sem("conv_done")
        silu_done = sem("silu_done")
        cb_mm, cb_done = sem("cb_mm"), sem("cb_done")
        xt_mm0, xt_mm1, xt_done0, xt_done1 = sem("xt_mm0"), sem("xt_mm1"), sem("xt_done0"), sem("xt_done1")
        db_ready = [sem(f"db_ready{i}") for i in range(4)]
        e_mask = sem("e_mask")
        e_exp = sem("e_exp")
        e_mul = sem("e_mul")
        e_used = sem("e_used")
        y_out = sem("y_out")
        z_silu = sem("z_silu")
        y_gated = sem("y_gated")
        y_sq = sem("y_sq")
        y_ss = sem("y_ss")
        y_rs = sem("y_rs")
        y_fin = sem("y_fin")
        y_hi, y_lo = sem("y_hi"), sem("y_lo")
        gates_done = sem("gates_done")
        att_proj = sem("att_proj")
        mx_sum, mx_hi, mx_lo = sem("mx_sum"), sem("mx_hi"), sem("mx_lo")
        x2_ready = sem("x2_ready")
        ln_sum, ln_mean, ln_c, ln_sq, ln_ss, ln_rs, ln_t, ln_hi, ln_x, ln_lo = [
            sem(n) for n in ("ln_sum", "ln_mean", "ln_c", "ln_sq", "ln_ss", "ln_rs", "ln_t", "ln_hi", "ln_x", "ln_lo")]
        o_turned = sem("o_turned")
        o_copied0, o_copied1 = sem("o_copied0"), sem("o_copied1")

        at[0] = 0
        xb = area(24 * T, 24, T)
        zb_at = at[0]
        zb = area(16 * T, 16, T)
        xt_at = at[0]
        xt = area(8 * T, 2, TT, 2 * T)
        cb = area(4 * T, 2, TT, T)
        work_at = at[0]
        decays = area(12 * T)
        lc2 = area(LC2)
        dtt = area(P, TT, 64)
        gb = arena[:, xt_at:xt_at + 16 * T].rearrange("p (b t) -> p b t", b=16)
        sq2 = arena[:, xt_at + 16 * T:xt_at + 20 * T].rearrange("p (b t) -> p b t", b=4)
        rs2 = arena[:, xt_at + 20 * T:xt_at + 24 * T].rearrange("p (n t) -> p n t", n=4)
        v2 = arena[:, zb_at:zb_at + 6 * T].rearrange("p (t n) -> p t n", t=TT)
        pp = [arena[:, zb_at + (6 + 3 * i) * T:zb_at + (9 + 3 * i) * T] for i in range(2)]
        dist = arena[:, zb_at + 12 * T:zb_at + 16 * T + 2 * T].rearrange("p (t a s) -> p t a s", t=TT, a=3)
        pt2 = arena[:, xt_at + 2 * T:xt_at + 8 * T].rearrange("p (n t) -> p n t", n=6)
        up = [arena[:, work_at + i * 520:work_at + (i + 1) * 520].rearrange("p (b t) -> p b t", b=2) for i in range(2)]
        dw = [arena[0:64, work_at + 1040 + i * T:work_at + 1040 + (i + 1) * T] for i in range(6)]
        qk = mixf[:, 0:12 * T].rearrange("p (b t) -> p b t", b=12)
        eb = [v[:, i * 6 * T:(i + 1) * 6 * T] for v in (mixf, decays) for i in range(2)]
        eb_far = [v[:, 0:4 * T].rearrange("p (h t) -> p h t", h=4) for v in eb]
        eb_near = [v[:, 4 * T:6 * T].rearrange("p (h t) -> p h t", h=4) for v in eb]
        m2 = zb[:, 0:8, :]
        mx = zb[:, 8:16, :]
        tb2 = xb[:, 0:8, :]
        obuf = xb[:, 8:16, :].rearrange("p b t -> p (b t)").rearrange("p (t d) -> p t d", t=TT)
        ea = small[0:64, 158:159]
        dens2, nm2 = small[:, 150:152], small[:, 152:154]
        dscr = nc.dram_tensor("dscr", (64, T), F32, kind="Internal").ap()
        ATT_SLOT = {0: 0, 1: 1, 3: 2, 4: 3, 6: 4, 7: 5, 9: 6, 10: 7}
        PV_SLOT = {2: 0, 5: 1, 8: 2, 11: 3}
        ALPHA = 2.0 ** 0.25
        slope = lambda h: 2.0 ** (-8.0 * (h + 1) / 12)

        def head2(p, j):
            h = 4 * p + j
            return h // 2, slice(64 * (h % 2), 64 * (h % 2) + 64), h

        def fetch(sp, e):
            hu, st = e // 2, e % 2
            for o, d, t0, t1 in ((eb_far, st, 0, T), (eb_near, 1 - st, st * P, (st + 1) * P)):
                src = dscr[32 * d + 4 * hu:32 * d + 4 * hu + 4, t0:t1].partition_broadcast(P)
                sp.dma_start(o[e % 4], src).then_inc(db_ready[e % 4], 16)

        def finish(sp):
            for k in range(2, 6):
                load(sp, M2, k)
            with sp.Fori(0, 4) as i:
                for k in (6, 7, 8, 9):
                    load(sp, M2 + i, k)
            load(sp, M2, 22)
            load(sp, M2, 23)
            sp.wait_ge(d_stored, 16)
            sp.wait_ge(s2_sc, 8)
            fetch(sp, 0)
            fetch(sp, 1)
            load(sp, M2, 24)
            load(sp, M2, 25)
            sp.wait_ge(conv_done, 12)
            fetch(sp, 2)
            fetch(sp, 3)
            for hu in range(8):
                load(sp, M2, 26 + hu)
                for e in (2 * hu + 4, 2 * hu + 5):
                    if e < 16:
                        sp.wait_ge(e_used, e - 3)
                        fetch(sp, e)
            with sp.Fori(7, 19) as i:
                for k in (6, 7, 8, 9):
                    load(sp, M2 + i, k)
            for half in range(2):
                cols = slice(512 * half, 512 * (half + 1))
                sp.wait_ge(o_copied0, half + 1)
                sp.wait_ge(o_copied1, half + 1)
                sp.dma_start(out.rearrange("b (t p) d -> p (b t) d", p=P)[:, :, cols], obuf[:, :, cols]).then_inc(out_written, 16)
            sp.wait_ge(out_written, 32)
            sp.wait_ge(d_stored, 16)

        def pool_second(pool):
            pool.wait_ge(x_ready, 16 * layers)
            pool.dma_start(lc2, a["lc2"]).then_inc(lc2_ready, 16)
            pool.wait_ge(x_ready, XR)
            pool.dma_start(dist.rearrange("p t a s -> p (t a s)"), a["dist"]).then_inc(dist_ready, 16)
            for i in range(2):
                for c0 in (0, 258):
                    last = nc.gpsimd.memset(up[i][:, :, c0:c0 + 2], 0.0)
            last.then_inc(pads_ready, 1)
            pool.wait_ge(dt_done, 1)
            pool.dma_start(dscr, dw[5]).then_inc(d_stored, 16)

        def pe_second(pe):
            arrive = lambda kc: pe.wait_ge(act_ready, 16 * layers + kc + 1)

            def panel2(k, arr=None):
                free2(pe, k)
                pe_used(pe, pe_panel(pe, M2, k, G2(k), act_hi, act_lo, arr))

            for k in range(6):
                panel2(k, arrive if k == 0 else None)
            for k in range(6, 9):
                free2(pe, k)
                pe.wait_ge(lo_done, 4 * M2 + k + 1)
                for tt in range(TT):
                    ts = slice(tt * P, (tt + 1) * P)
                    for kc in range(KC):
                        last = mm3(G2(k)[:, tt * T:(tt + 1) * T], act_hi[:, kc, ts], act_lo[:, kc, ts],
                                   w_hi[slot(k)][:, kc * 256:(kc + 1) * 256], w_lo[slot(k)][:, kc * 256:(kc + 1) * 256], kc == 0, kc == KC - 1)
                pe_used(pe, last)
            pe.wait_ge(lc2_ready, 16)
            for kc in range(KC):
                last = nc.tensor.matmul(bank[6][0:64, 0:T], lc2[:, L2_WDT + 64 * kc:L2_WDT + 64 * kc + 64], x[:, kc, :],
                                        start=kc == 0, stop=kc == KC - 1)
            last.then_inc(dt_mm, 1)
            scores2(pe, 0)
            scores2(pe, 1)
            for i in range(12):
                panel2(9 + i)
                if i == 5:
                    pe.wait_ge(dt_done, 1)
                    pe.wait_ge(s2_ev0, 4)
                    for tt in range(TT):
                        last = nc.tensor.transpose(bank[6][:, tt * 64:(tt + 1) * 64], dw[1][:, tt * P:(tt + 1) * P], ident[0:64, 0:64])
                    last.then_inc(dt_tr, 1)
                if i in ATT_SLOT:
                    u = ATT_SLOT[i]
                    pe.wait_ge(s2_p, u + 1)
                    if u:
                        pe.wait_ge(s2_ev0, u)
                        pe.wait_ge(s2_ev1, u)
                    if u == 4:
                        pe.wait_ge(s2_lo, 1)
                        pe.wait_ge(dt_cols, 1)
                    for n in range(6):
                        last = nc.tensor.transpose(bank[6 + n // 4][:, (n % 4) * P:(n % 4 + 1) * P], pp[u % 2][:, n * P:(n + 1) * P], ident)
                    last.then_inc(s2_tr, 1)
                    if u + 2 < 8:
                        pe.wait_ge(s2_nm, u + 1)
                        scores2(pe, u + 2)
                if i in PV_SLOT:
                    j = PV_SLOT[i]
                    pe.wait_ge(s2_ev0, 2 * j + 2)
                    pe.wait_ge(s2_ev1, 2 * j + 2)
                    o = bank[7][64 * (j % 2):64 * (j % 2) + 64, T:2 * T]
                    for n in range(6):
                        h = 4 * (n // 2) + j
                        last = nc.tensor.matmul(o, v2[:, n % 2, 64 * h:64 * h + 64], pt2[:, n, :], start=n == 0, stop=n == 5)
                    last.then_inc(s2_pv, 1)

            def prepare(g):
                if g == 0:
                    pe.wait_ge(s2_lo, 2)
                    pe.wait_ge(silu_done, 3)
                else:
                    pe.wait_ge(xt_done1, g)
                for st in range(TT):
                    last = nc.tensor.matmul(bank[7][:, st * T:(st + 1) * T], xb[:, 16 + g, st * P:(st + 1) * P], xb[:, 20 + g, :],
                                            start=True, stop=True)
                last.then_inc(cb_mm, 1)
                if g:
                    pe.wait_ge(xt_done0, g)
                for st in range(TT):
                    if st:
                        pe.wait_ge(cb_done, g + 1)
                    for b in range(4):
                        last = nc.tensor.transpose(bank[6 + st][:, b * P:(b + 1) * P], xb[:, 4 * g + b, st * P:(st + 1) * P], ident)
                    last.then_inc((xt_mm0, xt_mm1)[st], 1)

            panel2(21)
            prepare(0)
            for hu in range(8):
                g = hu // 2
                if hu < 7:
                    panel2(22 + hu)
                if hu % 2 and g < 3:
                    prepare(g + 1)
                if hu == 0 or hu % 2 == 0:
                    pe.wait_ge(xt_done0, g + 1)
                    pe.wait_ge(xt_done1, g + 1)
                if hu >= 4:
                    pe.wait_ge(y_out, hu - 3)
                for st in range(TT):
                    e = 2 * hu + st
                    pe.wait_ge(e_mul, e + 1)
                    for h in range(4):
                        o = bank[hu % 4][64 * (h % 2):64 * (h % 2) + 64, (h // 2) * T:(h // 2 + 1) * T]
                        w = xt[:, g % 2, st, 64 * (4 * (hu % 2) + h):64 * (4 * (hu % 2) + h) + 64]
                        last = nc.tensor.matmul(o, w, eb_far[e % 4][:, h, :], start=st == 0 and h < 2, stop=st == 1, skip_group_check=True)
                    last.then_inc(e_used, 1)
            for i in range(8):
                panel2(29 + i)
                if 1 <= i < 5:
                    n = i - 1
                    pe.wait_ge(y_sq, n + 1)
                    pe.wait_ge(xt_done0, 4)
                    pe.wait_ge(xt_done1, 4)
                    for b in range(4):
                        last = nc.tensor.matmul(bank[6 + n // 2][:, n % 2 * T:(n % 2 + 1) * T], ones, sq2[:, b, :], start=b == 0, stop=b == 3)
                    last.then_inc(y_ss, 1)
            free2(pe, 37)
            free2(pe, 38)
            pe.wait_ge(y_rs, 1)
            pe.wait_ge(s2_lo, 2)
            pe_used(pe, pe_panel_rows(pe, M2, 37, bank[4:8], lambda kk: ff_hi[:, 0, kk * T:(kk + 1) * T],
                                      lambda kk: ff_lo[:, 0, kk * T:(kk + 1) * T], True, True))
            pe.wait_ge(y_out, 8)
            for n in range(8):
                if n % 2 == 0:
                    pe.wait_ge(y_lo, n // 2 + 1)
                hi, lo = (mix_hi, mix_lo) if n < 4 else (act_hi, act_lo)
                c = 2 * n % 8
                pe_used(pe, pe_panel_rows(pe, M2, 38 + n, bank[0:4], lambda kk: hi[:, c + kk, :], lambda kk: lo[:, c + kk, :], n == 0, n == 7,
                                          parts=n == 7))
            pe.wait_ge(att_proj, 4)
            for n in range(4):
                if n == 2:
                    pe.wait_ge(x2_ready, 2)
                if n == 3:
                    pe.wait_ge(x2_ready, 4)
                pe_used(pe, pe_panel(pe, M2, 46 + n, bank[4 + n % 2], mix_hi, mix_lo,
                                     (lambda kc: pe.wait_ge(mx_lo, kc // 2 + 1)) if n == 0 else None))
            pe_layer_norm(pe, 0)
            pe_ff(pe, layers, M2, lambda kc: pe.wait_ge(ln_lo, kc + 1), 16 * layers, 50)
            pe_layer_norm(pe, 1)
            for c in range(4):
                for kc in (2 * c, 2 * c + 1):
                    pe.wait_ge(ln_x, 8 + kc + 1)
                    for tt in range(TT):
                        last = nc.tensor.transpose(bank[c][:, tt * T + (kc % 2) * P:tt * T + (kc % 2 + 1) * P], x[:, kc, tt * P:(tt + 1) * P], ident)
                last.then_inc(o_turned, 1)

        def scores2(pe, u):
            j, tt = u // 2, u % 2
            for p in range(3):
                b, r, _ = head2(p, j)
                o = bank[2 * (u % 2) + p // 2][:, (p % 2) * T:(p % 2 + 1) * T]
                last = nc.tensor.matmul(o, qk[r, b, tt * P:(tt + 1) * P], qk[r, 6 + b, :], start=True, stop=True)
            last.then_inc(s2_sc, 1)

        def pe_layer_norm(pe, q):
            for kc in range(KC):
                pe.wait_ge(x2_ready, 8 * q + kc + 1)
                last = nc.tensor.matmul(bank[6][:, 0:T], ones, x[:, kc, :], start=kc == 0, stop=kc == KC - 1)
            last.then_inc(ln_sum, 1)
            for kc in range(KC):
                pe.wait_ge(ln_sq, 8 * q + kc + 1)
                last = nc.tensor.matmul(bank[7][:, 0:T], ones, tb2[:, kc, :], start=kc == 0, stop=kc == KC - 1)
            last.then_inc(ln_ss, 1)

        def act_second(act):
            link = Chain(act, act_links, 0)
            link.base = layers * ACT_LINKS
            for kc in range(KC):
                act.wait_ge(x_ready, XR - 8 + kc + 1)
                nc.scalar.activation(act_hi[:, kc, :], x[:, kc, :], ACT.Copy).then_inc(act_his, 1)
            for k in (2, 3):
                split_hi(act, M2, k)
            for k in range(9):
                used2(act, k)
                if k < 6:
                    if k == 0:
                        act.wait_ge(x_ready, XR)
                    nc.scalar.activation(qk[:, 2 * k:2 * k + 2, :], blocks2(G2(k)[:, :]), ACT.Copy, scale=0.125 if k < 3 else 1.0)\
                        .then_inc(gfree[k % 2], 1)
                split_hi(act, M2, k + 4)
            act.wait_ge(dt_mm, 1)
            nc.scalar.activation(dw[0], bank[6][0:64, 0:T], ACT.Identity, bias=lc2[0:64, L2_DTB:L2_DTB + 1]).then_inc(dt_y, 1)
            nc.scalar.activation(ea, lc2[0:64, L2_ALOG:L2_ALOG + 1], ACT.Exp).then_inc(alog_e, 1)

            def exp2(u):
                act.wait_ge(s2_nm, u + 1)
                nc.scalar.activation(pp[u % 2], pp[u % 2], ACT.Exp, bias=nm2[:, u % 2:u % 2 + 1], accum_out=dens2[:, u % 2:u % 2 + 1])\
                    .then_inc(s2_exp, 1)

            def silu(n):
                nc.scalar.activation(xb[:, 8 * n:8 * n + 8, :], xb[:, 8 * n:8 * n + 8, :], ACT.Silu).then_inc(silu_done, 1)

            exp2(0)
            act.wait_ge(pads_ready, 1)
            for i in range(12):
                used2(act, 9 + i)
                if i >= 2:
                    act.wait_ge(conv_done, i - 1)
                nc.scalar.activation(up[i % 2][:, :, 2:2 + T], blocks2(G2(9 + i)[:, :]), ACT.Copy)
                for c in range(2):
                    b = 2 * i + c
                    last = nc.scalar.activation(xb[:, b, :], G2(9 + i)[:, c * T:(c + 1) * T], ACT.Identity,
                                                bias=lc2[:, L2_CB + b:L2_CB + b + 1], scale=lc2[:, L2_CW + 48 + b:L2_CW + 49 + b])
                last.then_inc(gfree[(9 + i) % 2], 1)
                if i == 1:
                    act.wait_ge(dt_n, 1)
                    nc.scalar.activation(dw[1], dw[1], ACT.Exp).then_inc(dt_e, 1)
                if i in ATT_SLOT and ATT_SLOT[i] + 1 < 8:
                    exp2(ATT_SLOT[i] + 1)
                if i == 4:
                    act.wait_ge(dt_pos, 1)
                    nc.scalar.activation(dw[1], dw[0], ACT.Ln).then_inc(dt_ln, 1)
                split_hi(act, M2, 13 + i)
                if i in ATT_SLOT:
                    u = ATT_SLOT[i]
                    act.wait_ge(s2_tr, u + 1)
                    if u % 2 == 0 and u:
                        act.wait_ge(s2_pv, u // 2)
                    nc.scalar.activation(pt2[:, 0:4, (u % 2) * P:(u % 2 + 1) * P], bank[6][:, :].rearrange("p (n t) -> p n t", n=4), ACT.Copy)\
                        .then_inc(s2_ev0, 1)
                if i >= 10:
                    act.wait_ge(conv_done, 8)
                    silu(i - 10)
                if i in PV_SLOT and PV_SLOT[i] % 2:
                    b = PV_SLOT[i] // 2
                    act.wait_ge(s2_pv, 2 * b + 2)
                    nc.scalar.activation(ff_hi[:, 0, b * T:(b + 1) * T], bank[7][:, T:2 * T], ACT.Copy).then_inc(s2_hi, 1)
            act.wait_ge(conv_done, 12)
            silu(2)

            def copies(g):
                act.wait_ge(cb_mm, g + 1)
                nc.scalar.activation(cb[:, g % 2, :, :], blocks2(bank[7][:, :]), ACT.Copy).then_inc(cb_done, 1)
                act.wait_ge(xt_mm0, g + 1)
                nc.scalar.activation(xt[:, g % 2, 0, :], bank[6][:, :], ACT.Copy).then_inc(xt_done0, 1)
                act.wait_ge(xt_mm1, g + 1)
                nc.scalar.activation(xt[:, g % 2, 1, :], bank[7][:, :], ACT.Copy).then_inc(xt_done1, 1)

            act.wait_ge(s2_pv, 4)
            copies(0)

            def decay(e):
                act.wait_ge(e_mask, e + 1)
                hu, st = e // 2, e % 2
                for h in range(4):
                    far, near = [dtt[:, st, 32 * d + 4 * hu + h:32 * d + 4 * hu + h + 1] for d in (st, 1 - st)]
                    nc.scalar.activation(eb_far[e % 4][:, h, :], eb_far[e % 4][:, h, :], ACT.Exp, bias=far)
                    last = nc.scalar.activation(eb_near[e % 4][:, h, :], eb_near[e % 4][:, h, :], ACT.Exp, bias=near)
                last.then_inc(e_exp, 1)

            act.wait_ge(dt_cols, 1)
            decay(0)
            decay(1)
            for hu in range(8):
                used2(act, 21 + hu)
                nc.scalar.activation(zb[:, 2 * hu:2 * hu + 2, :], blocks2(G2(21 + hu)[:, :]), ACT.Copy).then_inc(gfree[(21 + hu) % 2], 1)
                if hu < 7:
                    decay(2 * hu + 2)
                if hu % 2 and hu < 7:
                    if hu > 2:
                        act.wait_ge(e_used, 4 * (hu // 2))
                    copies(hu // 2 + 1)
                if hu < 7:
                    decay(2 * hu + 3)
                split_hi(act, M2, 25 + hu)
            act.wait_ge(gfree[0], 7 * layers + 28 // 2 + 1 + 1)
            act.wait_ge(gfree[1], 7 * layers + 28 // 2 + 1)
            for n in range(2):
                nc.scalar.activation(zb[:, 8 * n:8 * n + 8, :], zb[:, 8 * n:8 * n + 8, :], ACT.Silu).then_inc(z_silu, 1)
            act.wait_ge(e_used, 16)
            for i in range(8):
                used2(act, 29 + i)
                for c in range(2):
                    b = 2 * i + c
                    last = nc.scalar.activation(gb[:, b, :], G2(29 + i)[:, c * T:(c + 1) * T], ACT.Identity, bias=lc2[:, L2_BG + b:L2_BG + b + 1])
                last.then_inc(gfree[(29 + i) % 2], 1)
                split_hi(act, M2, 33 + i)
                if i < 4:
                    g = (2, 3, 0, 1)[i]
                    act.wait_ge(y_gated, i + 1)
                    if i:
                        act.wait_ge(y_ss, i)
                    nc.scalar.activation(sq2, xb[:, 4 * g:4 * g + 4, :], ACT.Square).then_inc(y_sq, 1)
                if i == 4:
                    act.wait_ge(y_ss, 4)
                    for b in range(2):
                        link(nc.scalar.activation(rs2[:, 2 * b:2 * b + 2, :], blocks2(bank[6 + b][:, :]), ACT.Ln,
                                                  bias=cst[:, C_LEPS:C_LEPS + 1], scale=1.0 / 512))
                    nc.scalar.activation(rs2, rs2, ACT.Exp, scale=-0.5).then_inc(y_rs, 1)
                if i in (5, 6):
                    n = i - 5
                    act.wait_ge(y_fin, n + 1)
                    nc.scalar.activation(mix_hi[:, 4 * n:4 * n + 4, :], xb[:, 8 + 4 * n:12 + 4 * n, :], ACT.Copy).then_inc(y_hi, 1)
            for n in (2, 3):
                act.wait_ge(y_fin, n + 1)
                nc.scalar.activation(act_hi[:, 4 * n - 8:4 * n - 4, :], xb[:, 4 * n - 8:4 * n - 4, :], ACT.Copy).then_inc(y_hi, 1)
            act.wait_ge(gfree[0], 7 * layers + 19 + 1)
            act.wait_ge(gfree[1], 7 * layers + 18 + 1)
            for n in (1, 0):
                nc.scalar.activation(gb[:, 8 * n:8 * n + 8, :], gb[:, 8 * n:8 * n + 8, :], ACT.Sigmoid).then_inc(gates_done, 1)
            for k in range(41, 49):
                split_hi(act, M2, k)
            for n in range(4):
                act.wait_ge(mx_sum, n + 1)
                nc.scalar.activation(mix_hi[:, 2 * n:2 * n + 2, :], mx[:, 2 * n:2 * n + 2, :], ACT.Copy).then_inc(mx_hi, 1)
            split_hi(act, M2, 49)
            act_layer_norm(act, 0, link, L2_LN1B, (50, 51, 52))
            act_ff(act, layers, M2, 50, 16 * layers, final=True)
            act_layer_norm(act, 1, link, L2_LN2B, ())
            for c in range(4):
                if c % 2 == 0:
                    act.wait_ge(o_turned, c + 1)
                    nc.scalar.activation(obuf[:, :, c * T:(c + 1) * T], blocks2(bank[c][:, :]), ACT.Copy).then_inc(o_copied0, 1)

        def act_layer_norm(act, q, link, bias, ks):
            act.wait_ge(ln_sum, q + 1)
            nc.scalar.activation(rs[:, :], bank[6][:, 0:T], ACT.Copy, scale=-1.0 / D).then_inc(ln_mean, 1)
            for kc in range(KC):
                act.wait_ge(ln_c, 8 * q + kc + 1)
                nc.scalar.activation(tb2[:, kc, :], x[:, kc, :], ACT.Square).then_inc(ln_sq, 1)
            ln_table()
            for k in ks[:1]:
                split_hi(act, M2, k)
            act.wait_ge(ln_ss, q + 1)
            rsqrt(link, rs[:, :], bank[7][:, 0:T], 1.0 / D, cst[:, C_LEPS:C_LEPS + 1]).then_inc(ln_rs, 1)
            for kc in range(KC):
                act.wait_ge(ln_t, 8 * q + kc + 1)
                b = lc2[:, bias + kc:bias + kc + 1]
                if q == 0:
                    nc.scalar.activation(act_hi[:, kc, :], tb2[:, kc, :], ACT.Identity, bias=b).then_inc(ln_hi, 1)
                    if kc in (3, 7):
                        for k in ks[1:][kc // 4:kc // 4 + 1]:
                            split_hi(act, M2, k)
                else:
                    nc.scalar.activation(x[:, kc, :], tb2[:, kc, :], ACT.Identity, bias=b).then_inc(ln_x, 1)
            if q == 0:
                for kc in range(KC):
                    nc.scalar.activation(x[:, kc, :], tb2[:, kc, :], ACT.Identity, bias=lc2[:, bias + kc:bias + kc + 1]).then_inc(ln_x, 1)

        def dve_second(dve):
            link = Chain(dve, dve_links, 0)
            link.base = layers * DVE_LINKS
            for kc in range(KC):
                dve.wait_ge(act_his, 16 * layers + kc + 1)
                nc.vector.tensor_tensor(act_lo[:, kc, :], x[:, kc, :], act_hi[:, kc, :].bitcast(F32), ALU.subtract).then_inc(act_ready, 1)
            for k in (2, 3):
                split_lo(dve, M2, k)
            for k in range(9):
                if k >= 6:
                    used2(dve, k)
                    nc.vector.tensor_copy(v2[:, :, (k - 6) * T:(k - 5) * T], blocks2(G2(k)[:, :])).then_inc(gfree[k % 2], 1)
                split_lo(dve, M2, k + 4)
            dve.wait_ge(dist_ready, 16)

            def biased(u):
                j, tt = u // 2, u % 2
                dve.wait_ge(s2_sc, u + 1)
                if u >= 2:
                    dve.wait_ge(s2_tr, u - 1)
                for p in range(3):
                    _, _, h = head2(p, j)
                    ins = nc.vector.scalar_tensor_tensor(pp[u % 2][:, p * T:(p + 1) * T], dist[:, tt, p, :], -slope(h),
                                                         bank[2 * (u % 2) + p // 2][:, (p % 2) * T:(p % 2 + 1) * T], ALU.mult, ALU.add)
                link(ins)
                nc.vector.tensor_reduce(nm2[:, u % 2:u % 2 + 1], pp[u % 2], AX.X, ALU.max, negate=True).then_inc(s2_nm, 1)

            def dt_part(n):
                if n == 0:
                    dve.wait_ge(dt_y, 1)
                    link(nc.vector.scalar_tensor_tensor(dw[1], dw[0], -1.0, dw[0], ALU.mult, ALU.min))
                    dve.sem_inc(dt_n, 1)
                elif n == 1:
                    dve.wait_ge(dt_e, 1)
                    link(nc.vector.tensor_scalar(dw[2], dw[1], 2.0, None, ALU.add))
                    link(nc.vector.reciprocal(dw[2], dw[2]))
                    link(nc.vector.tensor_tensor(dw[3], dw[1], dw[2], ALU.mult))
                    link(nc.vector.tensor_tensor(dw[4], dw[3], dw[3], ALU.mult))
                    link(nc.vector.tensor_scalar(dw[2], dw[4], 1.0 / 15, None, ALU.mult))
                elif n == 2:
                    for c in (13, 11, 9, 7, 5, 3):
                        link(nc.vector.scalar_tensor_tensor(dw[2], dw[2], 1.0 / c, dw[4], ALU.add, ALU.mult))
                elif n == 3:
                    link(nc.vector.scalar_tensor_tensor(dw[2], dw[2], 1.0, dw[3], ALU.add, ALU.mult))
                    link(nc.vector.tensor_scalar(dw[0], dw[0], 0.0, None, ALU.max))
                    link(nc.vector.scalar_tensor_tensor(dw[2], dw[2], 2.0, dw[0], ALU.mult, ALU.add))
                    nc.vector.tensor_scalar(dw[0], dw[2], 1e-37, None, ALU.max).then_inc(dt_pos, 1)
                    dve.wait_ge(alog_e, 1)
                    link(nc.vector.tensor_scalar(dw[3], dw[2], ea, -1.0, ALU.mult, ALU.mult))
                    link(nc.vector.tensor_tensor_scan(dw[4], cst[0:64, C_ONE:C_ONE + 1].to_broadcast([64, T]), dw[3], 0.0, ALU.mult, ALU.add))
                    link(nc.vector.scalar_tensor_tensor(dw[4], dw[3], cst[0:64, C_NM:C_NM + 1], dw[4], ALU.mult, ALU.add))
                    link(nc.vector.tensor_scalar(dw[5], dw[4], cst[0:64, C_SG:C_SG + 1], None, ALU.mult))

            def dt_bias():
                dve.wait_ge(dt_ln, 1)
                nc.vector.tensor_tensor(dw[1], dw[1], dw[5], ALU.subtract).then_inc(dt_done, 1)

            def normalized(u):
                dve.wait_ge(s2_exp, u + 1)
                link(nc.vector.reciprocal(dens2[:, u % 2:u % 2 + 1], dens2[:, u % 2:u % 2 + 1]))
                nc.vector.tensor_scalar(pp[u % 2], pp[u % 2], dens2[:, u % 2:u % 2 + 1], None, ALU.mult).then_inc(s2_p, 1)

            biased(0)
            normalized(0)
            for i in range(12):
                if i in ATT_SLOT and ATT_SLOT[i] + 1 < 8:
                    biased(ATT_SLOT[i] + 1)
                if i == 5:
                    dve.wait_ge(dt_tr, 1)
                    nc.vector.tensor_copy(dtt.rearrange("p t h -> p (t h)"), bank[6][:, 0:P]).then_inc(dt_cols, 1)
                dve.wait_ge(gfree[(9 + i) % 2], 7 * layers + (9 + i) // 2 + 2)
                for tap in (0, 1, 3, 4):
                    for c in range(2):
                        b = 2 * i + c
                        src, w = up[i % 2][:, c, tap:tap + T], lc2[:, L2_CW + 24 * tap + b:L2_CW + 24 * tap + b + 1]
                        if tap:
                            dve.wait_ge(dve_links, link.base + link.n - 1)
                        ins = nc.vector.scalar_tensor_tensor(xb[:, b, :], src, w, xb[:, b, :], ALU.mult, ALU.add)
                        if tap < 4:
                            ins.then_inc(dve_links, 1)
                            link.n += 1
                        elif c == 1:
                            ins.then_inc(conv_done, 1)
                        else:
                            ins.then_inc(dve_links, 1)
                            link.n += 1
                if i + 1 in ATT_SLOT:
                    normalized(ATT_SLOT[i + 1])
                split_lo(dve, M2, 13 + i)
                if i in ATT_SLOT:
                    u = ATT_SLOT[i]
                    dve.wait_ge(s2_tr, u + 1)
                    if u % 2 == 0 and u:
                        dve.wait_ge(s2_pv, u // 2)
                    nc.vector.tensor_copy(pt2[:, 4:6, (u % 2) * P:(u % 2 + 1) * P], bank[7][:, 0:T].rearrange("p (n t) -> p n t", n=2))\
                        .then_inc(s2_ev1, 1)
                if i in PV_SLOT and PV_SLOT[i] % 2:
                    b = PV_SLOT[i] // 2
                    dve.wait_ge(s2_hi, b + 1)
                    nc.vector.tensor_tensor(ff_lo[:, 0, b * T:(b + 1) * T], bank[7][:, T:2 * T], ff_hi[:, 0, b * T:(b + 1) * T].bitcast(F32),
                                            ALU.subtract).then_inc(s2_lo, 1)
                if i < 4:
                    dt_part(i)
                if i == 4:
                    dt_bias()

            def mask(e):
                st = e % 2
                far, near = eb_far[e % 4][:, :, st * P:(st + 1) * P], eb_near[e % 4]
                dve.wait_ge(db_ready[e % 4], 32 * (e // 4 + 1))
                mf, mb = [cst[:, c:c + P].unsqueeze(1).to_broadcast([P, 4, P]) for c in (C_MF, C_MB)]
                m_far, m_near = (mf, mb) if st == 0 else (mb, mf)
                nc.vector.tensor_tensor(far, far, m_far, ALU.add)
                nc.vector.tensor_tensor(near, near, m_near, ALU.add).then_inc(e_mask, 1)

            def weigh2(e):
                st, g = e % 2, e // 4
                if e % 4 == 0:
                    dve.wait_ge(cb_done, g + 1)
                dve.wait_ge(e_exp, e + 1)
                own = eb_far[e % 4][:, :, st * P:(st + 1) * P]
                link(nc.vector.tensor_tensor(own, own, eb_near[e % 4], ALU.add))
                nc.vector.tensor_tensor(eb_far[e % 4], eb_far[e % 4], cb[:, g % 2, st, :].unsqueeze(1).to_broadcast([P, 4, T]), ALU.mult)\
                    .then_inc(e_mul, 1)

            def take_y(hu):
                dve.wait_ge(e_used, 2 * hu + 2)
                for c in range(2):
                    b = 2 * hu + c
                    last = nc.vector.scalar_tensor_tensor(xb[:, b, :], xb[:, b, :], lc2[:, L2_DS + b:L2_DS + b + 1],
                                                          bank[hu % 4][:, c * T:(c + 1) * T], ALU.mult, ALU.add)
                last.then_inc(y_out, 1)

            mask(0)
            mask(1)
            for hu in range(8):
                weigh2(2 * hu)
                if hu < 7:
                    mask(2 * hu + 2)
                if 0 < hu < 7:
                    split_lo(dve, M2, 24 + hu)
                weigh2(2 * hu + 1)
                if hu < 7:
                    mask(2 * hu + 3)
                if hu:
                    dve.wait_ge(xt_mm1, (hu - 1) // 2 + 1)
                    take_y(hu - 1)
            split_lo(dve, M2, 31)
            split_lo(dve, M2, 32)
            take_y(7)
            dve.wait_ge(z_silu, 2)
            dve.wait_ge(y_out, 8)
            for n in range(4):
                g = (2, 3, 0, 1)[n]
                nc.vector.tensor_tensor(xb[:, 4 * g:4 * g + 4, :], xb[:, 4 * g:4 * g + 4, :], zb[:, 4 * g:4 * g + 4, :], ALU.mult).then_inc(y_gated, 1)
                split_lo(dve, M2, 33 + n)
            split_lo(dve, M2, 37)
            dve.wait_ge(y_rs, 1)
            dve.wait_ge(y_gated, 4)
            for n in range(4):
                g = (2, 3, 0, 1)[n]
                for b in range(4 * g, 4 * g + 4):
                    last = nc.vector.scalar_tensor_tensor(xb[:, b, :], xb[:, b, :], lc2[:, L2_SN + b:L2_SN + b + 1], rs2[:, n, :], ALU.mult, ALU.mult)
                last.then_inc(y_fin, 1)
                if n in (1, 2):
                    k = n - 1
                    dve.wait_ge(y_hi, k + 1)
                    nc.vector.tensor_tensor(mix_lo[:, 4 * k:4 * k + 4, :], xb[:, 8 + 4 * k:12 + 4 * k, :], mix_hi[:, 4 * k:4 * k + 4, :].bitcast(F32),
                                            ALU.subtract).then_inc(y_lo, 1)
                if n < 3:
                    split_lo(dve, M2, 38 + n)
            for n in (0, 1):
                dve.wait_ge(y_hi, n + 3)
                nc.vector.tensor_tensor(act_lo[:, 4 * n:4 * n + 4, :], xb[:, 4 * n:4 * n + 4, :], act_hi[:, 4 * n:4 * n + 4, :].bitcast(F32),
                                        ALU.subtract).then_inc(y_lo, 1)
            used2(dve, 37)
            dve.wait_ge(gates_done, 1)
            for n in range(4):
                nc.vector.tensor_tensor(m2[:, 2 * n:2 * n + 2, :], blocks2(bank[4 + n][:, :]), gb[:, 8 + 2 * n:10 + 2 * n, :], ALU.mult).then_inc(att_proj, 1)
            for k in range(41, 49):
                split_lo(dve, M2, k)
            dve.wait_ge(gates_done, 2)
            for n in range(4):
                v = slice(2 * n, 2 * n + 2)
                if n == 3:
                    used2(dve, 45)
                else:
                    dve.wait_ge(rows_done, 3 * layers + n + 1)
                link(nc.vector.tensor_tensor(mx[:, v, :], blocks2(bank[n][:, :]), gb[:, v, :], ALU.mult))
                nc.vector.tensor_tensor(mx[:, v, :], mx[:, v, :], m2[:, v, :], ALU.add).then_inc(mx_sum, 1)
                if n:
                    mixed2(dve, n - 1)
            mixed2(dve, 3)
            split_lo(dve, M2, 49)
            for n in range(4):
                used2(dve, 46 + n)
                for c in range(2):
                    kc = 2 * n + c
                    nc.vector.scalar_tensor_tensor(x[:, kc, :], x[:, kc, :], ALPHA, bank[4 + n % 2][:, c * T:(c + 1) * T], ALU.mult, ALU.add)\
                        .then_inc(x2_ready, 1)
            dve_layer_norm(dve, 0, L2_LN1G, L2_LN1B, (50, 51, 52))
            dve_ff(dve, M2, 50, 16 * layers, final=True)
            for kc in range(KC):
                if kc == 6:
                    used2(dve, 81)
                elif kc % 2 == 0:
                    dve.wait_ge(rows_done, 3 * layers + 3 + kc // 2 + 1)
                nc.vector.scalar_tensor_tensor(x[:, kc, :], x[:, kc, :], ALPHA, bank[kc // 2][:, (kc % 2) * T:(kc % 2 + 1) * T], ALU.mult, ALU.add)\
                    .then_inc(x2_ready, 1)
            dve_layer_norm(dve, 1, L2_LN2G, L2_LN2B, ())
            for c in range(4):
                if c % 2:
                    dve.wait_ge(o_turned, c + 1)
                    nc.vector.tensor_copy(obuf[:, :, c * T:(c + 1) * T], blocks2(bank[c][:, :])).then_inc(o_copied1, 1)

        def mixed2(dve, n):
            v = slice(2 * n, 2 * n + 2)
            dve.wait_ge(mx_hi, n + 1)
            nc.vector.tensor_tensor(mix_lo[:, v, :], mx[:, v, :], mix_hi[:, v, :].bitcast(F32), ALU.subtract).then_inc(mx_lo, 1)

        def dve_layer_norm(dve, q, gain, bias, ks):
            dve.wait_ge(ln_mean, q + 1)
            for kc in range(KC):
                nc.vector.tensor_tensor(x[:, kc, :], x[:, kc, :], rs[:, :], ALU.add).then_inc(ln_c, 1)
            for k in ks[:1]:
                split_lo(dve, M2, k)
            dve.wait_ge(ln_rs, q + 1)
            for kc in range(KC + 1):
                if kc < KC:
                    nc.vector.scalar_tensor_tensor(tb2[:, kc, :], x[:, kc, :], lc2[:, gain + kc:gain + kc + 1], rs[:, :], ALU.mult, ALU.mult)\
                        .then_inc(ln_t, 1)
                if kc and q == 0:
                    c = kc - 1
                    dve.wait_ge(ln_hi, c + 1)
                    nc.vector.scalar_tensor_tensor(act_lo[:, c, :], tb2[:, c, :], lc2[:, bias + c:bias + c + 1], act_hi[:, c, :].bitcast(F32),
                                                   ALU.add, ALU.subtract).then_inc(ln_lo, 1)
            for k in ks[1:]:
                split_lo(dve, M2, k)

        block = ctx.enter_context(nc.Block())

        @block.sync
        def _(sp):
            sp.dma_start(x_in, a["x"].rearrange("b (t p) d -> p (b t) d", p=P)).then_inc(x_loaded, 16)
            sp.dma_start(cst[:, :], a["cst"]).then_inc(cst_loaded, 16)
            for u in range(8):
                if u in (4, 5):
                    sp.wait_ge(mod_used, 2 + u - 4 + 1)
                if u in (6, 7):
                    sp.wait_ge(mod_used, 2 + u - 2 + 1)
                slots, got = (modw_x, modraw_x) if u in (2, 3) else (modw, modraw)
                sp.dma_start(slots[:, u % 2, :], a["modw"][u]).then_inc(got[u % 2], 16)
                if u in (5, 6):
                    sp.dma_start(raw[:, u - 5, :], a["panels"][u - 5]).then_inc(raw_ready[u - 5], 16)
            with sp.Fori(0, layers - 1) as l:
                sp_layer(sp, l, True)
            sp_layer(sp, layers - 1, False)
            finish(sp)

        @block.gpsimd
        def _(pool):
            link = Chain(pool, pool_links, 7)
            pool.dma_start(ccol[:, :], a["ccol"]).then_inc(c_loaded, 16)
            nc.gpsimd.memset(ub, 0.0)
            nc.gpsimd.memset(wb[0], 0.0)
            link(nc.gpsimd.memset(wb[1], 0.0))
            link.first = link.n
            with pool.Fori(0, layers) as l:
                link.layer(l)
                pool.wait_ge(x_ready, 16 * l + 8)
                pool.dma_start(lc[:, :], a["lcs"][l]).then_inc(lc_ready, 16)
                pool_rope(pool, l)
                pool_window(pool, l, link)
                link.end()
            pool_second(pool)

        @block.tensor
        def _(pe):
            pe.sem_inc(split_free, SPLIT)
            pe.sem_inc(mod_used, 2)
            pe.sem_inc(macc_free, 2)
            pe.sem_inc(gfree[0], 1)
            pe.sem_inc(gfree[1], 1)
            pe.sem_inc(ff_relu, 2)
            pe.sem_inc(ff_ready, 2)
            pe.wait_ge(x_loaded, 16)
            pe.wait_ge(cst_loaded, 16)
            for kc in range(KC):
                for tt in range(TT):
                    o = bank[kc // 2][:, (kc % 2) * T + tt * P:(kc % 2) * T + (tt + 1) * P]
                    last = nc.tensor.transpose(o, x_in[:, tt, kc * P:(kc + 1) * P], ident)
                last.then_inc(x_turned, 1)
            pe_norm_sum(pe, 0)
            for half in range(2):
                pe.wait_ge(modraw_x[half], 16)
            for c in range(4):
                for kc in range(KC):
                    s = (c // 2) * 4 * 256 + (kc % 4) * 256 + (c % 2) * P
                    col = MOD_AT + 48 + 4 + c
                    last = nc.tensor.matmul(bank[7][:, col:col + 1], modw_x[:, kc // 4, s:s + P], cact[:, kc:kc + 1],
                                            start=kc == 0, stop=kc == KC - 1)
            last.then_inc(macc_free, 2)
            for n, pair in enumerate((0, 2, 3)):
                pe_mod(pe, pair, first_sums[:, 2 * n:2 * n + 2, :], MOD_AT + 48 + 4 * pair)
            with pe.Fori(0, layers - 1) as l:
                pe_layer(pe, l, True)
            pe_layer(pe, layers - 1, False)
            pe_second(pe)

        @block.scalar
        def _(act):
            link = Chain(act, act_links, ACT_LINKS)
            act.wait_ge(cst_loaded, 16)
            nc.scalar.activation(idb[:, :], ident, ACT.Copy).then_inc(masks_ready, 1)
            nc.scalar.activation(causb[:, :], cst[:, C_CAUS:C_CAUS + P], ACT.Copy).then_inc(masks_ready, 1)
            nc.scalar.activation(cmpmb[:, :], cst[:, C_CMPM:C_CMPM + 32], ACT.Copy).then_inc(masks_ready, 1)
            act.wait_ge(c_loaded, 16)
            nc.scalar.activation(cact[:, :], ccol[:, 0:KC], ACT.Silu).then_inc(cact_ready, 1)
            act_squares(act, 0)
            split_hi(act, 0, 0)
            split_hi(act, 0, 1)
            with act.Fori(0, layers - 1) as l:
                link.layer(l)
                act_layer(act, l, link, True)
                link.end()
            link.layer(layers - 1)
            act_layer(act, layers - 1, link, False)
            link.end()
            act_second(act)

        @block.vector
        def _(dve):
            link = Chain(dve, dve_links, DVE_LINKS)
            for kc in range(KC):
                dve.wait_ge(x_turned, kc // 2 * 2 + 2)
                nc.vector.tensor_copy(x[:, kc, :], bank[kc // 2][:, (kc % 2) * T:(kc % 2 + 1) * T]).then_inc(x_ready, 1)
            dve.wait_ge(c_loaded, 16)
            dve.wait_ge(cact_ready, 1)
            for n, pair in enumerate((0, 2, 3)):
                for half in range(2):
                    dve_mod(dve, pair, first_sums[:, 2 * n:2 * n + 2, :], half)
                if pair == 2:
                    split_lo(dve, 0, 0)
                if pair == 0:
                    dve.wait_ge(mod_used, 4)
                    dve.sem_inc(mod_used, 2)
                    dve.sem_inc(mod_links, 14)
            dve_modc(dve, modc_ready, 1, 48, ccol[:, 2 * KC:2 * KC + 16], 3)
            nc.vector.scalar_tensor_tensor(gcol[:, 0:KC], modc[:, 8:16], 1.0, ccol[:, KC:2 * KC], ALU.add, ALU.mult).then_inc(gcol_ready, 1)
            dve.wait_ge(gcol_ready, 1)
            split_lo(dve, 0, 1)
            with dve.Fori(0, layers - 1) as l:
                link.layer(l)
                dve_layer(dve, l, link, True)
                link.end()
            link.layer(layers - 1)
            dve_layer(dve, layers - 1, link, False)
            link.end()
            dve_second(dve)


def col_panel(w, cols):
    return w[:, cols].reshape(KC, P, 256).transpose(1, 0, 2).reshape(P, PANEL)


def row_panel(w, j):
    return w[256 * j:256 * j + 256].reshape(2, P, D).transpose(1, 0, 2).reshape(P, PANEL)


def as_cols(v):
    return v.reshape(-1, P).T


def ff_panels(up, down):
    ups = [col_panel(up, slice(256 * j, 256 * j + 256)) for j in range(FF_STEPS)]
    downs = [row_panel(down, j) for j in range(FF_STEPS)]
    got = [ups[0]]
    for j in range(FF_STEPS - 1):
        got += [ups[j + 1], downs[j]]
    return got + [downs[-1]]


def lay_out(i):
    panels, lcs = [], []
    for l in range(DEPTH):
        w = i["w_in"][l]
        heads = [np.r_[512 + 64 * b:576 + 64 * b, 768 + 64 * b:832 + 64 * b] for b in range(4)]
        for cols in (slice(1024, 1280), slice(1280, 1536), slice(1536, 1792),
                     np.concatenate(heads[:2])):
            panels.append(col_panel(w, cols))
        panels.append(i["cmp_w1"][l].reshape(2, 16, 2, 64, 64).transpose(2, 3, 1, 0, 4).reshape(P, PANEL))
        panels += [col_panel(w, cols) for cols in (np.concatenate(heads[2:]), slice(0, 256), slice(256, 512))]
        rows = np.concatenate([np.arange(512), np.concatenate(heads)])
        panels += [col_panel(i["w_out"][l][rows], slice(256 * j, 256 * j + 256)) for j in range(4)]
        panels += ff_panels(i["w_ff1"][l], i["w_ff2"][l])
        following = (as_cols(i["b_mod"][l + 1])[:, :16], as_cols(i["norm1"][l + 1])) if l + 1 < DEPTH else (np.zeros((P, 24), np.float32),)
        twice = lambda v: np.concatenate([v, v])[:, None]
        lcs.append(np.concatenate([
            as_cols(i["b_mod"][l])[:, 16:], *following, as_cols(i["norm2"][l]), as_cols(i["pool_scale"][l]),
            twice(i["q_norm"][l]), *[twice(i["k_norm"][l, n]) for n in range(3)],
            i["cmp_pe"][l].reshape(2, 16, 2, 64).transpose(2, 3, 1, 0).reshape(P, 32),
            i["cmp_w2"][l].reshape(P, 64), i["pool_w"][l].transpose(1, 0, 2).reshape(P, 512),
            w[:, 1792:1816].reshape(KC, P, 24).transpose(1, 0, 2).reshape(P, 192)], axis=1))
    modw = i["w_mod"].reshape(DEPTH, 2, 4, P, MOD_PANELS // 2, 2, 256).transpose(0, 4, 1, 3, 5, 2, 6).reshape(-1, P, PANEL)
    w = i["w_in_2"]
    z, xbc, dt_f, _, q, k, v, gates = [int(n) for n in N_SPLITS[:-1]]
    cols = [n + 256 * j for n, count in ((q, 3), (k, 3), (v, 3), (xbc, 12), (z, 8), (gates, 8)) for j in range(count)]
    panels += [col_panel(w, slice(c, c + 256)) for c in cols]
    panels.append(row_panel(i["w_proj_attn_2"], 0))
    panels += [row_panel(i["w_proj_ssd_2"], j) for j in (4, 5, 6, 7, 0, 1, 2, 3)]
    panels += [col_panel(i["w_out_2"], slice(256 * j, 256 * j + 256)) for j in range(4)]
    panels += ff_panels(i["w_up_2"], i["w_down_2"])
    in_rows = lambda *v: np.concatenate([*v, np.zeros(P - 2 * N_HEADS, np.float32)])[:, None]
    lc2 = np.concatenate([
        w[:, dt_f:dt_f + 64].reshape(KC, P, 64).transpose(1, 0, 2).reshape(P, 512),
        in_rows(i["dt_bias_f_2"], i["dt_bias_b_2"]), in_rows(i["a_log_f_2"], i["a_log_b_2"]),
        *[as_cols(i["conv_w_2"][tap]) for tap in range(D_CONV)], as_cols(i["conv_b_2"]),
        as_cols(np.repeat(i["d_skip_2"], 64)), as_cols(i["ssd_norm_w_2"]), as_cols(i["b_gate_2"]),
        as_cols(i["ln1_g_2"]), as_cols(i["ln1_b_2"]), as_cols(i["ln2_g_2"]), as_cols(i["ln2_b_2"])], axis=1)
    first = np.concatenate([as_cols(i["c"][0]), as_cols(i["norm1"][0]), as_cols(i["b_mod"][0])[:, :16]], axis=1)
    return dict(x=i["x"], ccol=first, cst=constants(), lcs=np.stack(lcs), modw=modw, panels=np.stack(panels),
                lc2=lc2, dist=distances())


SETTINGS = dict(target_bir_lowering=False, num_devices=1, dynamic_dma_scratch_size=4096)


def kernel(**inputs):
    import numpy as _np
    import concourse.bacc as _bacc
    from concourse import mybir as _mybir
    from concourse.bass_utils import run_bass_kernel_spmd as _run

    laid_out = lay_out({name: _np.asarray(v) for name, v in inputs.items()})
    nc = _bacc.Bacc("TRN2", **SETTINGS)
    arrays, views = {}, {}
    for name, v in laid_out.items():
        arrays[f"in_{name}"] = _np.ascontiguousarray(v)
        views[name] = nc.dram_tensor(f"in_{name}", v.shape, _mybir.dt.float32, kind="ExternalInput").ap()
    out = nc.dram_tensor("out", (1, T, D), _mybir.dt.float32, kind="ExternalOutput").ap()
    build(nc, views, out)
    return _run(nc, [arrays], core_ids=[0]).results[0]["out"]
```
